# Optimizing a Trainium2 kernel written in Bass

```python
import math
import jax
import jax.numpy as jnp
from jax import lax
import numpy as np

D_MODEL = 1024
BATCH = 1
SEQ = 256
DEPTH = 2

PLE_DIM = 256
DN_ALPHA = (2.0 * DEPTH) ** 0.25
DN_BETA = (8.0 * DEPTH) ** -0.25
LN_EPS = 1e-5
HEAD_NORM_EPS = 1e-6
N_EVEN = (DEPTH + 1) // 2
N_ODD = DEPTH // 2

MOBA_HEADS = 8
MOBA_HEAD_DIM = 64
MOBA_BLOCK = 256
MOBA_TOPK = 3
MOBA_Q_BLOCK = 128
REL_BUCKETS = 32
REL_MAX_DIST = 128
GLA_HEADS = 4
GLA_DK = 64
GLA_DV = 128
GLA_GATE_RANK = 16
GLA_TAU = 16.0
HGRN_HEADS = 4
HGRN_DK = 64
HGRN_DV = 128
RET_HEADS = 4
RET_DK = 64
RET_DV = 128
ROPE_BASE = 10000.0
CHUNK = 64
FFN_DENSE = 2752
N_EXPERTS = 8
TOP_K = 2
FFN_EXPERT = 3584
MOE_BLOCK = 128

MOBA_W = MOBA_HEADS * MOBA_HEAD_DIM
EVEN_SPLITS = (MOBA_W, MOBA_W, MOBA_W,
               GLA_HEADS * GLA_DK, GLA_HEADS * GLA_DK, GLA_HEADS * GLA_DV,
               GLA_GATE_RANK, GLA_HEADS * GLA_DV)
ODD_SPLITS = (HGRN_HEADS * HGRN_DK, HGRN_HEADS * HGRN_DK, HGRN_HEADS * HGRN_DV, HGRN_HEADS * HGRN_DV,
              RET_HEADS * RET_DK, RET_HEADS * RET_DK, RET_HEADS * RET_DV, RET_HEADS * RET_DV)
EVEN_IN = sum(EVEN_SPLITS)
ODD_IN = sum(ODD_SPLITS)
EVEN_OUT = MOBA_W + GLA_HEADS * GLA_DV
ODD_OUT = HGRN_HEADS * HGRN_DV + RET_HEADS * RET_DV

kernel_name = 'hybrid_moba_gla_hgrn2_retnet_moe'

def split_cols(h, sizes):
    return jnp.split(h, [int(c) for c in np.cumsum(sizes)[:-1]], axis=-1)

def split_heads(t, n_heads):
    b, s, w = t.shape
    return t.reshape(b, s, n_heads, w // n_heads).transpose(0, 2, 1, 3)

def merge_heads(o):
    b, h, s, d = o.shape
    return o.transpose(0, 2, 1, 3).reshape(b, s, h * d)

def layer_norm(x, g, b):
    xf = x.astype(jnp.float32)
    xc = xf - jnp.mean(xf, axis=-1, keepdims=True)
    y = xc * lax.rsqrt(jnp.mean(xc * xc, axis=-1, keepdims=True) + LN_EPS)
    return (y * g.astype(jnp.float32) + b.astype(jnp.float32)).astype(x.dtype)

def head_rms_norm(o, g):
    o = o * lax.rsqrt(jnp.mean(o * o, axis=-1, keepdims=True) + HEAD_NORM_EPS)
    return merge_heads(o) * g.astype(jnp.float32)

def head_layer_norm(o, g):
    o = o - jnp.mean(o, axis=-1, keepdims=True)
    o = o * lax.rsqrt(jnp.mean(o * o, axis=-1, keepdims=True) + HEAD_NORM_EPS)
    return merge_heads(o) * g.astype(jnp.float32)

def t5_bucket(dist):
    n = jnp.maximum(dist, 0)
    max_exact = REL_BUCKETS // 2
    nf = jnp.maximum(n, 1).astype(jnp.float32)
    large = max_exact + (jnp.log(nf / max_exact) / math.log(REL_MAX_DIST / max_exact)
                         * (REL_BUCKETS - max_exact)).astype(jnp.int32)
    large = jnp.minimum(large, REL_BUCKETS - 1)
    return jnp.where(n < max_exact, n, large)

def moba_attention(q, k, v, rel_bias):
    B, H, S, dh = q.shape
    n_blk = max(-(-S // MOBA_BLOCK), MOBA_TOPK)
    pad = n_blk * MOBA_BLOCK - S
    kf = jnp.pad(k.astype(jnp.float32), ((0, 0), (0, 0), (0, pad), (0, 0)))
    vf = jnp.pad(v.astype(jnp.float32), ((0, 0), (0, 0), (0, pad), (0, 0)))
    kb = kf.reshape(B, H, n_blk, MOBA_BLOCK, dh)
    vb = vf.reshape(B, H, n_blk, MOBA_BLOCK, dh)
    k_mean = jnp.mean(kb, axis=3)
    tbl = rel_bias.astype(jnp.float32).T
    scale = dh ** -0.5
    n_q = S // MOBA_Q_BLOCK
    qs = q.astype(jnp.float32).reshape(B, H, n_q, MOBA_Q_BLOCK, dh).transpose(2, 0, 1, 3, 4)
    b_idx = jnp.arange(B)[:, None, None, None]
    h_idx = jnp.arange(H)[None, :, None, None]
    blk_ids = jnp.arange(n_blk)
    offs = jnp.arange(MOBA_BLOCK)
    rank_ids = jnp.arange(MOBA_TOPK)
    sel_w = MOBA_TOPK * MOBA_BLOCK

    def attend(args):
        qb, ci = args
        q0 = ci * MOBA_Q_BLOCK
        q_pos = q0 + jnp.arange(MOBA_Q_BLOCK)
        cur = q0 // MOBA_BLOCK
        gate = jnp.einsum('bhqd,bhnd->bhqn', qb, k_mean)
        gate = jnp.where(blk_ids < cur, gate, -jnp.inf)
        _, sel = lax.top_k(gate, MOBA_TOPK)
        valid = rank_ids < cur
        ks = kb[b_idx, h_idx, sel]
        vs = vb[b_idx, h_idx, sel]
        k_pos = sel[..., None] * MOBA_BLOCK + offs
        dist = q_pos[:, None, None] - k_pos
        s_sel = (jnp.einsum('bhqd,bhqnkd->bhqnk', qb, ks) * scale
                 + tbl[h_idx[..., None], t5_bucket(dist)])
        s_sel = jnp.where(valid[:, None], s_sel, -jnp.inf)
        k_own = lax.dynamic_index_in_dim(kb, cur, axis=2, keepdims=False)
        v_own = lax.dynamic_index_in_dim(vb, cur, axis=2, keepdims=False)
        dist_own = q_pos[:, None] - (cur * MOBA_BLOCK + offs)[None, :]
        s_own = jnp.einsum('bhqd,bhkd->bhqk', qb, k_own) * scale + tbl[:, t5_bucket(dist_own)]
        s_own = jnp.where(dist_own >= 0, s_own, -jnp.inf)
        logits = jnp.concatenate([s_sel.reshape(B, H, MOBA_Q_BLOCK, sel_w), s_own], axis=-1)
        probs = jax.nn.softmax(logits, axis=-1)
        p_sel = probs[..., :sel_w].reshape(B, H, MOBA_Q_BLOCK, MOBA_TOPK, MOBA_BLOCK)
        p_own = probs[..., sel_w:]
        return (jnp.einsum('bhqnk,bhqnkd->bhqd', p_sel, vs)
                + jnp.einsum('bhqk,bhkd->bhqd', p_own, v_own))

    out = lax.map(attend, (qs, jnp.arange(n_q)))
    return out.transpose(1, 2, 0, 3, 4).reshape(B, H, S, dh)

def chunked_gated_linear(q, k, v, log_a):
    B, H, S, dk = q.shape
    dv = v.shape[-1]
    n = S // CHUNK

    def to_chunks(t):
        return t.astype(jnp.float32).reshape(B, H, n, CHUNK, t.shape[-1]).transpose(2, 0, 1, 3, 4)

    qc, kc, vc, ac = to_chunks(q), to_chunks(k), to_chunks(v), to_chunks(log_a)
    bc = jnp.cumsum(ac, axis=-2)
    causal = jnp.tril(jnp.ones((CHUNK, CHUNK), dtype=bool))

    def step(state, inp):
        qb, kb, vb, bb = inp
        o_inter = jnp.einsum('bhtd,bhde->bhte', qb * jnp.exp(bb), state)
        diff = bb[:, :, :, None, :] - bb[:, :, None, :, :]
        decay = jnp.exp(jnp.where(causal[:, :, None], diff, -jnp.inf))
        scores = jnp.einsum('bhtd,bhsd,bhtsd->bhts', qb, kb, decay)
        o_intra = jnp.einsum('bhts,bhse->bhte', scores, vb)
        b_last = bb[:, :, -1:, :]
        new_state = (jnp.exp(b_last[:, :, 0, :])[..., None] * state
                     + jnp.einsum('bhsd,bhse->bhde', kb * jnp.exp(b_last - bb), vb))
        return new_state, o_inter + o_intra

    init = jnp.zeros((B, H, dk, dv), jnp.float32)
    _, out = lax.scan(step, init, (qc, kc, vc, bc))
    return out.transpose(1, 2, 0, 3, 4).reshape(B, H, S, dv)

def rotary(x):
    S, d = x.shape[2], x.shape[3]
    half = d // 2
    inv = ROPE_BASE ** (-jnp.arange(half, dtype=jnp.float32) / half)
    ang = jnp.arange(S, dtype=jnp.float32)[:, None] * inv[None, :]
    cos, sin = jnp.cos(ang), jnp.sin(ang)
    xf = x.astype(jnp.float32)
    x1, x2 = xf[..., :half], xf[..., half:]
    return jnp.concatenate([x1 * cos - x2 * sin, x1 * sin + x2 * cos], axis=-1)

def retention_chunkwise(q, k, v):
    B, H, S, dk = q.shape
    dv = v.shape[-1]
    n = S // CHUNK
    log_g = jnp.log1p(-jnp.exp2(-5.0 - jnp.arange(H, dtype=jnp.float32)))
    qc = q.astype(jnp.float32).reshape(B, H, n, CHUNK, dk)
    kc = k.astype(jnp.float32).reshape(B, H, n, CHUNK, dk)
    vc = v.astype(jnp.float32).reshape(B, H, n, CHUNK, dv)
    pos = jnp.arange(CHUNK, dtype=jnp.float32)
    rel = pos[:, None] - pos[None, :]
    dmask = jnp.where(rel >= 0, jnp.exp(jnp.maximum(rel, 0.0)[None] * log_g[:, None, None]), 0.0)
    scores = jnp.einsum('bhnid,bhnjd->bhnij', qc, kc) * dmask[:, None]
    o_intra = jnp.einsum('bhnij,bhnje->bhnie', scores, vc)
    zeta = jnp.exp((CHUNK - 1 - pos)[None, :] * log_g[:, None])
    u = jnp.einsum('bhnjd,bhnje->nbhde', kc * zeta[:, None, :, None], vc)
    g_chunk = jnp.exp(CHUNK * log_g)[:, None, None]

    def step(state, u_n):
        return g_chunk * state + u_n, state

    _, s_prev = lax.scan(step, jnp.zeros((B, H, dk, dv), jnp.float32), u)
    xi = jnp.exp((pos + 1.0)[None, :] * log_g[:, None])
    o_cross = jnp.einsum('bhnid,nbhde->bhnie', qc * xi[:, None, :, None], s_prev)
    return (o_intra + o_cross).reshape(B, H, S, dv)

def even_mixer(x, w_in, gla_w_gate, gla_b_gate, gla_norm, w_out, rel_bias):
    h = x @ w_in
    mq, mk, mv, gq, gk, gv, ga, gr = split_cols(h, EVEN_SPLITS)
    o_a = merge_heads(moba_attention(split_heads(mq, MOBA_HEADS), split_heads(mk, MOBA_HEADS),
                                     split_heads(mv, MOBA_HEADS), rel_bias))
    log_a = jax.nn.log_sigmoid((ga @ gla_w_gate + gla_b_gate).astype(jnp.float32)) / GLA_TAU
    o_b = chunked_gated_linear(split_heads(gq, GLA_HEADS).astype(jnp.float32) * GLA_DK ** -0.5,
                               split_heads(gk, GLA_HEADS), split_heads(gv, GLA_HEADS),
                               split_heads(log_a, GLA_HEADS))
    o_b = head_rms_norm(o_b, gla_norm) * jax.nn.silu(gr.astype(jnp.float32))
    return jnp.concatenate([o_a, o_b], axis=-1).astype(x.dtype) @ w_out

def odd_mixer(x, w_in, lb, hgrn_norm, ret_norm, w_out):
    h = x @ w_in
    hq, hf, hi, hg, rq, rk, rv, rg = split_cols(h, ODD_SPLITS)
    f = lb + (1.0 - lb) * jax.nn.sigmoid(hf.astype(jnp.float32))
    o_c = chunked_gated_linear(split_heads(hq, HGRN_HEADS), split_heads(1.0 - f, HGRN_HEADS),
                               split_heads(hi, HGRN_HEADS), split_heads(jnp.log(f), HGRN_HEADS))
    o_c = head_rms_norm(o_c, hgrn_norm) * jax.nn.silu(hg.astype(jnp.float32))
    q = rotary(split_heads(rq, RET_HEADS))
    k = rotary(split_heads(rk, RET_HEADS)) * RET_DK ** -0.5
    o_d = retention_chunkwise(q, k, split_heads(rv, RET_HEADS))
    o_d = head_layer_norm(o_d, ret_norm) * jax.nn.silu(rg.astype(jnp.float32))
    return jnp.concatenate([o_c, o_d], axis=-1).astype(x.dtype) @ w_out

def swiglu(x, w1, w3, w2):
    return (jax.nn.silu(x @ w1) * (x @ w3)) @ w2

def moe_swiglu(x, w_router, b_router, w1, w3, w2):
    B, S, D = x.shape
    n_tok = B * S
    n_asg = n_tok * TOP_K
    xf = x.reshape(n_tok, D)
    logits = (xf @ w_router).astype(jnp.float32) + b_router.astype(jnp.float32)
    top_logit, top_e = lax.top_k(logits, TOP_K)
    gates = jax.nn.softmax(top_logit, axis=-1)
    e_flat = top_e.reshape(-1).astype(jnp.int32)
    tok_flat = jnp.repeat(jnp.arange(n_tok, dtype=jnp.int32), TOP_K)
    g_flat = gates.reshape(-1)
    order = jnp.argsort(e_flat)
    e_s, tok_s, g_s = e_flat[order], tok_flat[order], g_flat[order]
    counts = jax.ops.segment_sum(jnp.ones_like(e_flat), e_flat, num_segments=N_EXPERTS)
    starts = jnp.cumsum(counts) - counts
    padded = (counts + MOE_BLOCK - 1) // MOE_BLOCK * MOE_BLOCK
    p_ends = jnp.cumsum(padded)
    p_starts = p_ends - padded
    dest = p_starts[e_s] + jnp.arange(n_asg, dtype=jnp.int32) - starts[e_s]
    n_rows = n_asg + N_EXPERTS * MOE_BLOCK
    tok_buf = jnp.zeros((n_rows,), jnp.int32).at[dest].set(tok_s)
    g_buf = jnp.zeros((n_rows,), jnp.float32).at[dest].set(g_s)
    n_blocks = n_rows // MOE_BLOCK
    blk_start = jnp.arange(n_blocks, dtype=jnp.int32) * MOE_BLOCK
    blk_e = jnp.minimum(jnp.searchsorted(p_ends, blk_start, side='right'), N_EXPERTS - 1)

    def expert_block(args):
        toks, e = args
        xb = xf[toks]
        return (jax.nn.silu(xb @ w1[e]) * (xb @ w3[e])) @ w2[e]

    y = lax.map(expert_block, (tok_buf.reshape(n_blocks, MOE_BLOCK), blk_e))
    y = y.reshape(n_rows, D).astype(jnp.float32) * g_buf[:, None]
    out = jnp.zeros((n_tok, D), jnp.float32).at[tok_buf].add(y)
    return out.reshape(B, S, D).astype(x.dtype)

def setup_inputs(seed: int = 0) -> dict:
    key = jax.random.key(seed)
    ks = iter(jax.random.split(key, 32))

    def nrm(shape, scale):
        return jax.random.normal(next(ks), shape, jnp.float32) * scale

    D = D_MODEL
    return {
        'x': nrm((BATCH, SEQ, D), 1.0),
        'p': nrm((DEPTH, BATCH, SEQ, PLE_DIM), 1.0),
        'rel_bias': nrm((REL_BUCKETS, MOBA_HEADS), 0.5),
        'even_w_in': nrm((N_EVEN, D, EVEN_IN), D ** -0.5),
        'gla_w_gate': nrm((N_EVEN, GLA_GATE_RANK, GLA_HEADS * GLA_DK), GLA_GATE_RANK ** -0.5),
        'gla_b_gate': nrm((N_EVEN, GLA_HEADS * GLA_DK), 0.1),
        'gla_norm': 1.0 + nrm((N_EVEN, GLA_HEADS * GLA_DV), 0.02),
        'even_w_out': nrm((N_EVEN, EVEN_OUT, D), EVEN_OUT ** -0.5 * DN_BETA),
        'odd_w_in': nrm((N_ODD, D, ODD_IN), D ** -0.5),
        'hgrn_gamma': nrm((DEPTH, HGRN_HEADS * HGRN_DK), 1.0),
        'hgrn_norm': 1.0 + nrm((N_ODD, HGRN_HEADS * HGRN_DV), 0.02),
        'ret_norm': 1.0 + nrm((N_ODD, RET_HEADS * RET_DV), 0.02),
        'odd_w_out': nrm((N_ODD, ODD_OUT, D), ODD_OUT ** -0.5 * DN_BETA),
        'ln_mix_g': 1.0 + nrm((DEPTH, D), 0.02),
        'ln_mix_b': nrm((DEPTH, D), 0.02),
        'ln_ffn_g': 1.0 + nrm((DEPTH, D), 0.02),
        'ln_ffn_b': nrm((DEPTH, D), 0.02),
        'ffn_w1': nrm((N_EVEN, D, FFN_DENSE), D ** -0.5),
        'ffn_w3': nrm((N_EVEN, D, FFN_DENSE), D ** -0.5),
        'ffn_w2': nrm((N_EVEN, FFN_DENSE, D), FFN_DENSE ** -0.5 * DN_BETA),
        'router_w': nrm((N_ODD, D, N_EXPERTS), D ** -0.5),
        'router_b': nrm((N_ODD, N_EXPERTS), 0.01),
        'expert_w1': nrm((N_ODD, N_EXPERTS, D, FFN_EXPERT), D ** -0.5),
        'expert_w3': nrm((N_ODD, N_EXPERTS, D, FFN_EXPERT), D ** -0.5),
        'expert_w2': nrm((N_ODD, N_EXPERTS, FFN_EXPERT, D), FFN_EXPERT ** -0.5 * DN_BETA),
        'ple_w_gate': nrm((DEPTH, D, D), D ** -0.5),
        'ple_w_proj': nrm((DEPTH, PLE_DIM, D), PLE_DIM ** -0.5),
    }

def reference(x, p, rel_bias, even_w_in, gla_w_gate, gla_b_gate, gla_norm, even_w_out,
              odd_w_in, hgrn_gamma, hgrn_norm, ret_norm, odd_w_out,
              ln_mix_g, ln_mix_b, ln_ffn_g, ln_ffn_b, ffn_w1, ffn_w3, ffn_w2,
              router_w, router_b, expert_w1, expert_w3, expert_w2, ple_w_gate, ple_w_proj):
    lb_p = jax.nn.softmax(hgrn_gamma.astype(jnp.float32), axis=0)
    lb_all = jnp.cumsum(lb_p, axis=0) - lb_p[0]
    for i in range(DEPTH):
        j = i // 2
        if i % 2 == 0:
            mix = even_mixer(x, even_w_in[j], gla_w_gate[j], gla_b_gate[j], gla_norm[j],
                             even_w_out[j], rel_bias)
        else:
            mix = odd_mixer(x, odd_w_in[j], lb_all[i], hgrn_norm[j], ret_norm[j], odd_w_out[j])
        x = layer_norm(DN_ALPHA * x + mix, ln_mix_g[i], ln_mix_b[i])
        if i % 2 == 0:
            ffn = swiglu(x, ffn_w1[j], ffn_w3[j], ffn_w2[j])
        else:
            ffn = moe_swiglu(x, router_w[j], router_b[j], expert_w1[j], expert_w3[j], expert_w2[j])
        x = layer_norm(DN_ALPHA * x + ffn, ln_ffn_g[i], ln_ffn_b[i])
        x = x + jax.nn.sigmoid(x @ ple_w_gate[i]) * (p[i] @ ple_w_proj[i])
    return x


_drawn_inputs = setup_inputs


def setup_inputs(seed=0):
    import zlib

    import numpy as np

    out = dict(_drawn_inputs(seed))
    spreads = {}
    factors = {'gla_w_gate': 3.47,
     'gla_b_gate': 5.537,
     'gla_norm': 8.0,
     'hgrn_norm': 26.965,
     'ret_norm': 28.571,
     'router_b': 30.15}
    for name, (base, spread) in spreads.items():
        noise = np.random.default_rng([zlib.crc32(name.encode()), seed]).standard_normal(out[name].shape)
        drawn = base * np.exp(spread * noise) if base else spread * noise
        out[name] = jnp.asarray(drawn.astype(out[name].dtype))
    for name, factor in factors.items():
        out[name] = (out[name] * factor).astype(out[name].dtype)
    return out
```

```python
from contextlib import ExitStack
import math

import numpy as np

import concourse.bass as bass
from concourse import mybir

F32 = mybir.dt.float32
F32R = mybir.dt.float32r
I32 = mybir.dt.int32
U32 = mybir.dt.uint32
U8 = mybir.dt.uint8
ALU = mybir.AluOpType
ACT = mybir.ActivationFunctionType
AX_X = mybir.AxisListType.X

P = 128
SEQ = 256
NT = SEQ // P
D = 1024
KD = D // P
NC = 512
DEPTH = 2
ALPHA = (2.0 * DEPTH) ** 0.25
LN_EPS = 1e-5
HEAD_EPS = 1e-6
MH, MD = 8, 64
LH, LK, LV = 4, 64, 128
BUCKETS, MAX_DIST = 32, 128
RANK = 16
FFN = 2752
NE = 8
FE = 3584
CE = FE // NC
EXTRA = 3
PLE = 256
LEVELS = 7
RAW, SPLIT = 6, 3
PIECE = 2048
NEG = -1e30

C_ID, C_IOTA, C_BEFORE, C_ONE = 0, 128, 256, 384
C_SUM = 512
C_COS = C_SUM + 9 * P
C_SIN = C_COS + NT * 32
C_SMALL = C_SIN + NT * 32
C_ALL = C_SMALL + 4


def constants():
    c = np.zeros((P, C_ALL), np.float32)
    i = np.arange(P)
    c[:, C_ID:C_ID + P] = np.eye(P)
    c[:, C_IOTA:C_IOTA + P] = i[None, :]
    c[:, C_BEFORE:C_BEFORE + P] = i[:, None] < i[None, :]
    c[:, C_ONE:C_ONE + P] = 1.0
    masks = np.zeros((P, LEVELS, P), np.float32)
    s, t = i[:, None], i[None, :]
    for level in range(LEVELS):
        half = 1 << level
        mid = t // (2 * half) * 2 * half + half
        right = t >= mid
        c[:, C_SUM + level * P:C_SUM + (level + 1) * P] = np.where(
            right, (s >= mid) & (s <= t), (s > t) & (s < mid))
        masks[:, level, :] = (s // (2 * half) == t // (2 * half)) & (s < mid) & right
    c[:, C_SUM + 7 * P:C_SUM + 8 * P] = s > t
    c[:, C_SUM + 8 * P:C_SUM + 9 * P] = s <= t
    half_dim = 32
    inv = (10000.0 ** (-np.arange(half_dim, dtype=np.float32) / np.float32(half_dim))).astype(np.float32)
    ang = np.arange(SEQ, dtype=np.float32)[:, None] * inv[None, :]
    for tile in range(NT):
        c[:, C_COS + 32 * tile:C_COS + 32 * tile + 32] = np.cos(ang[P * tile:P * tile + P])
        c[:, C_SIN + 32 * tile:C_SIN + 32 * tile + 32] = np.sin(ang[P * tile:P * tile + P])
    c[:, C_SMALL:] = [LN_EPS, HEAD_EPS, 1.0, 0.0]
    log_g = np.log1p(-np.exp2(-5.0 - np.arange(LH)))
    rel = np.arange(SEQ)[None, :] - i[:, None]
    dm = np.where(rel[:, None, :] >= 0, np.exp(np.maximum(rel, 0)[:, None, :] * log_g[None, :, None]), 0.0)
    dm = dm * LK ** -0.5
    decay = np.concatenate([dm, dm[:, :, 0:P]], axis=2).astype(np.float32)
    dist = np.arange(-127, 256)
    n = np.maximum(dist, 0)
    nf = np.maximum(n, 1).astype(np.float32)
    large = 16 + (np.log(nf / np.float32(16)) / np.float32(math.log(MAX_DIST / 16)) * np.float32(16)).astype(np.int32)
    bucket = np.where(n < 16, n, np.minimum(large, BUCKETS - 1))
    hot = np.zeros((BUCKETS + 1, 384), np.float32)
    hot[bucket, dist + 127] = dist >= 0
    hot[BUCKETS, dist + 127] = dist < 0
    return c, masks, decay, hot


class Piece:

    def __init__(self, src, rows, k, n):
        self.src, self.rows, self.k, self.n = src, rows, k, n


def column_pieces(w, n0, width):
    v = w.rearrange("(k p) n -> p k n", p=P)
    return [Piece(v[:, 4 * h:4 * h + 4, n0:n0 + width], P, 4, width) for h in range(2)]


def row_piece(w, f0):
    v = w[f0:f0 + 2 * P, :].rearrange("(k p) n -> p k n", p=P)
    return Piece(v, P, 2, D)


def trunk(nc, x, p, rel_bias, even_w_in, gla_w_gate, gla_b_gate, gla_norm, even_w_out, odd_w_in,
          hgrn_gamma, hgrn_norm, ret_norm, odd_w_out, ln_mix_g, ln_mix_b, ln_ffn_g, ln_ffn_b,
          ffn_w1, ffn_w3, ffn_w2, router_w, router_b, expert_w1, expert_w3, expert_w2,
          ple_w_gate, ple_w_proj, tab, masks, decay, hot, out, debug=None):
    even_cols = [0, 512, 1024, 1536, 2048, 2576]
    pieces = []
    where = {}

    def add(name, some):
        where[name] = len(pieces)
        pieces.extend(some)

    for j, n0 in enumerate(even_cols):
        add(("in", 0, j), column_pieces(even_w_in[0], n0, NC))
    for n in range(2):
        add(("out", 0, n), column_pieces(even_w_out[0], n * NC, NC))
    CF = -(-FFN // NC)

    def ffn_w2_pieces(c):
        if c < CF - 1:
            return [row_piece(ffn_w2[0], c * NC), row_piece(ffn_w2[0], c * NC + 2 * P)]
        rest = FFN - c * NC - P
        v = ffn_w2[0]
        return [Piece(v[c * NC:c * NC + P, :].rearrange("(k p) n -> p k n", p=P), P, 1, D),
                Piece(v[c * NC + P:FFN, :].rearrange("(k p) n -> p k n", p=rest), rest, 1, D)]

    for c in range(CF + 1):
        if c < CF:
            width = min(NC, FFN - c * NC)
            add(("w1", c), column_pieces(ffn_w1[0], c * NC, width))
            add(("w3", c), column_pieces(ffn_w3[0], c * NC, width))
        if c > 0:
            add(("w2", c - 1), ffn_w2_pieces(c - 1))

    def add_ple(i):
        for n in range(2):
            add(("gate", i, n), column_pieces(ple_w_gate[i], n * NC, NC))
        add(("proj", i), [row_piece(ple_w_proj[i], 0)])

    add_ple(0)
    for j in range(6):
        add(("in", 1, j), column_pieces(odd_w_in[0], j * NC, NC))
    for n in range(2):
        add(("out", 1, n), column_pieces(odd_w_out[0], n * NC, NC))
    N1 = len(pieces)
    PASS = 6 * CE
    before_tail = list(pieces)
    add_ple(1)
    tail = pieces[N1:]
    pieces = before_tail
    T0 = N1 + (NE + EXTRA) * PASS

    with ExitStack() as ctx:
        def sb(name, shape, dt=F32):
            return ctx.enter_context(nc.sbuf_tensor(name, shape, dt))

        sems = {}

        def S(name):
            if name not in sems:
                sems[name] = ctx.enter_context(nc.semaphore(name))
            return sems[name]

        raw = sb("raw", [P, RAW, PIECE])
        hi = sb("hi", [P, SPLIT, PIECE], F32R)
        lo = sb("lo", [P, SPLIT, PIECE], F32R)
        X = sb("X", [P, NT, D])
        xh = sb("xh", [P, KD, SEQ], F32R)
        xl = sb("xl", [P, KD, SEQ], F32R)
        ah = sb("ah", [P, 1024], F32R)
        al = sb("al", [P, 1024], F32R)
        XO = sb("XO", [P, 2048])
        lnp = sb("lnp", [P, 2, D])
        T = sb("T", [P, C_ALL])
        mask_sb = sb("mask_sb", [P, LEVELS, P], U8)
        st = sb("st", [P, 256])
        ctrl = sb("ctrl", [P, 8], I32)
        W = sb("W", [P, 13824])
        bias_dram = nc.dram_tensor("bias_rows", [MH, 384], F32).ap()
        ps = ctx.enter_context(nc.psum_tensor("ps", [P, 8, NC], F32))

        XT = XO[:].rearrange("p (k t) -> p k t", k=KD)
        O = XO[:].rearrange("p (t n) -> p t n", t=NT)
        ident = T[:, C_ID:C_ID + P]
        iota = T[:, C_IOTA:C_IOTA + P]
        before = T[:, C_BEFORE:C_BEFORE + P]
        ones = T[:, C_ONE:C_ONE + P]
        eps_ln = T[:, C_SMALL:C_SMALL + 1]
        eps_head = T[:, C_SMALL + 1:C_SMALL + 2]

        def arena(w0, *shape):
            n = int(np.prod(shape))
            v = W[:, w0:w0 + n]
            if len(shape) == 2:
                v = v.rearrange("p (a b) -> p a b", a=shape[0])
            if len(shape) == 3:
                v = v.rearrange("p (a b c) -> p a b c", a=shape[0], b=shape[1])
            return v

        H = [arena(w0, NT, NC) for w0 in (4096, 5120, 0, 1024, 2048, 3072)]
        logits = arena(4096, MH, 384)
        bias_t = arena(7168, MH, SEQ)
        qkT = arena(9216, 2, 4, SEQ)
        PT = [arena(12288 + 384 * b, 384) for b in range(2)]
        E = arena(7168, 2 * 8, SEQ)
        gT = arena(11264, 2 * 2, SEQ)
        gT2 = gT
        normw = arena(13312, NC)
        gla_b = arena(13056, SEQ)
        la = {0: arena(4096, NT, SEQ), 1: arena(6144, NT, SEQ)}
        SC = {0: arena(4608, LH, P), 1: arena(6144, LH, P)}
        tmp = {0: [arena(5120, NC), arena(5632, NC)], 1: [arena(12288, NC), arena(12800, NC)]}
        score = {0: H[3], 1: H[0]}
        lb, oml = arena(6656, SEQ), arena(6912, SEQ)
        ret_score = arena(7168, LH, 384)
        ret_decay = arena(8704, LH, 384)
        p_sb = arena(4096, NT, PLE)
        s1T, aT = arena(0, 1024), arena(1024, 1024)
        s1, a1, ysb = arena(0, NC), arena(512, NC), arena(1024, 1024)
        pick, pickg, pickgT = arena(2048, NT, P), arena(2304, NT, P), arena(2560, SEQ)
        posm, gates = arena(2816, NT, NE + EXTRA), arena(2838, NT, NE + EXTRA)
        wr = arena(5120, KD, NE)
        br = arena(5184, NE)
        rt = arena(5200, 16, 16)
        wga = lnp[:, 0, 0:P].rearrange("p (k n) -> p k n", k=KD)
        wgate, gaT = lnp[:, 0, P:P + SEQ], lnp[:, 0, P + SEQ:P + 2 * SEQ]
        relb = sb("relb", [33, MH])
        masks_f = arena(9984, LEVELS, P)
        hot_sb = arena(9216, 384)
        row_sb = arena(9600, 384)

        block = ctx.enter_context(nc.Block())

        def count_from_one(eng, *names):
            for name in names:
                eng.sem_inc(S(name), 1)

        def multiplied(eng, name, k=2):
            eng.wait_ge(S("piece_used"), where[name] + k)

        def landed(g):
            return 16 * (g // RAW + 1)

        @block.sync
        def _(sp):
            def load(slot, pc_src, n, rows, ready):
                sp.dma_start(raw[0:rows, slot, 0:n].rearrange("p (k n) -> p k n", k=pc_src.shape[1]),
                             pc_src).then_inc(S(f"loaded{slot}"), 16)

            for g, pc in enumerate(pieces):
                if g >= RAW:
                    sp.wait_ge(S("lo_done"), g - RAW + 1)
                load(g % RAW, pc.src, pc.k * pc.n, pc.rows, None)

            w1 = expert_w1[0].rearrange("e (k p) n -> p e k n", p=P)
            w3 = expert_w3[0].rearrange("e (k p) n -> p e k n", p=P)
            w2 = expert_w2[0].rearrange("e (k p) n -> p e k n", p=P)

            def expert_piece(i, e, idx, off, src):
                slot = (N1 + idx) % RAW
                sp.wait_ge(S("lo_done"), i * PASS + off + (N1 + idx - RAW + 1))
                sp.dma_start(raw[:, slot, :].rearrange("p (k n) -> p k n", k=src.shape[2]),
                             src.rearrange("p e k n -> p (e k) n")).then_inc(S(f"loaded{slot}"), 16)

            def columns(w, e, c, h):
                return w[:, bass.ds(e, 1), 4 * h:4 * h + 4, bass.ds(c * NC, NC)]

            def rows(e, c, h):
                return w2[:, bass.ds(e, 1), bass.ds(c * 4 + 2 * h, 2), :]

            def expert(i, e):
                for j, w in enumerate((w1, w3)):
                    for h in range(2):
                        expert_piece(i, e, 2 * j + h, 0, columns(w, e, 0, h))
                with sp.Fori(1, CE) as c:
                    for j, w in enumerate((w1, w3)):
                        for h in range(2):
                            expert_piece(i, e, 4 + 2 * j + h, (c - 1) * 6, columns(w, e, c, h))
                    for h in range(2):
                        expert_piece(i, e, 8 + h, (c - 1) * 6, rows(e, c - 1, h))
                for h in range(2):
                    expert_piece(i, e, 40 + h, 0, rows(e, CE - 1, h))

            with sp.Fori(0, NE) as i:
                expert(i, i)
            sp.wait_ge(S("routed"), 1)
            n_extra = sp.value_load(ctrl[0:1, 0:1], min_val=0, max_val=EXTRA)
            with sp.Fori(0, EXTRA) as j:
                with sp.If(j < n_extra):
                    e = sp.value_load(ctrl[0:1, bass.ds(j + 1, 1)], min_val=0, max_val=NE - 1)
                    expert(j + NE, e)
            for u, pc in enumerate(tail):
                slot = (N1 + u) % RAW
                sp.wait_ge(S("lo_done"), (n_extra + NE) * PASS + (N1 + u - RAW + 1))
                load(slot, pc.src, pc.k * pc.n, pc.rows, None)
            sp.wait_ge(S("x_final"), 1)
            sp.dma_start(out[0].rearrange("(t p) n -> p t n", p=P), X[:]).then_inc(S("stored"), 16)
            sp.wait_ge(S("stored"), 16)

        assert PASS % RAW == 0 and PASS % SPLIT == 0

        @block.gpsimd
        def _(pool):
            def small(dst, src, name):
                pool.dma_start(dst, src).then_inc(S(name), 16)

            def on_all(v, n):
                return v.rearrange("(a n) -> a n", a=1).partition_broadcast(P).rearrange("p a n -> p (a n)")

            small(X[:], x[0].rearrange("(t p) n -> p t n", p=P), "x_loaded")
            small(T[:], tab, "tab_loaded")
            small(relb[0:32, :], rel_bias, "hot_loaded")
            small(hot_sb[0:33, :], hot, "hot_loaded")
            small(masks_f, masks, "mask_loaded")
            pool.wait_ge(S("mask_loaded"), 16)
            nc.gpsimd.tensor_copy(mask_sb[:], masks_f).then_inc(S("mask_ready"), 1)
            small(wga, even_w_in[0].rearrange("(k p) n -> p k n", p=P)[:, :, 2560:2560 + RANK], "ga_loaded")
            small(wgate[0:RANK, :], gla_w_gate[0], "ga_loaded")
            small(gla_b, on_all(gla_b_gate[0], SEQ), "ga_loaded")
            small(normw, on_all(gla_norm[0], NC), "normw_loaded")
            pool.wait_ge(S("row_ready"), 1)
            small(bias_dram, row_sb[0:MH, :], "row_stored")
            pool.wait_ge(S("row_stored"), 16)
            for q in range(MH):
                toeplitz = bass.AP(bias_dram.tensor, q * 384, [[1, P], [1, SEQ]])
                small(bias_t[:, q, :], toeplitz, "bias_loaded")
            pool.wait_ge(S("z_psum"), 1)
            small(lnp[:, 0, :], on_all(ln_mix_g[0], D), "lnp_loaded")
            small(lnp[:, 1, :], on_all(ln_mix_b[0], D), "lnp_loaded")
            def dump(k):
                if debug is not None:
                    small(debug[k].rearrange("(t p) n -> p t n", p=P), X[:], "dump")
            if debug is not None:
                pool.wait_ge(S("mix_out"), 2)
                small(debug[0].rearrange("(t p) n -> p t n", p=P), O, "dump")
            pool.wait_ge(S("ln_done"), 1)
            dump(1)
            small(lnp[:, 0, :], on_all(ln_ffn_g[0], D), "lnp_loaded")
            small(lnp[:, 1, :], on_all(ln_ffn_b[0], D), "lnp_loaded")
            small(p_sb[:], p[0, 0].rearrange("(t p) n -> p t n", p=P), "p_loaded")
            small(normw, on_all(hgrn_norm[0], NC), "normw_loaded")
            small(lb, on_all(hgrn_gamma[0], SEQ), "gamma_loaded")
            small(oml, on_all(hgrn_gamma[1], SEQ), "gamma_loaded")
            pool.wait_ge(S("ln_done"), 2)
            if debug is not None:
                pool.wait_ge(S("ple_x"), 2)
            dump(2)
            small(lnp[:, 0, :], on_all(ln_mix_g[1], D), "lnp_loaded")
            small(lnp[:, 1, :], on_all(ln_mix_b[1], D), "lnp_loaded")
            pool.wait_ge(S("hgrn_done"), 1)
            small(ret_decay[:], decay, "decay_loaded")
            small(normw, on_all(ret_norm[0], NC), "normw_loaded")
            if debug is not None:
                pool.wait_ge(S("mix_out"), 6)
                small(debug[3].rearrange("(t p) n -> p t n", p=P), O, "dump")
            pool.wait_ge(S("ln_done"), 3)
            dump(4)
            small(lnp[:, 0, :], on_all(ln_ffn_g[1], D), "lnp_loaded")
            small(lnp[:, 1, :], on_all(ln_ffn_b[1], D), "lnp_loaded")
            small(p_sb[:], p[1, 0].rearrange("(t p) n -> p t n", p=P), "p_loaded")
            small(wr[:], router_w[0].rearrange("(k p) n -> p k n", p=P), "wr_loaded")
            small(br, on_all(router_b[0], NE), "wr_loaded")

        @block.scalar
        def _(act):
            count_from_one(act, "e_gT", "e_yout", "e_s")
            count = {}

            def inc(ins, name):
                count[name] = count.get(name, 0) + 1
                ins.then_inc(S(name), 1)

            def fin(ins, name="act_step"):
                inc(ins, name)
                act.wait_ge(S(name), count[name])

            def copy(o, i, scale=1.0):
                return nc.scalar.activation(o, i, ACT.Copy, scale=scale)

            def split(g, pc):
                act.wait_ge(S(f"loaded{g % RAW}"), landed(g))
                if g >= SPLIT:
                    act.wait_ge(S("piece_used"), g - SPLIT + 1)
                n = pc.k * pc.n
                copy(hi[0:pc.rows, g % SPLIT, 0:n], raw[0:pc.rows, g % RAW, 0:n]).then_inc(S("hi_done"), 1)

            def split_all(name, k=2):
                for g in range(where[name], where[name] + k):
                    split(g, pieces[g])

            nxt = [0]

            def transposed(keep):
                for q in range(4):
                    act.wait_ge(S("xT_psum"), nxt[0] + 1)
                    nxt[0] += 1
                    t, half = q // 2, q % 2
                    src = ps[:, 4 + q, :].rearrange("p (k t) -> p k t", k=4)
                    if keep:
                        copy(XT[:, 4 * half:4 * half + 4, t * P:(t + 1) * P], src).then_inc(S("xT_full"), 1)
                    copy(xh[:, 4 * half:4 * half + 4, t * P:(t + 1) * P], src).then_inc(S("xT_hi"), 1)

            proj_n = [0]

            def projected(layer, j, how):
                n = proj_n[0]
                proj_n[0] += 1
                multiplied(act, ("in", layer, j))
                for t in range(NT):
                    src = ps[:, 2 * (n % 2) + t, :]
                    if how == "forget":
                        copy(H[j][:, t, 0:SEQ], src[:, 0:SEQ])
                        ins = nc.scalar.activation(H[j][:, t, SEQ:NC], src[:, SEQ:NC], ACT.Sigmoid)
                    elif how == "silu":
                        ins = nc.scalar.activation(H[j][:, t, :], src, ACT.Silu)
                    else:
                        ins = copy(H[j][:, t, :], src)
                    ins.then_inc(S("proj_out"), 1)

            def decays(layer):
                for t in range(NT):
                    act.wait_ge(S("gT_psum"), 2 * layer + t + 1)
                    src = ps[:, 4 + t, :].rearrange("p (i t) -> p i t", i=4)
                    copy(gT[:, 0:2, t * P:(t + 1) * P], src[:, 0:2, :], scale=LK ** -0.5 if layer == 0 else 1.0)
                    copy(gT[:, 2:4, t * P:(t + 1) * P], src[:, 2:4, :]).then_inc(S("gT_out"), 1)
                n = 0
                for dt in range(2):
                    for t in range(NT):
                        for half in range(2):
                            act.wait_ge(S("sum_psum"), 8 * layer + n + 1)
                            nc.scalar.activation(
                                E[:, 8 * dt + 4 * half:8 * dt + 4 * half + 4, t * P:(t + 1) * P],
                                ps[:, 4 + n % 4, :].rearrange("p (l t) -> p l t", l=4), ACT.Exp,
                                scale=1.0 / 16 if layer == 0 else 1.0).then_inc(S("decay_out"), 1)
                            n += 1

            def join_out(layer):
                act.wait_ge(S("join_psum"), layer + 1)
                copy(SC[layer].rearrange("p (b d) t -> p b (d t)", b=2), ps[:, 4:6, 0:SEQ]).then_inc(S("join_out"), 1)

            norm_n = [0]

            def head_norm(banks, k):
                for t in range(NT):
                    n = norm_n[0]
                    norm_n[0] += 1
                    act.wait_ge(S("sumsq"), n + 1)
                    v = st[:, 64 + 4 * t:68 + 4 * t]
                    fin(nc.scalar.activation(v, v, ACT.Ln, bias=eps_head, scale=1.0 / LV))
                    nc.scalar.activation(v, v, ACT.Exp, scale=-0.5).then_inc(S("head_rstd"), 1)

            ln_n = [0]

            def layer_norm():
                n = ln_n[0]
                ln_n[0] += 1
                act.wait_ge(S("ln_var"), n + 1)
                v = st[:, 80:84].rearrange("p (t a) -> p t a", t=NT)[:, :, 1]
                fin(nc.scalar.activation(st[:, 84:86], v, ACT.Ln, bias=eps_ln))
                nc.scalar.activation(st[:, 84:86], st[:, 84:86], ACT.Exp, scale=-0.5).then_inc(S("ln_rstd"), 1)

            def ple(i, tail_wait=None, tail_passes=None):
                act.wait_ge(S("pT_psum"), i + 1)
                copy(ah[:, 0:NC], ps[:, 4, :]).then_inc(S("pT_hi"), 1)
                for n in range(2):
                    if i == 0:
                        split_all(("gate", 0, n))
                    else:
                        tail_wait(2 * n)
                        tail_wait(2 * n + 1)
                if i == 0:
                    split_all(("proj", 0), 1)
                else:
                    tail_wait(4)
                for n in range(2):
                    for t in range(NT):
                        if i == 0:
                            multiplied(act, ("gate", 0, n))
                        else:
                            act.wait_ge(S("piece_used"), (tail_passes() * PASS) + (N1 + 2 * n + 2))
                        nc.scalar.activation(O[:, t, n * NC:(n + 1) * NC], ps[:, 2 * n + t, :],
                                             ACT.Sigmoid).then_inc(S("gate_out"), 1)

            act.wait_ge(S("tab_loaded"), 16)
            transposed(True)
            split_all(("in", 0, 0))
            split_all(("in", 0, 1))
            projected(0, 0, "copy")
            act.wait_ge(S("gaT_psum"), 1)
            copy(gaT[0:RANK, :], ps[0:RANK, 4, 0:SEQ]).then_inc(S("gaT_out"), 1)
            split_all(("in", 0, 2))
            projected(0, 1, "copy")
            act.wait_ge(S("row_stored"), 16)
            act.wait_ge(S("mask_ready"), 1)
            for i in range(2):
                for t in range(NT):
                    act.wait_ge(S("mT_psum"), 2 * i + t + 1)
                    copy(qkT[:, i, :, t * P:(t + 1) * P],
                         ps[:, 4 + 2 * i + t, :].rearrange("p (g t) -> p g t", g=4)).then_inc(S("mT_out"), 1)
            split_all(("in", 0, 3))
            projected(0, 2, "copy")
            split_all(("in", 0, 4))
            for h in range(MH):
                for t in range(NT):
                    act.wait_ge(S("row_max"), 1)
                    sl = logits[:, h, 0:P] if t == 0 else logits[:, h, P:384]
                    nc.scalar.activation(sl, sl, ACT.Exp, bias=st[:, 16 + t * 8 + h:17 + t * 8 + h],
                                         accum_out=st[:, 32 + t * 8 + h:33 + t * 8 + h]).then_inc(S("exp_done"), 1)
            projected(0, 3, "copy")
            split_all(("in", 0, 5))
            projected(0, 4, "copy")
            projected(0, 5, "silu")
            for t in range(NT):
                act.wait_ge(S("gate_abs"), t + 1)
                v = tmp[0][t][:, 0:SEQ]
                fin(nc.scalar.activation(v, v, ACT.Exp))
                nc.scalar.activation(v, v, ACT.Ln, bias=1.0).then_inc(S("softplus"), 1)
            decays(0)
            join_out(0)
            def squares(banks, k):
                for t in range(NT):
                    act.wait_ge(S("lin_psum"), 2 * k + t + 1)
                    nc.scalar.activation(tmp[0 if k == 0 else 1][t], ps[:, banks + t, :],
                                         ACT.Square).then_inc(S("squares"), 1)
            squares(6, 0)
            head_norm(6, 0)
            transposed(False)
            split_all(("out", 0, 0))
            split_all(("out", 0, 1))
            layer_norm()
            transposed(False)
            def ffn_first(c):
                split_all(("w1", c))
                split_all(("w3", c))
                multiplied(act, ("w1", c))
                if c > 0:
                    act.wait_ge(S("a_done"), c)
                w = min(NC, FFN - c * NC)
                m = -(-w // P) * SEQ
                for b in range(0, m, NC):
                    ins = nc.scalar.activation(s1T[:, b:b + NC], ps[:, 4 + b // NC, :], ACT.Silu)
                ins.then_inc(S("s_done"), 1)

            def ffn_second(c):
                m = -(-min(NC, FFN - c * NC) // P) * SEQ
                act.wait_ge(S("a_done"), c + 1)
                if c > 0:
                    multiplied(act, ("w2", c - 1))
                copy(ah[:, 0:m], aT[:, 0:m]).then_inc(S("ah_done"), 1)

            for c in range(CF + 1):
                if c < CF:
                    ffn_first(c)
                if c > 0:
                    split_all(("w2", c - 1))
                if c < CF:
                    ffn_second(c)
            layer_norm()
            transposed(False)
            ple(0)
            transposed(False)
            act.wait_ge(S("gamma_diff"), 1)
            nc.scalar.activation(lb, lb, ACT.Sigmoid).then_inc(S("lb_done"), 1)
            for j in range(6):
                split_all(("in", 1, j))
                if j > 0:
                    projected(1, j - 1, {0: "forget", 2: "silu"}.get(j - 1, "copy"))
            projected(1, 5, "silu")
            act.wait_ge(S("forget"), 1)
            for t in range(NT):
                nc.scalar.activation(la[1][:, t, :], la[1][:, t, :], ACT.Ln).then_inc(S("log_f"), 1)
            decays(1)
            join_out(1)
            squares(6, 1)
            head_norm(6, 1)
            for t in range(NT):
                act.wait_ge(S("rT_psum"), t + 1)
                copy(gT[:, :, t * P:(t + 1) * P],
                     ps[:, 4 + t, :].rearrange("p (i t) -> p i t", i=4)).then_inc(S("rT_out"), 1)
            for t in range(NT):
                act.wait_ge(S("ret_centred"), t + 1)
                nc.scalar.activation(tmp[1][t], H[3][:, t, :], ACT.Square).then_inc(S("squares"), 1)
            head_norm(6, 2)
            transposed(False)
            split_all(("out", 1, 0))
            split_all(("out", 1, 1))
            layer_norm()
            transposed(True)
            for t in range(NT):
                act.wait_ge(S("top_diff"), t + 1)
                nc.scalar.activation(rt[:, 4 + t, 0:1], rt[:, 4 + t, 0:1], ACT.Exp).then_inc(S("top_exp"), 1)

            def xsplit(i, idx, off=0):
                g = N1 + idx
                act.wait_ge(S(f"loaded{g % RAW}"), i * (16 * PASS // RAW) + off * 16 + landed(g))
                act.wait_ge(S("piece_used"), i * PASS + off * 6 + (g - SPLIT + 1))
                copy(hi[:, g % SPLIT, :], raw[:, g % RAW, :]).then_inc(S("hi_done"), 1)

            def expert_silu(i, c):
                act.wait_ge(S("piece_used"), i * PASS + (c * 6 + N1 if not (isinstance(c, int) and c == 0) else N1 + 2))
                act.wait_ge(S("e_a"), i * CE + c + 1)
                nc.scalar.activation(s1, ps[:, 2, :], ACT.Silu).then_inc(S("e_s"), 1)

            def expert_ah(i, c):
                act.wait_ge(S("e_T"), i * CE + c + 2)
                copy(ah[:, 0:NC], ps[:, 4, :]).then_inc(S("e_ah"), 1)

            def expert(i):
                xsplit(i, 0)
                xsplit(i, 1)
                act.wait_ge(S("e_gather"), i * 3 + 2)
                act.wait_ge(S("e_scatter"), i * 4 + 1)
                copy(pickgT, ps[:, 7, 0:SEQ]).then_inc(S("e_gT"), 1)
                for half in range(2):
                    act.wait_ge(S("e_gather"), i * 3 + 3 + half)
                    copy(xh[:, 4 * half:4 * half + 4, 0:P],
                         ps[:, 5 + half, :].rearrange("p (k t) -> p k t", k=4)).then_inc(S("e_xh"), 1)
                xsplit(i, 2)
                xsplit(i, 3)
                expert_silu(i, 0)
                with act.Fori(1, CE) as c:
                    for j in range(4):
                        xsplit(i, 4 + j, c - 1)
                    expert_ah(i, c - 1)
                    expert_silu(i, c)
                    for j in range(2):
                        xsplit(i, 8 + j, c - 1)
                xsplit(i, 40)
                xsplit(i, 41)
                expert_ah(i, CE - 1)
                act.wait_ge(S("piece_used"), i * PASS + (N1 + PASS))
                copy(ysb, ps[:, 0:2, :].rearrange("p a n -> p (a n)")).then_inc(S("e_yout"), 1)

            with act.Fori(0, NE) as i:
                expert(i)
            act.wait_ge(S("routed"), 1)
            n_extra = act.value_load(ctrl[0:1, 0:1], min_val=0, max_val=EXTRA)
            with act.Fori(0, EXTRA) as j:
                with act.If(j < n_extra):
                    expert(j + NE)
            layer_norm()
            transposed(False)

            def tail_split(u):
                g = N1 + u
                act.wait_ge(S(f"loaded{g % RAW}"), (n_extra + NE) * (16 * PASS // RAW) + landed(g))
                act.wait_ge(S("piece_used"), (n_extra + NE) * PASS + (g - SPLIT + 1))
                copy(hi[:, g % SPLIT, :], raw[:, g % RAW, :]).then_inc(S("hi_done"), 1)

            ple(1, tail_split, lambda: n_extra + NE)

        @block.vector
        def _(dve):
            count_from_one(dve, "e_added", "e_a", "e_al")
            count = {}
            V = nc.vector

            def inc(ins, name):
                count[name] = count.get(name, 0) + 1
                ins.then_inc(S(name), 1)

            def fin(ins, name="dve_step"):
                inc(ins, name)
                dve.wait_ge(S(name), count[name])

            def rest(g, pc):
                n = pc.k * pc.n
                dve.wait_ge(S("hi_done"), g + 1)
                V.tensor_tensor(lo[0:pc.rows, g % SPLIT, 0:n], raw[0:pc.rows, g % RAW, 0:n],
                                hi[0:pc.rows, g % SPLIT, 0:n].bitcast(F32), ALU.subtract).then_inc(S("lo_done"), 1)

            def rest_all(name, k=2):
                for g in range(where[name], where[name] + k):
                    rest(g, pieces[g])

            nxt = [0]

            def transposed():
                for q in range(4):
                    nxt[0] += 1
                    dve.wait_ge(S("xT_hi"), nxt[0])
                    t, half = q // 2, q % 2
                    sl = slice(4 * half, 4 * half + 4)
                    V.tensor_tensor(xl[:, sl, t * P:(t + 1) * P], ps[:, 4 + q, :].rearrange("p (k t) -> p k t", k=4),
                                    xh[:, sl, t * P:(t + 1) * P].bitcast(F32), ALU.subtract).then_inc(S("xT_lo"), 1)

            def col(v, n):
                return v.rearrange("p (a b) -> p a b", b=1).broadcast_to([P, v.shape[1], n])

            def each(v, a):
                return v.rearrange("p (a n) -> p a n", a=1).broadcast_to([P, a, v.shape[1]])

            def linear(layer):
                dve.wait_ge(S("mask_ready"), 1)
                dve.wait_ge(S("gT_out"), 2 * layer + 2)
                for dt in range(2):
                    dve.wait_ge(S("decay_out"), 8 * layer + 4 * dt + 4)
                    for level in range(8):
                        half = 1 << level
                        z = E[:, 8 * dt + level, :].rearrange("p (b s h) -> p b s h", s=2, h=half)
                        for side, i in ((1, 0), (0, 1)):
                            v = gT[:, 2 * i + dt, :].rearrange("p (b s h) -> p b s h", s=2, h=half)
                            ins = V.tensor_tensor(z[:, :, side, :], z[:, :, side, :], v[:, :, side, :], ALU.mult)
                        inc(ins, "Z_done")
                n = 0
                for t in range(NT):
                    for plane in range(8):
                        dve.wait_ge(S("plane_psum"), 16 * layer + n + 1)
                        b = 4 + 2 * (n % 2)
                        src = ps[:, b:b + 2, 0:SEQ].rearrange("p b (d t) -> p b d t", d=2)
                        dst = score[layer][:, t, :].rearrange("p (b d t) -> p b d t", b=2, d=2)
                        if plane == 0:
                            m = ident.rearrange("p (a b t) -> p a b t", a=1, b=1).broadcast_to([P, 2, 2, P])
                            fin(V.tensor_tensor(dst, src, m, ALU.mult), "plane_done")
                        else:
                            m = mask_sb[:, plane - 1, :].rearrange("p (a b t) -> p a b t", a=1, b=1)
                            fin(V.copy_predicated(dst, m.broadcast_to([P, 2, 2, P]), src), "plane_done")
                        n += 1

            norm_n = [0]

            def head_norm(layer, k, src, gate, o0):
                dve.wait_ge(S("normw_loaded"), 16 * (k + 1))
                for t in range(NT):
                    dve.wait_ge(S("squares"), 2 * k + t + 1)
                    V.tensor_reduce(st[:, 64 + 4 * t:68 + 4 * t],
                                    tmp[layer][t].rearrange("p (h n) -> p h n", h=LH), AX_X,
                                    ALU.add).then_inc(S("sumsq"), 1)
                for t in range(NT):
                    dve.wait_ge(S("head_rstd"), 2 * k + t + 1)
                    v = tmp[layer][t]
                    fin(V.tensor_tensor(v.rearrange("p (h n) -> p h n", h=LH), src(t).rearrange("p (h n) -> p h n", h=LH),
                                        col(st[:, 64 + 4 * t:68 + 4 * t], LV), ALU.mult))
                    fin(V.tensor_tensor(v, v, normw, ALU.mult))
                    inc(V.tensor_tensor(O[:, t, o0:o0 + NC], v, gate[:, t, :], ALU.mult), "mix_out")
                dve.wait_ge(S("mix_out"), count["mix_out"])

            ln_n = [0]

            def layer_norm(src, ready):
                n = ln_n[0]
                ln_n[0] += 1
                for nn in range(2):
                    ready(nn)
                    for t in range(NT):
                        sl = slice(nn * NC, (nn + 1) * NC)
                        inc(V.scalar_tensor_tensor(out=O[:, t, sl], in0=X[:, t, sl], scalar=ALPHA, in1=src(t, nn),
                                                   op0=ALU.mult, op1=ALU.add), "dve_step")
                dve.wait_ge(S("dve_step"), count["dve_step"])
                stats = st[:, 96:120].rearrange("p (t n s) -> p t n s", t=NT, n=2)
                for t in range(NT):
                    for nn in range(2):
                        inc(V.bn_stats(stats[:, t, nn, :], O[:, t, nn * NC:(nn + 1) * NC]), "dve_step")
                dve.wait_ge(S("dve_step"), count["dve_step"])
                for t in range(NT):
                    ins = V.bn_aggr(st[:, 80 + 2 * t:82 + 2 * t], stats[:, t, :, :].rearrange("p n s -> p (n s)"))
                ins.then_inc(S("ln_var"), 1)
                dve.wait_ge(S("ln_rstd"), n + 1)
                dve.wait_ge(S("lnp_loaded"), 32 * (n + 1))
                for t in range(NT):
                    inc(V.tensor_scalar(O[:, t, :], O[:, t, :], st[:, 80 + 2 * t:81 + 2 * t], st[:, 84 + t:85 + t],
                                        ALU.subtract, ALU.mult), "dve_step")
                dve.wait_ge(S("dve_step"), count["dve_step"])
                for t in range(NT):
                    inc(V.tensor_tensor(O[:, t, :], O[:, t, :], lnp[:, 0, :], ALU.mult), "dve_step")
                dve.wait_ge(S("dve_step"), count["dve_step"])
                for t in range(NT):
                    inc(V.tensor_tensor(X[:, t, :], O[:, t, :], lnp[:, 1, :], ALU.add), "dve_step")
                dve.wait_ge(S("dve_step"), count["dve_step"])
                fin(V.tensor_copy(st[:, 90:91], st[:, 84:85]), "ln_done")

            def ple(i, tail_rest=None, tail_passes=None):
                dve.wait_ge(S("pT_hi"), i + 1)
                V.tensor_tensor(al[:, 0:NC], ps[:, 4, :], ah[:, 0:NC].bitcast(F32), ALU.subtract).then_inc(S("pT_lo"), 1)
                if i == 0:
                    rest_all(("gate", 0, 0))
                    rest_all(("gate", 0, 1))
                    rest_all(("proj", 0), 1)
                else:
                    for u in range(5):
                        tail_rest(u)
                if i == 0:
                    multiplied(dve, ("proj", 0), 1)
                else:
                    dve.wait_ge(S("piece_used"), tail_passes() * PASS + (N1 + 5))
                for n in range(2):
                    for t in range(NT):
                        sl = slice(n * NC, (n + 1) * NC)
                        dve.wait_ge(S("gate_out"), 4 * i + 2 * n + t + 1)
                        inc(V.tensor_tensor(O[:, t, sl], O[:, t, sl], ps[:, 4 + 2 * n + t, :], ALU.mult), "dve_step")
                dve.wait_ge(S("dve_step"), count["dve_step"])
                for t in range(NT):
                    inc(V.tensor_tensor(X[:, t, :], X[:, t, :], O[:, t, :], ALU.add), "ple_x")
                dve.wait_ge(S("ple_x"), count["ple_x"])

            V.memset(relb[32:33, :], NEG).then_inc(S("rel_neg"), 1)
            dve.wait_ge(S("row_psum"), 1)
            V.tensor_copy(row_sb[0:MH, :], ps[0:MH, 0, 0:384]).then_inc(S("row_ready"), 1)
            transposed()
            rest_all(("in", 0, 0))
            rest_all(("in", 0, 1))
            rest_all(("in", 0, 2))
            rest_all(("in", 0, 3))
            dve.wait_ge(S("bias_loaded"), 16 * MH)
            for h in range(MH):
                dve.wait_ge(S("score_psum"), h + 1)
                V.scalar_tensor_tensor(out=logits[:, h, 0:P], in0=ps[:, 4 + h % 4, 0:P], scalar=MD ** -0.5,
                                       in1=bias_t[:, h, P - 1::-1], op0=ALU.mult, op1=ALU.add)
                fin(V.scalar_tensor_tensor(out=logits[:, h, P:384], in0=ps[:, 4 + h % 4, P:384], scalar=MD ** -0.5,
                                           in1=bias_t[:, h, ::-1], op0=ALU.mult, op1=ALU.add), "logits_done")
            V.tensor_reduce(st[:, 0:8], logits[:, :, 0:P], AX_X, ALU.max)
            fin(V.tensor_reduce(st[:, 8:16], logits[:, :, P:384], AX_X, ALU.max))
            fin(V.tensor_scalar(st[:, 16:32], st[:, 0:16], -1.0, None, ALU.mult), "row_max")
            rest_all(("in", 0, 4))
            for h in range(MH):
                dve.wait_ge(S("PT_psum"), h + 1)
                if h >= 2:
                    dve.wait_ge(S("PV_used"), h - 1)
                V.tensor_copy(PT[h % 2], ps[:, 4 + h % 2, 0:384]).then_inc(S("PT_out"), 1)
            dve.wait_ge(S("exp_done"), 2 * MH)
            fin(V.reciprocal(st[:, 48:64], st[:, 32:48]))
            dve.wait_ge(S("PV_used"), MH)
            for t in range(NT):
                ins = V.tensor_tensor(O[:, t, 0:NC].rearrange("p (h n) -> p h n", h=MH),
                                      ps[:, 6 + t, :].rearrange("p (h n) -> p h n", h=MH),
                                      col(st[:, 48 + 8 * t:56 + 8 * t], MD), ALU.mult)
            ins.then_inc(S("moba_out"), 1)
            rest_all(("in", 0, 5))
            dve.wait_ge(S("ga_loaded"), 48)
            dve.wait_ge(S("z_psum"), 1)
            for t in range(NT):
                z = tmp[0][t][:, SEQ:NC]
                v = tmp[0][t][:, 0:SEQ]
                fin(V.tensor_tensor(z, ps[:, 5, t * SEQ:(t + 1) * SEQ], gla_b, ALU.add))
                inc(V.scalar_tensor_tensor(out=v, in0=z, scalar=-1.0, in1=z, op0=ALU.mult, op1=ALU.min), "gate_abs")
            for t in range(NT):
                dve.wait_ge(S("softplus"), t + 1)
                inc(V.scalar_tensor_tensor(out=la[0][:, t, :], in0=tmp[0][t][:, SEQ:NC], scalar=0.0,
                                           in1=tmp[0][t][:, 0:SEQ], op0=ALU.min, op1=ALU.subtract), "la_done")
            linear(0)
            head_norm(0, 0, lambda t: ps[:, 6 + t, :], H[5], NC)
            transposed()
            rest_all(("out", 0, 0))
            rest_all(("out", 0, 1))

            layer_norm(lambda t, n: ps[:, 2 * n + t, :], lambda n: multiplied(dve, ("out", 0, n)))
            transposed()
            for c in range(CF + 1):
                if c < CF:
                    rest_all(("w1", c))
                    rest_all(("w3", c))
                if c > 0:
                    dve.wait_ge(S("ah_done"), c)
                    m = -(-min(NC, FFN - (c - 1) * NC) // P) * SEQ
                    if c > 1:
                        multiplied(dve, ("w2", c - 2))
                    V.tensor_tensor(al[:, 0:m], aT[:, 0:m], ah[:, 0:m].bitcast(F32), ALU.subtract).then_inc(S("al_done"), 1)
                    rest_all(("w2", c - 1))
                if c < CF:
                    m = -(-min(NC, FFN - c * NC) // P) * SEQ
                    multiplied(dve, ("w3", c))
                    dve.wait_ge(S("s_done"), c + 1)
                    if c > 0:
                        dve.wait_ge(S("al_done"), c)
                    V.tensor_tensor(aT[:, 0:m], s1T[:, 0:m], ps[:, 6:8, :].rearrange("p a n -> p (a n)")[:, 0:m],
                                    ALU.mult).then_inc(S("a_done"), 1)
            layer_norm(lambda t, n: ps[:, 2 * n + t, :], lambda n: multiplied(dve, ("w2", CF - 1)))
            transposed()
            ple(0)
            transposed()
            dve.wait_ge(S("gamma_loaded"), 32)
            inc(V.tensor_tensor(lb, oml, lb, ALU.subtract), "gamma_diff")
            for j in range(6):
                rest_all(("in", 1, j))
                if j == 1:
                    dve.wait_ge(S("lb_done"), 1)
                    fin(V.tensor_scalar(oml, lb, -1.0, 1.0, ALU.mult, ALU.add))
            for t in range(NT):
                dve.wait_ge(S("proj_out"), 12 + t + 1)
                f = H[0][:, t, SEQ:NC]
                fin(V.tensor_tensor(f, f, oml, ALU.mult))
                fin(V.tensor_tensor(f, f, lb, ALU.add))
                V.tensor_scalar(la[1][:, t, :], f, 2.0 ** -63, None, ALU.max)
                fin(V.tensor_scalar(f, f, -1.0, 1.0, ALU.mult, ALU.add), "k_done")
            fin(V.tensor_copy(st[:, 91:92], st[:, 84:85]), "forget")
            linear(1)
            head_norm(1, 1, lambda t: ps[:, 6 + t, :], H[2], 0)
            fin(V.tensor_copy(st[:, 92:93], st[:, 84:85]), "hgrn_done")
            for t in range(NT):
                dve.wait_ge(S("proj_out"), 12 + 2 * 3 + t + 1)
                v = H[3][:, t, :].rearrange("p (h s n) -> p h s n", h=8, s=2)
                x1, x2 = v[:, :, 0, :], v[:, :, 1, :]
                cos = each(T[:, C_COS + 32 * t:C_COS + 32 * t + 32], 8)
                sin = each(T[:, C_SIN + 32 * t:C_SIN + 32 * t + 32], 8)
                r = [tmp[1][b][:, q * SEQ:(q + 1) * SEQ].rearrange("p (h n) -> p h n", h=8) for b in range(2) for q in range(2)]
                for d, a, b in ((0, x1, cos), (1, x2, sin), (2, x1, sin), (3, x2, cos)):
                    inc(V.tensor_tensor(r[d], a, b, ALU.mult), "dve_step")
                dve.wait_ge(S("dve_step"), count["dve_step"])
                inc(V.tensor_tensor(x1, r[0], r[1], ALU.subtract), "dve_step")
                inc(V.tensor_tensor(x2, r[2], r[3], ALU.add), "dve_step")
                dve.wait_ge(S("dve_step"), count["dve_step"])
                fin(V.tensor_copy(st[:, 93:94], st[:, 84:85]), "rotated")
            dve.wait_ge(S("decay_loaded"), 16)
            for h in range(LH):
                dve.wait_ge(S("ret_psum"), h + 1)
                V.tensor_tensor(ret_score[:, h, :], ps[:, 4 + h % 2, 0:384], ret_decay[:, h, :],
                                ALU.mult).then_inc(S("ret_scored"), 1)
            for t in range(NT):
                dve.wait_ge(S("ret_out"), t + 1)
                m = st[:, 72 + 4 * t:76 + 4 * t]
                src = ps[:, 6 + t, :].rearrange("p (h n) -> p h n", h=LH)
                fin(V.tensor_reduce(m, src, AX_X, ALU.add))
                fin(V.tensor_scalar(m, m, 1.0 / LV, None, ALU.mult))
                fin(V.tensor_tensor(H[3][:, t, :].rearrange("p (h n) -> p h n", h=LH), src, col(m, LV),
                                    ALU.subtract), "ret_centred")
            head_norm(1, 2, lambda t: H[3][:, t, :], H[5], NC)
            transposed()
            rest_all(("out", 1, 0))
            rest_all(("out", 1, 1))
            layer_norm(lambda t, n: ps[:, 2 * n + t, :], lambda n: multiplied(dve, ("out", 1, n)))
            transposed()
            dve.wait_ge(S("wr_loaded"), 32)
            dve.wait_ge(S("route_psum"), 1)
            sel = [rt[:, 0 + t, 0:NE] for t in range(NT)]
            gate8 = [rt[:, 2 + t, 0:NE] for t in range(NT)]
            iota8 = iota[:, 0:NE]
            for t in range(NT):
                lg, top, idx, idf = rt[:, 6, 0:8], rt[:, 6, 8:16], rt[:, 7, 0:8].bitcast(U32), rt[:, 7, 8:16]
                e, g1, g2 = rt[:, 4 + t, 0:1], rt[:, 4 + t, 1:2], rt[:, 4 + t, 2:3]
                fin(V.tensor_tensor(lg, ps[:, 0, 8 * t:8 * t + 8], br, ALU.add))
                fin(V.max(top, lg))
                fin(V.max_index(idx, top, lg))
                fin(V.tensor_copy(idf, idx))
                fin(V.tensor_tensor(e, top[:, 1:2], top[:, 0:1], ALU.subtract), "top_diff")
                hot1, hot2 = rt[:, 8, 0:8], rt[:, 8, 8:16]
                V.tensor_scalar(hot1, iota8, idf[:, 0:1], None, ALU.is_equal)
                fin(V.tensor_scalar(hot2, iota8, idf[:, 1:2], None, ALU.is_equal))
                fin(V.tensor_tensor(sel[t], hot1, hot2, ALU.add), "selected")
                dve.wait_ge(S("top_exp"), t + 1)
                fin(V.tensor_scalar(g1, e, 1.0, None, ALU.add))
                fin(V.reciprocal(g1, g1))
                fin(V.tensor_tensor(g2, g1, e, ALU.mult))
                fin(V.tensor_scalar(hot1, hot1, g1, None, ALU.mult))
                fin(V.tensor_scalar(hot2, hot2, g2, None, ALU.mult))
                fin(V.tensor_tensor(gate8[t], hot1, hot2, ALU.add))
                fin(V.tensor_copy(gates[:, t, 0:NE], gate8[t]))
            dve.wait_ge(S("rank_psum"), 1)
            for t in range(NT):
                v = posm[:, t, 0:NE]
                fin(V.tensor_scalar(v, ps[:, 1, 8 * t:8 * t + 8], 1.0, None, ALU.add))
                fin(V.tensor_tensor(v, v, sel[t], ALU.mult))
                fin(V.tensor_scalar(v, v, -1.0, None, ALU.add))
            over, upto, rank, pick1 = rt[:, 9, 0:8], rt[:, 9, 8:16], rt[:, 10, 0:8], rt[:, 10, 8:16]
            prod, one8 = rt[:, 11, 0:8], rt[:, 11, 8:16]
            count_of = ps[:, 1, 16:24]
            fin(V.tensor_scalar(over, count_of, float(P) + 0.5, None, ALU.is_gt))
            fin(V.tensor_copy(upto, over))
            for e in range(1, NE):
                fin(V.tensor_tensor(upto[:, e:e + 1], upto[:, e - 1:e], over[:, e:e + 1], ALU.add))
            fin(V.tensor_tensor(rank, upto, over, ALU.subtract))
            listf = rt[:, 12, 0:8]
            fin(V.memset(listf, 0.0))
            fin(V.tensor_copy(listf[:, 0:1], upto[:, 7:8]))
            for j in range(EXTRA):
                fin(V.tensor_scalar(pick1, rank, float(j), None, ALU.is_equal))
                fin(V.tensor_tensor(pick1, pick1, over, ALU.mult))
                fin(V.tensor_tensor(prod, pick1, iota8, ALU.mult))
                fin(V.tensor_reduce(listf[:, j + 1:j + 2], prod, AX_X, ALU.add))
                for t in range(NT):
                    fin(V.tensor_scalar(one8, posm[:, t, 0:NE], -float(P), None, ALU.add))
                    fin(V.tensor_tensor(one8, one8, pick1, ALU.mult))
                    fin(V.tensor_reduce(posm[:, t, NE + j:NE + j + 1], one8, AX_X, ALU.add))
                    fin(V.tensor_tensor(one8, gate8[t], pick1, ALU.mult))
                    fin(V.tensor_reduce(gates[:, t, NE + j:NE + j + 1], one8, AX_X, ALU.add))
            fin(V.memset(O[:, :, :], 0.0))
            fin(V.tensor_copy(ctrl[:, 0:8], listf), "routed")

            def xrest(i, idx, off=0):
                g = N1 + idx
                dve.wait_ge(S("hi_done"), i * PASS + off * 6 + (g + 1))
                V.tensor_tensor(lo[:, g % SPLIT, :], raw[:, g % RAW, :], hi[:, g % SPLIT, :].bitcast(F32),
                                ALU.subtract).then_inc(S("lo_done"), 1)

            def expert_a(i, c, last=False):
                dve.wait_ge(S("e_s"), i * CE + c + 2)
                dve.wait_ge(S("piece_used"), i * PASS + c * 6 + (N1 + (2 if last else 4)))
                dve.wait_ge(S("e_T"), i * CE + c + 1)
                V.tensor_tensor(a1, s1, ps[:, 3, :], ALU.mult).then_inc(S("e_a"), 1)

            def expert_al(i, c):
                dve.wait_ge(S("e_ah"), i * CE + c + 1)
                V.tensor_tensor(al[:, 0:NC], ps[:, 4, :], ah[:, 0:NC].bitcast(F32), ALU.subtract).then_inc(S("e_al"), 1)

            def expert(i):
                dve.wait_ge(S("e_gather"), i * 3 + 1)
                for t in range(NT):
                    V.tensor_scalar(pick[:, t, :], iota, posm[:, t, bass.ds(i, 1)], None, ALU.is_equal)
                    ins = V.tensor_scalar(pickg[:, t, :], iota, posm[:, t, bass.ds(i, 1)], gates[:, t, bass.ds(i, 1)],
                                          ALU.is_equal, ALU.mult)
                ins.then_inc(S("e_pick"), 1)
                xrest(i, 0)
                xrest(i, 1)
                for half in range(2):
                    dve.wait_ge(S("e_xh"), i * 2 + half + 1)
                    sl = slice(4 * half, 4 * half + 4)
                    V.tensor_tensor(xl[:, sl, 0:P], ps[:, 5 + half, :].rearrange("p (k t) -> p k t", k=4),
                                    xh[:, sl, 0:P].bitcast(F32), ALU.subtract).then_inc(S("e_xl"), 1)
                xrest(i, 2)
                xrest(i, 3)
                with dve.Fori(1, CE) as c:
                    xrest(i, 4, c - 1)
                    xrest(i, 5, c - 1)
                    expert_a(i, c - 1)
                    xrest(i, 6, c - 1)
                    xrest(i, 7, c - 1)
                    expert_al(i, c - 1)
                    xrest(i, 8, c - 1)
                    xrest(i, 9, c - 1)
                xrest(i, 40)
                expert_a(i, CE - 1, True)
                xrest(i, 41)
                expert_al(i, CE - 1)
                for q in range(4):
                    t, n = q // 2, q % 2
                    dve.wait_ge(S("e_scatter"), i * 4 + q + 2)
                    sl = slice(n * NC, (n + 1) * NC)
                    V.tensor_tensor(O[:, t, sl], O[:, t, sl], ps[:, 5 + q % 2, :], ALU.add).then_inc(S("e_added"), 1)

            with dve.Fori(0, NE) as i:
                expert(i)
            n_extra = dve.value_load(ctrl[0:1, 0:1], min_val=0, max_val=EXTRA)
            with dve.Fori(0, EXTRA) as j:
                with dve.If(j < n_extra):
                    expert(j + NE)
            dve.wait_ge(S("e_added"), (n_extra + NE) * 4 + 1)

            layer_norm(lambda t, n: O[:, t, n * NC:(n + 1) * NC], lambda n: None)
            transposed()

            def tail_rest(u):
                g = N1 + u
                dve.wait_ge(S("hi_done"), (n_extra + NE) * PASS + (g + 1))
                V.tensor_tensor(lo[:, g % SPLIT, :], raw[:, g % RAW, :], hi[:, g % SPLIT, :].bitcast(F32),
                                ALU.subtract).then_inc(S("lo_done"), 1)

            ple(1, tail_rest, lambda: n_extra + NE)
            fin(V.tensor_copy(st[:, 94:95], st[:, 84:85]), "x_final")

        @block.tensor
        def _(pe):
            count_from_one(pe, "e_gather", "e_scatter", "e_T")
            mm = nc.tensor.matmul

            def three(o, l_hi, l_lo, r_hi, r_lo, start, stop, **kw):
                mm(o, l_hi, r_hi, start=start, stop=False, **kw)
                mm(o, l_hi, r_lo, start=False, stop=False, **kw)
                return mm(o, l_lo, r_hi, start=False, stop=stop, **kw)

            nxt = [0]

            def transpose_x(src):
                for q in range(4):
                    t, half = q // 2, q % 2
                    for k in range(4):
                        c0 = (4 * half + k) * P
                        ins = nc.tensor.transpose(ps[:, 4 + q, k * P:(k + 1) * P], src[:, t, c0:c0 + P], ident)
                    ins.then_inc(S("xT_psum"), 1)
                nxt[0] += 4

            def need_xT():
                pe.wait_ge(S("xT_lo"), nxt[0])

            def product(g0, banks, wait_piece=None):
                for h in range(2):
                    g = g0 + h
                    if wait_piece is None:
                        pe.wait_ge(S("lo_done"), g + 1)
                    else:
                        wait_piece(g)
                    wh = hi[:, g % SPLIT, :].rearrange("p (k n) -> p k n", k=4)
                    wl = lo[:, g % SPLIT, :].rearrange("p (k n) -> p k n", k=4)
                    for t in range(NT):
                        for k in range(4):
                            kk = 4 * h + k
                            ins = three(ps[:, banks[t], :], xh[:, kk, t * P:(t + 1) * P], xl[:, kk, t * P:(t + 1) * P],
                                        wh[:, k, :], wl[:, k, :], kk == 0, kk == KD - 1)
                    ins.then_inc(S("piece_used"), 1)
                return ins

            proj_n = [0]

            def project(layer, j):
                n = proj_n[0]
                proj_n[0] += 1
                if n >= 2:
                    pe.wait_ge(S("proj_out"), 2 * (n - 1))
                product(where[("in", layer, j)], [2 * (n % 2), 2 * (n % 2) + 1])

            def linear(layer, j):
                v = H[j + 1]
                for t in range(NT):
                    for i in range(4):
                        ins = nc.tensor.transpose(ps[:, 4 + t, i * P:(i + 1) * P], H[j][:, t, i * P:(i + 1) * P], ident)
                    ins.then_inc(S("gT_psum"), 1)
                pe.wait_ge(S("gT_out"), 2 * layer + 2)
                n = 0
                for dt in range(2):
                    for t in range(NT):
                        for half in range(2):
                            if n >= 4:
                                pe.wait_ge(S("decay_out"), 8 * layer + n - 3)
                            lhs = la[layer][:, t, dt * P:(dt + 1) * P]
                            o = ps[:, 4 + n % 4, :]
                            c0 = C_SUM + 4 * half * P
                            if half and t:
                                mm(o[:, 0:3 * P], lhs, T[:, c0:c0 + 3 * P], start=True, stop=True)
                                ins = mm(o[:, 3 * P:], lhs, T[:, c0 + 4 * P:c0 + 5 * P], start=True, stop=True)
                            else:
                                ins = mm(o, lhs, T[:, c0:c0 + 4 * P], start=True, stop=True)
                            ins.then_inc(S("sum_psum"), 1)
                            n += 1
                pe.wait_ge(S("decay_out"), 8 * layer + 8)
                n = 0
                for t in range(NT):
                    for plane in range(8):
                        if n >= 2:
                            pe.wait_ge(S("plane_done"), 16 * layer + n - 1)
                        pe.wait_ge(S("Z_done"), 16 * layer + (16 if plane else 0))
                        for h in range(LH):
                            dt, r = h // 2, 64 * (h % 2)
                            if plane == 0:
                                a, b = gT[r:r + 64, 2 + dt, t * P:(t + 1) * P], gT[r:r + 64, dt, t * P:(t + 1) * P]
                            else:
                                a = b = E[r:r + 64, 8 * dt + plane - 1, t * P:(t + 1) * P]
                            ins = mm(ps[:, 4 + 2 * (n % 2) + h % 2, dt * P:(dt + 1) * P], a, b, start=True, stop=True)
                        ins.then_inc(S("plane_psum"), 1)
                        n += 1
                pe.wait_ge(S("plane_done"), 16 * layer + 15)
                for h in range(LH):
                    dt, r = h // 2, 64 * (h % 2)
                    ins = mm(ps[:, 4 + h % 2, dt * P:(dt + 1) * P], E[r:r + 64, 8 * dt + 7, 0:P],
                             E[r:r + 64, 8 * dt + 7, P:SEQ], start=True, stop=True)
                ins.then_inc(S("join_psum"), 1)
                pe.wait_ge(S("plane_done"), 16 * layer + 16)
                pe.wait_ge(S("join_out"), layer + 1)
                sc = [score[layer][:, t, :].rearrange("p (h t) -> p h t", h=LH) for t in range(NT)]
                place = [2 * (h % 2) + h // 2 for h in range(LH)]
                for h in range(LH):
                    ins = mm(ps[:, 6, h * P:(h + 1) * P], sc[0][:, place[h], :], v[:, 0, h * P:(h + 1) * P], start=True, stop=True)
                ins.then_inc(S("lin_psum"), 1)
                for h in range(LH):
                    mm(ps[:, 7, h * P:(h + 1) * P], SC[layer][:, place[h], :], v[:, 0, h * P:(h + 1) * P], start=True, stop=False)
                    ins = mm(ps[:, 7, h * P:(h + 1) * P], sc[1][:, place[h], :], v[:, 1, h * P:(h + 1) * P], start=False, stop=True)
                ins.then_inc(S("lin_psum"), 1)

            def output(layer):
                for n in range(2):
                    product(where[("out", layer, n)], [2 * n, 2 * n + 1])

            def ple(i, wait_piece=None, g0=None):
                pe.wait_ge(S("p_loaded"), 16 * (i + 1))
                for t in range(NT):
                    for k in range(2):
                        ins = nc.tensor.transpose(ps[:, 4, (2 * t + k) * P:(2 * t + k + 1) * P],
                                                  p_sb[:, t, k * P:(k + 1) * P], ident)
                ins.then_inc(S("pT_psum"), 1)
                for n in range(2):
                    product(g0 + 2 * n, [2 * n, 2 * n + 1], wait_piece)
                pe.wait_ge(S("pT_lo"), i + 1)
                g = g0 + 4
                if wait_piece is None:
                    pe.wait_ge(S("lo_done"), g + 1)
                else:
                    wait_piece(g)
                wh = hi[:, g % SPLIT, :].rearrange("p (k n) -> p k n", k=2)
                wl = lo[:, g % SPLIT, :].rearrange("p (k n) -> p k n", k=2)
                for t in range(NT):
                    for n in range(2):
                        for k in range(2):
                            sl = slice((2 * t + k) * P, (2 * t + k + 1) * P)
                            ins = three(ps[:, 4 + 2 * n + t, :], ah[:, sl], al[:, sl], wh[:, k, n * NC:(n + 1) * NC],
                                        wl[:, k, n * NC:(n + 1) * NC], k == 0, k == 1)
                ins.then_inc(S("piece_used"), 1)

            pe.wait_ge(S("hot_loaded"), 32)
            pe.wait_ge(S("rel_neg"), 1)
            mm(ps[0:MH, 0, 0:384], relb[:, :], hot_sb[0:33, :], start=True, stop=True).then_inc(S("row_psum"), 1)
            pe.wait_ge(S("x_loaded"), 16)
            pe.wait_ge(S("tab_loaded"), 16)
            transpose_x(X)
            need_xT()
            pe.wait_ge(S("row_ready"), 1)
            project(0, 0)
            pe.wait_ge(S("ga_loaded"), 48)
            pe.wait_ge(S("xT_full"), 4)
            for k in range(KD):
                ins = mm(ps[0:RANK, 4, 0:SEQ], wga[:, k, :], XT[:, k, :], start=(k == 0), stop=(k == KD - 1))
            ins.then_inc(S("gaT_psum"), 1)
            pe.wait_ge(S("gaT_out"), 1)
            project(0, 1)
            for i in range(2):
                pe.wait_ge(S("proj_out"), 2 * i + 2)
                for t in range(NT):
                    for g in range(4):
                        ins = nc.tensor.transpose(ps[:, 4 + 2 * i + t, g * P:(g + 1) * P],
                                                  H[i][:, t, g * P:(g + 1) * P], ident)
                    ins.then_inc(S("mT_psum"), 1)
            project(0, 2)
            pe.wait_ge(S("mT_out"), 4)
            for h in range(MH):
                g, r = h // 2, 64 * (h % 2)
                if h >= 4:
                    pe.wait_ge(S("logits_done"), h - 3)
                mm(ps[:, 4 + h % 4, 0:P], qkT[r:r + 64, 0, g, 0:P], qkT[r:r + 64, 1, g, 0:P], start=True, stop=True)
                mm(ps[:, 4 + h % 4, P:384], qkT[r:r + 64, 0, g, P:SEQ], qkT[r:r + 64, 1, g, :], start=True,
                   stop=True).then_inc(S("score_psum"), 1)
            project(0, 3)
            pe.wait_ge(S("logits_done"), MH)
            pe.wait_ge(S("proj_out"), 6)
            for h in range(MH):
                pe.wait_ge(S("exp_done"), 2 * h + 2)
                if h >= 2:
                    pe.wait_ge(S("PT_out"), h - 1)
                for b in range(3):
                    ins = nc.tensor.transpose(ps[:, 4 + h % 2, b * P:(b + 1) * P], logits[:, h, b * P:(b + 1) * P], ident)
                ins.then_inc(S("PT_psum"), 1)
                pe.wait_ge(S("PT_out"), h + 1)
                sl = slice(h * MD, (h + 1) * MD)
                mm(ps[:, 6, sl], PT[h % 2][:, 0:P], H[2][:, 0, sl], start=True, stop=True)
                mm(ps[:, 7, sl], PT[h % 2][:, P:2 * P], H[2][:, 0, sl], start=True, stop=False)
                mm(ps[:, 7, sl], PT[h % 2][:, 2 * P:384], H[2][:, 1, sl], start=False, stop=True).then_inc(S("PV_used"), 1)
            project(0, 4)
            project(0, 5)
            for t in range(NT):
                ins = mm(ps[:, 5, t * SEQ:(t + 1) * SEQ], gaT[0:RANK, t * P:(t + 1) * P], wgate[0:RANK, :],
                         start=True, stop=True)
            ins.then_inc(S("z_psum"), 1)
            pe.wait_ge(S("moba_out"), 1)
            pe.wait_ge(S("proj_out"), 12)
            pe.wait_ge(S("la_done"), 2)
            linear(0, 3)
            pe.wait_ge(S("mix_out"), 2)
            transpose_x(O)
            need_xT()
            output(0)
            pe.wait_ge(S("ln_done"), 1)
            transpose_x(X)
            need_xT()
            for c in range(CF + 1):
                if c < CF:
                    w = min(NC, FFN - c * NC)
                    for j, name in enumerate(("w1", "w3")):
                        if c > 0:
                            pe.wait_ge(S("s_done" if j == 0 else "a_done"), c)
                        for h in range(2):
                            g = where[(name, c)] + h
                            pe.wait_ge(S("lo_done"), g + 1)
                            for m in range(-(-w // P)):
                                o = ps[:, 4 + 2 * j + m // 2, (m % 2) * SEQ:(m % 2 + 1) * SEQ]
                                for k in range(4):
                                    kk = 4 * h + k
                                    c0 = k * w + m * P
                                    wh, wl = hi[:, g % SPLIT, c0:c0 + P], lo[:, g % SPLIT, c0:c0 + P]
                                    first = kk == 0 and m % 2 == 0
                                    ins = three(o, wh, wl, xh[:, kk, :], xl[:, kk, :], first, kk == KD - 1,
                                                skip_group_check=True)
                            ins.then_inc(S("piece_used"), 1)
                if c > 0:
                    pe.wait_ge(S("al_done"), c)
                    w = min(NC, FFN - (c - 1) * NC)
                    g0 = where[("w2", c - 1)]
                    for h in range(2):
                        g = g0 + h
                        pe.wait_ge(S("lo_done"), g + 1)
                        kn = pieces[g].k
                        rows = pieces[g].rows
                        wh = hi[0:rows, g % SPLIT, 0:kn * D].rearrange("p (k n) -> p k n", k=kn)
                        wl = lo[0:rows, g % SPLIT, 0:kn * D].rearrange("p (k n) -> p k n", k=kn)
                        for t in range(NT):
                            for n in range(2):
                                for k in range(kn):
                                    m = kn * h + k
                                    sl = slice(m * SEQ + t * P, m * SEQ + (t + 1) * P)
                                    last = c == CF and h == 1
                                    ins = three(ps[:, 2 * n + t, :], ah[0:rows, sl], al[0:rows, sl],
                                                wh[:, k, n * NC:(n + 1) * NC], wl[:, k, n * NC:(n + 1) * NC],
                                                c == 1 and m == 0, last, skip_group_check=True)
                        ins.then_inc(S("piece_used"), 1)
            pe.wait_ge(S("ln_done"), 2)
            transpose_x(X)
            need_xT()
            ple(0, None, where[("gate", 0, 0)])
            pe.wait_ge(S("ple_x"), 2)
            transpose_x(X)
            need_xT()
            for j in range(6):
                project(1, j)
            pe.wait_ge(S("k_done"), 2)
            pe.wait_ge(S("log_f"), 2)
            linear(1, 0)
            for t in range(NT):
                pe.wait_ge(S("rotated"), t + 1)
                for i in range(4):
                    ins = nc.tensor.transpose(ps[:, 4 + t, i * P:(i + 1) * P], H[3][:, t, i * P:(i + 1) * P], ident)
                ins.then_inc(S("rT_psum"), 1)
            pe.wait_ge(S("rT_out"), 2)
            for h in range(LH):
                dt, r = h // 2, 64 * (h % 2)
                if h >= 2:
                    pe.wait_ge(S("ret_scored"), h - 1)
                mm(ps[:, 4 + h % 2, 0:SEQ], gT[r:r + 64, 2 + dt, 0:P], gT[r:r + 64, dt, :], start=True, stop=True)
                mm(ps[:, 4 + h % 2, SEQ:384], gT[r:r + 64, 2 + dt, P:SEQ], gT[r:r + 64, dt, P:SEQ], start=True,
                   stop=True).then_inc(S("ret_psum"), 1)
            pe.wait_ge(S("ret_scored"), LH)
            for t in range(NT):
                for h in range(LH):
                    o, sl = ps[:, 6 + t, h * P:(h + 1) * P], slice(h * P, (h + 1) * P)
                    if t == 0:
                        ins = mm(o, ret_score[:, h, 0:P], H[4][:, 0, sl], start=True, stop=True)
                    else:
                        mm(o, ret_score[:, h, P:SEQ], H[4][:, 0, sl], start=True, stop=False)
                        ins = mm(o, ret_score[:, h, SEQ:384], H[4][:, 1, sl], start=False, stop=True)
                ins.then_inc(S("ret_out"), 1)
            pe.wait_ge(S("mix_out"), 6)
            transpose_x(O)
            need_xT()
            output(1)
            pe.wait_ge(S("ln_done"), 3)
            transpose_x(X)
            need_xT()
            pe.wait_ge(S("wr_loaded"), 32)
            pe.wait_ge(S("xT_full"), 8)
            for t in range(NT):
                for k in range(KD):
                    ins = mm(ps[:, 0, 8 * t:8 * t + 8], XT[:, k, t * P:(t + 1) * P], wr[:, k, :],
                             start=(k == 0), stop=(k == KD - 1))
            ins.then_inc(S("route_psum"), 1)
            pe.wait_ge(S("selected"), 2)
            sel = [rt[:, t, 0:NE] for t in range(NT)]
            mm(ps[:, 1, 0:8], before, sel[0], start=True, stop=True)
            mm(ps[:, 1, 8:16], ones, sel[0], start=True, stop=False)
            mm(ps[:, 1, 8:16], before, sel[1], start=False, stop=True)
            mm(ps[:, 1, 16:24], ones, sel[0], start=True, stop=False)
            mm(ps[:, 1, 16:24], ones, sel[1], start=False, stop=True).then_inc(S("rank_psum"), 1)
            pe.wait_ge(S("routed"), 1)

            def need(i, idx, off=0):
                pe.wait_ge(S("lo_done"), i * PASS + off * 6 + (N1 + idx + 1))

            def columns(i, idx, off, bank):
                for h in range(2):
                    need(i, idx + h, off)
                    s = (N1 + idx + h) % SPLIT
                    wh = hi[:, s, :].rearrange("p (k n) -> p k n", k=4)
                    wl = lo[:, s, :].rearrange("p (k n) -> p k n", k=4)
                    for k in range(4):
                        kk = 4 * h + k
                        ins = three(ps[:, bank, :], xh[:, kk, 0:P], xl[:, kk, 0:P], wh[:, k, :], wl[:, k, :],
                                    kk == 0, kk == KD - 1)
                    ins.then_inc(S("piece_used"), 1)

            def h1(i, c, idx, off=0):
                pe.wait_ge(S("e_s"), i * CE + c + 1)
                columns(i, idx, off, 2)

            def h3(i, c, idx, off=0):
                pe.wait_ge(S("e_a"), i * CE + c + 1)
                columns(i, idx, off, 3)

            def turn(i, c):
                pe.wait_ge(S("e_a"), i * CE + c + 2)
                pe.wait_ge(S("e_al"), i * CE + c + 1)
                for k in range(4):
                    ins = nc.tensor.transpose(ps[:, 4, k * P:(k + 1) * P], a1[:, k * P:(k + 1) * P], ident)
                ins.then_inc(S("e_T"), 1)

            def second(i, c, idx, off, first, last):
                pe.wait_ge(S("e_al"), i * CE + c + 2)
                for h in range(2):
                    need(i, idx + h, off)
                    s = (N1 + idx + h) % SPLIT
                    wh = hi[:, s, :].rearrange("p (k n) -> p k n", k=2)
                    wl = lo[:, s, :].rearrange("p (k n) -> p k n", k=2)
                    for n in range(2):
                        for k in range(2):
                            m = 2 * h + k
                            sl = slice(m * P, (m + 1) * P)
                            ins = three(ps[:, n, :], ah[:, sl], al[:, sl], wh[:, k, n * NC:(n + 1) * NC],
                                        wl[:, k, n * NC:(n + 1) * NC], first and m == 0, last and m == 3,
                                        skip_group_check=True)
                    ins.then_inc(S("piece_used"), 1)

            def expert(i):
                pe.wait_ge(S("e_pick"), i + 1)
                pe.wait_ge(S("e_gT"), i + 1)
                for t in range(NT):
                    ins = nc.tensor.transpose(ps[:, 7, t * P:(t + 1) * P], pickg[:, t, :], ident)
                ins.then_inc(S("e_gather"), 1)
                pe.wait_ge(S("e_added"), i * 4 + 1)
                for half in range(2):
                    for k in range(4):
                        kk = 4 * half + k
                        for t in range(NT):
                            ins = mm(ps[:, 5 + half, k * P:(k + 1) * P], X[:, t, kk * P:(kk + 1) * P], pick[:, t, :],
                                     start=(t == 0), stop=(t == NT - 1))
                    ins.then_inc(S("e_gather"), 1)
                pe.wait_ge(S("e_xl"), i * 2 + 2)
                h1(i, 0, 0)
                h3(i, 0, 2)
                pe.wait_ge(S("e_yout"), i + 1)
                h1(i, 1, 4)
                turn(i, 0)
                h3(i, 1, 6)
                second(i, 0, 8, 0, True, False)
                with pe.Fori(2, CE) as c:
                    h1(i, c, 4, c - 1)
                    turn(i, c - 1)
                    h3(i, c, 6, c - 1)
                    second(i, c - 1, 8, c - 1, False, False)
                turn(i, CE - 1)
                second(i, CE - 1, 40, 0, False, True)
                pe.wait_ge(S("e_yout"), i + 2)
                for q in range(4):
                    t, n = q // 2, q % 2
                    if q >= 2:
                        pe.wait_ge(S("e_added"), i * 4 + q)
                    mm(ps[:, 5 + q % 2, :], pickgT[:, t * P:(t + 1) * P], ysb[:, n * NC:(n + 1) * NC],
                       start=True, stop=True).then_inc(S("e_scatter"), 1)

            with pe.Fori(0, NE) as i:
                expert(i)
            n_extra = pe.value_load(ctrl[0:1, 0:1], min_val=0, max_val=EXTRA)
            with pe.Fori(0, EXTRA) as j:
                with pe.If(j < n_extra):
                    expert(j + NE)
            pe.wait_ge(S("ln_done"), 4)
            transpose_x(X)
            need_xT()
            ple(1, lambda g: pe.wait_ge(S("lo_done"), (n_extra + NE) * PASS + (g + 1)), N1)


_INS = ['x', 'p', 'rel_bias', 'even_w_in', 'gla_w_gate', 'gla_b_gate', 'gla_norm', 'even_w_out',
        'odd_w_in', 'hgrn_gamma', 'hgrn_norm', 'ret_norm', 'odd_w_out', 'ln_mix_g', 'ln_mix_b',
        'ln_ffn_g', 'ln_ffn_b', 'ffn_w1', 'ffn_w3', 'ffn_w2', 'router_w', 'router_b', 'expert_w1',
        'expert_w3', 'expert_w2', 'ple_w_gate', 'ple_w_proj']


def kernel(**inputs):
    import concourse.bacc as bacc
    from concourse.bass_utils import run_bass_kernel_spmd

    nc = bacc.Bacc("TRN2", target_bir_lowering=False, num_devices=1)
    arrays, args = {}, []
    tables = dict(zip(("tab", "masks", "decay", "hot"), constants()))
    for name in _INS + list(tables):
        a = np.ascontiguousarray(tables[name] if name in tables else inputs[name])
        arrays[f"in_{name}"] = a
        args.append(nc.dram_tensor(f"in_{name}", a.shape, mybir.dt.from_np(a.dtype), kind="ExternalInput").ap())
    out = nc.dram_tensor("out_x", (1, SEQ, D), F32, kind="ExternalOutput").ap()
    trunk(nc, *args, out)
    r = run_bass_kernel_spmd(nc, [arrays], core_ids=[0])
    return r.results[0]["out_x"]
```

```python
from contextlib import ExitStack
import math

import numpy as np

import concourse.bass as bass
from concourse import mybir

F32 = mybir.dt.float32
F32R = mybir.dt.float32r
I32 = mybir.dt.int32
U32 = mybir.dt.uint32
U8 = mybir.dt.uint8
ALU = mybir.AluOpType
ACT = mybir.ActivationFunctionType
AX_X = mybir.AxisListType.X

P = 128
SEQ = 256
NT = SEQ // P
D = 1024
KD = D // P
NC = 512
DEPTH = 2
ALPHA = (2.0 * DEPTH) ** 0.25
LN_EPS = 1e-5
HEAD_EPS = 1e-6
MH, MD = 8, 64
LH, LK, LV = 4, 64, 128
BUCKETS, MAX_DIST = 32, 128
RANK = 16
FFN = 2752
NE = 8
FE = 3584
CE = FE // NC
EXTRA = 3
PLE = 256
LEVELS = 7
RAW, SPLIT = 6, 3
PIECE = 2048
NEG = -1e30

C_ID, C_IOTA, C_BEFORE, C_ONE = 0, 128, 256, 384
C_SUM = 512
C_COS = C_SUM + 9 * P
C_SIN = C_COS + NT * 32
C_SMALL = C_SIN + NT * 32
C_ALL = C_SMALL + 4


def constants():
    c = np.zeros((P, C_ALL), np.float32)
    i = np.arange(P)
    c[:, C_ID:C_ID + P] = np.eye(P)
    c[:, C_IOTA:C_IOTA + P] = i[None, :]
    c[:, C_BEFORE:C_BEFORE + P] = i[:, None] < i[None, :]
    c[:, C_ONE:C_ONE + P] = 1.0
    masks = np.zeros((P, LEVELS, P), np.float32)
    s, t = i[:, None], i[None, :]
    for level in range(LEVELS):
        half = 1 << level
        mid = t // (2 * half) * 2 * half + half
        right = t >= mid
        c[:, C_SUM + level * P:C_SUM + (level + 1) * P] = np.where(
            right, (s >= mid) & (s <= t), (s > t) & (s < mid))
        masks[:, level, :] = (s // (2 * half) == t // (2 * half)) & (s < mid) & right
    c[:, C_SUM + 7 * P:C_SUM + 8 * P] = s > t
    c[:, C_SUM + 8 * P:C_SUM + 9 * P] = s <= t
    half_dim = 32
    inv = (10000.0 ** (-np.arange(half_dim, dtype=np.float32) / np.float32(half_dim))).astype(np.float32)
    ang = np.arange(SEQ, dtype=np.float32)[:, None] * inv[None, :]
    for tile in range(NT):
        c[:, C_COS + 32 * tile:C_COS + 32 * tile + 32] = np.cos(ang[P * tile:P * tile + P])
        c[:, C_SIN + 32 * tile:C_SIN + 32 * tile + 32] = np.sin(ang[P * tile:P * tile + P])
    c[:, C_SMALL:] = [LN_EPS, HEAD_EPS, 1.0, 0.0]
    log_g = np.log1p(-np.exp2(-5.0 - np.arange(LH)))
    rel = np.arange(SEQ)[None, :] - i[:, None]
    dm = np.where(rel[:, None, :] >= 0, np.exp(np.maximum(rel, 0)[:, None, :] * log_g[None, :, None]), 0.0)
    dm = dm * LK ** -0.5
    decay = np.concatenate([dm, dm[:, :, 0:P]], axis=2).astype(np.float32)
    dist = np.arange(-127, 256)
    n = np.maximum(dist, 0)
    nf = np.maximum(n, 1).astype(np.float32)
    large = 16 + (np.log(nf / np.float32(16)) / np.float32(math.log(MAX_DIST / 16)) * np.float32(16)).astype(np.int32)
    bucket = np.where(n < 16, n, np.minimum(large, BUCKETS - 1))
    hot = np.zeros((BUCKETS + 1, 384), np.float32)
    hot[bucket, dist + 127] = dist >= 0
    hot[BUCKETS, dist + 127] = dist < 0
    return c, masks, decay, hot


class Piece:

    def __init__(self, src, rows, k, n):
        self.src, self.rows, self.k, self.n = src, rows, k, n


def column_pieces(w, n0, width):
    v = w.rearrange("(k p) n -> p k n", p=P)
    return [Piece(v[:, 4 * h:4 * h + 4, n0:n0 + width], P, 4, width) for h in range(2)]


def row_piece(w, f0):
    v = w[f0:f0 + 2 * P, :].rearrange("(k p) n -> p k n", p=P)
    return Piece(v, P, 2, D)


def trunk(nc, x, p, rel_bias, even_w_in, gla_w_gate, gla_b_gate, gla_norm, even_w_out, odd_w_in,
          hgrn_gamma, hgrn_norm, ret_norm, odd_w_out, ln_mix_g, ln_mix_b, ln_ffn_g, ln_ffn_b,
          ffn_w1, ffn_w3, ffn_w2, router_w, router_b, expert_w1, expert_w3, expert_w2,
          ple_w_gate, ple_w_proj, tab, masks, decay, hot, out, debug=None):
    even_cols = [0, 512, 1024, 1536, 2048, 2576]
    pieces = []
    where = {}

    def add(name, some):
        where[name] = len(pieces)
        pieces.extend(some)

    for j, n0 in enumerate(even_cols):
        add(("in", 0, j), column_pieces(even_w_in[0], n0, NC))
    for n in range(2):
        add(("out", 0, n), column_pieces(even_w_out[0], n * NC, NC))
    CF = -(-FFN // NC)

    def ffn_w2_pieces(c):
        if c < CF - 1:
            return [row_piece(ffn_w2[0], c * NC), row_piece(ffn_w2[0], c * NC + 2 * P)]
        rest = FFN - c * NC - P
        v = ffn_w2[0]
        return [Piece(v[c * NC:c * NC + P, :].rearrange("(k p) n -> p k n", p=P), P, 1, D),
                Piece(v[c * NC + P:FFN, :].rearrange("(k p) n -> p k n", p=rest), rest, 1, D)]

    for c in range(CF + 1):
        if c < CF:
            width = min(NC, FFN - c * NC)
            add(("w1", c), column_pieces(ffn_w1[0], c * NC, width))
            add(("w3", c), column_pieces(ffn_w3[0], c * NC, width))
        if c > 0:
            add(("w2", c - 1), ffn_w2_pieces(c - 1))

    def add_ple(i):
        add(("proj", i), [row_piece(ple_w_proj[i], 0)])
        for n in range(2):
            add(("gate", i, n), column_pieces(ple_w_gate[i], n * NC, NC))

    add_ple(0)
    for j in range(6):
        add(("in", 1, j), column_pieces(odd_w_in[0], j * NC, NC))
    for n in range(2):
        add(("out", 1, n), column_pieces(odd_w_out[0], n * NC, NC))
    N1 = len(pieces)
    PASS = 6 * CE
    before_tail = list(pieces)
    add_ple(1)
    tail = pieces[N1:]
    pieces = before_tail
    T0 = N1 + (NE + EXTRA) * PASS

    with ExitStack() as ctx:
        def sb(name, shape, dt=F32):
            return ctx.enter_context(nc.sbuf_tensor(name, shape, dt))

        sems = {}

        def S(name):
            if name not in sems:
                sems[name] = ctx.enter_context(nc.semaphore(name))
            return sems[name]

        raw = sb("raw", [P, RAW, PIECE])
        hi = sb("hi", [P, SPLIT, PIECE], F32R)
        lo = sb("lo", [P, SPLIT, PIECE], F32R)
        X = sb("X", [P, NT, D])
        xh = sb("xh", [P, KD, SEQ], F32R)
        xl = sb("xl", [P, KD, SEQ], F32R)
        ah = sb("ah", [P, 1024], F32R)
        al = sb("al", [P, 1024], F32R)
        XO = sb("XO", [P, 2048])
        lnp = sb("lnp", [P, 2, D])
        T = sb("T", [P, C_ALL])
        mask_sb = sb("mask_sb", [P, LEVELS, P], U8)
        st = sb("st", [P, 256])
        ctrl = sb("ctrl", [P, 8], I32)
        W = sb("W", [P, 13824])
        bias_dram = nc.dram_tensor("bias_rows", [MH, 384], F32).ap()
        ps = ctx.enter_context(nc.psum_tensor("ps", [P, 8, NC], F32))

        XT = XO[:].rearrange("p (k t) -> p k t", k=KD)
        O = XO[:].rearrange("p (t n) -> p t n", t=NT)
        ident = T[:, C_ID:C_ID + P]
        iota = T[:, C_IOTA:C_IOTA + P]
        before = T[:, C_BEFORE:C_BEFORE + P]
        ones = T[:, C_ONE:C_ONE + P]
        eps_ln = T[:, C_SMALL:C_SMALL + 1]
        eps_head = T[:, C_SMALL + 1:C_SMALL + 2]

        def arena(w0, *shape):
            n = int(np.prod(shape))
            v = W[:, w0:w0 + n]
            if len(shape) == 2:
                v = v.rearrange("p (a b) -> p a b", a=shape[0])
            if len(shape) == 3:
                v = v.rearrange("p (a b c) -> p a b c", a=shape[0], b=shape[1])
            return v

        H = [arena(w0, NT, NC) for w0 in (4096, 5120, 0, 1024, 2048, 3072)]
        logits = arena(4096, MH, 384)
        bias_t = arena(7168, MH, SEQ)
        qkT = arena(9216, 2, 4, SEQ)
        PT = [arena(12288 + 384 * b, 384) for b in range(2)]
        E = arena(7168, 2 * 8, SEQ)
        gT = arena(11264, 2 * 2, SEQ)
        gT2 = gT
        normw = arena(13312, NC)
        gla_b = arena(13056, SEQ)
        la = {0: arena(4096, NT, SEQ), 1: arena(6144, NT, SEQ)}
        SC = {0: arena(4608, LH, P), 1: arena(6144, LH, P)}
        tmp = {0: [arena(5120, NC), arena(5632, NC)], 1: [arena(12288, NC), arena(12800, NC)]}
        score = {0: H[3], 1: H[0]}
        lb, oml = arena(6656, SEQ), arena(6912, SEQ)
        ret_score = arena(7168, LH, 384)
        ret_decay = arena(8704, LH, 384)
        p_sb = arena(4096, NT, PLE)
        PW = arena(7168, 4, NC)
        s1T, aT = arena(0, 1024), arena(1024, 1024)
        XR = arena(0, KD, SEQ)
        s1, a1, ysb = arena(0, NC), arena(512, NC), arena(1024, 1024)
        pick, pickg, pickgT = arena(2048, NT, P), arena(2304, NT, P), arena(2560, SEQ)
        PASSES = NE + EXTRA + 1
        posm, gates = arena(2816, NT, PASSES), arena(2816 + NT * PASSES, NT, PASSES)
        wr = arena(5120, KD, NE)
        br = arena(5184, NE)
        rt = arena(5200, 16, 16)
        count_of = rt[:, 12, 0:8]
        wga = lnp[:, 0, 0:P].rearrange("p (k n) -> p k n", k=KD)
        wgate, gaT = lnp[:, 0, P:P + SEQ], lnp[:, 0, P + SEQ:P + 2 * SEQ]
        relb = sb("relb", [33, MH])
        masks_f = arena(9984, LEVELS, P)
        hot_sb = arena(9216, 384)
        row_sb = arena(9600, 384)

        block = ctx.enter_context(nc.Block())

        def count_from_one(eng, *names):
            for name in names:
                eng.sem_inc(S(name), 1)

        def multiplied(eng, name, k=2):
            eng.wait_ge(S("piece_used"), where[name] + k)

        def landed(g):
            return 16 * (g // RAW + 1)

        @block.sync
        def _(sp):
            def load(slot, pc_src, n, rows, ready):
                sp.dma_start(raw[0:rows, slot, 0:n].rearrange("p (k n) -> p k n", k=pc_src.shape[1]),
                             pc_src).then_inc(S(f"loaded{slot}"), 16)

            sp.dma_start(X[:], x[0].rearrange("(t p) n -> p t n", p=P)).then_inc(S("x_loaded"), 16)
            sp.dma_start(T[:], tab).then_inc(S("tab_loaded"), 16)
            for g, pc in enumerate(pieces):
                if g >= RAW:
                    sp.wait_ge(S("lo_done"), g - RAW + 1)
                load(g % RAW, pc.src, pc.k * pc.n, pc.rows, None)

            w1 = expert_w1[0].rearrange("e (k p) n -> p e k n", p=P)
            w3 = expert_w3[0].rearrange("e (k p) n -> p e k n", p=P)
            w2 = expert_w2[0].rearrange("e (k p) n -> p e k n", p=P)

            def expert_piece(i, e, idx, off, src):
                slot = (N1 + idx) % RAW
                sp.wait_ge(S("lo_done"), i * PASS + off + (N1 + idx - RAW + 1))
                sp.dma_start(raw[:, slot, :].rearrange("p (k n) -> p k n", k=src.shape[2]),
                             src.rearrange("p e k n -> p (e k) n")).then_inc(S(f"loaded{slot}"), 16)

            def columns(w, e, c, h):
                return w[:, bass.ds(e, 1), 4 * h:4 * h + 4, bass.ds(c * NC, NC)]

            def rows(e, c, h):
                return w2[:, bass.ds(e, 1), bass.ds(c * 4 + 2 * h, 2), :]

            def expert(i, e):
                for j, w in enumerate((w1, w3)):
                    for h in range(2):
                        expert_piece(i, e, 2 * j + h, 0, columns(w, e, 0, h))
                with sp.Fori(1, CE) as c:
                    for j, w in enumerate((w1, w3)):
                        for h in range(2):
                            expert_piece(i, e, 4 + 2 * j + h, (c - 1) * 6, columns(w, e, c, h))
                    for h in range(2):
                        expert_piece(i, e, 8 + h, (c - 1) * 6, rows(e, c - 1, h))
                for h in range(2):
                    expert_piece(i, e, 40 + h, 0, rows(e, CE - 1, h))

            with sp.Fori(0, NE) as i:
                expert(i, i)
            sp.wait_ge(S("routed"), 1)
            n_extra = sp.value_load(ctrl[0:1, 0:1], min_val=0, max_val=EXTRA)
            with sp.Fori(0, EXTRA) as j:
                with sp.If(j < n_extra):
                    e = sp.value_load(ctrl[0:1, bass.ds(j + 1, 1)], min_val=0, max_val=NE - 1)
                    expert(j + NE, e)
            for u, pc in enumerate(tail):
                slot = (N1 + u) % RAW
                sp.wait_ge(S("lo_done"), (n_extra + NE) * PASS + (N1 + u - RAW + 1))
                load(slot, pc.src, pc.k * pc.n, pc.rows, None)
            for n in range(2):
                sp.wait_ge(S("ple_x"), 4 + 2 * (n + 1))
                sp.dma_start(out[0].rearrange("(t p) n -> p t n", p=P)[:, :, n * NC:(n + 1) * NC],
                             X[:, :, n * NC:(n + 1) * NC]).then_inc(S("stored"), 16)
            sp.wait_ge(S("stored"), 32)

        assert PASS % RAW == 0 and PASS % SPLIT == 0

        @block.gpsimd
        def _(pool):
            def small(dst, src, name):
                pool.dma_start(dst, src).then_inc(S(name), 16)

            def on_all(v, n):
                return v.rearrange("(a n) -> a n", a=1).partition_broadcast(P).rearrange("p a n -> p (a n)")

            small(relb[0:32, :], rel_bias, "hot_loaded")
            small(hot_sb[0:33, :], hot, "hot_loaded")
            small(masks_f, masks, "mask_loaded")
            pool.wait_ge(S("mask_loaded"), 16)
            nc.gpsimd.tensor_copy(mask_sb[:], masks_f).then_inc(S("mask_ready"), 1)
            small(wga, even_w_in[0].rearrange("(k p) n -> p k n", p=P)[:, :, 2560:2560 + RANK], "ga_loaded")
            small(wgate[0:RANK, :], gla_w_gate[0], "ga_loaded")
            small(gla_b, on_all(gla_b_gate[0], SEQ), "ga_loaded")
            small(normw, on_all(gla_norm[0], NC), "normw_loaded")
            pool.wait_ge(S("row_ready"), 1)
            small(bias_dram, row_sb[0:MH, :], "row_stored")
            pool.wait_ge(S("row_stored"), 16)
            for q in range(MH):
                toeplitz = bass.AP(bias_dram.tensor, q * 384, [[1, P], [1, SEQ]])
                small(bias_t[:, q, :], toeplitz, "bias_loaded")
            pool.wait_ge(S("z_psum"), 1)
            small(lnp[:, 0, :], on_all(ln_mix_g[0], D), "lnp_loaded")
            small(lnp[:, 1, :], on_all(ln_mix_b[0], D), "lnp_loaded")
            def dump(k):
                if debug is not None:
                    small(debug[k].rearrange("(t p) n -> p t n", p=P), X[:], "dump")
            if debug is not None:
                pool.wait_ge(S("mix_out"), 2)
                small(debug[0].rearrange("(t p) n -> p t n", p=P), O, "dump")
            pool.wait_ge(S("ln_x"), 2)
            dump(1)
            small(lnp[:, 0, :], on_all(ln_ffn_g[0], D), "lnp_loaded")
            small(lnp[:, 1, :], on_all(ln_ffn_b[0], D), "lnp_loaded")
            small(p_sb[:], p[0, 0].rearrange("(t p) n -> p t n", p=P), "p_loaded")
            small(normw, on_all(hgrn_norm[0], NC), "normw_loaded")
            small(lb, on_all(hgrn_gamma[0], SEQ), "gamma_loaded")
            small(oml, on_all(hgrn_gamma[1], SEQ), "gamma_loaded")
            pool.wait_ge(S("ln_x"), 4)
            if debug is not None:
                pool.wait_ge(S("ple_x"), 4)
            dump(2)
            small(lnp[:, 0, :], on_all(ln_mix_g[1], D), "lnp_loaded")
            small(lnp[:, 1, :], on_all(ln_mix_b[1], D), "lnp_loaded")
            pool.wait_ge(S("hgrn_done"), 1)
            small(ret_decay[:], decay, "decay_loaded")
            small(normw, on_all(ret_norm[0], NC), "normw_loaded")
            if debug is not None:
                pool.wait_ge(S("mix_out"), 6)
                small(debug[3].rearrange("(t p) n -> p t n", p=P), O, "dump")
            pool.wait_ge(S("ln_x"), 6)
            dump(4)
            small(lnp[:, 0, :], on_all(ln_ffn_g[1], D), "lnp_loaded")
            small(lnp[:, 1, :], on_all(ln_ffn_b[1], D), "lnp_loaded")
            small(p_sb[:], p[1, 0].rearrange("(t p) n -> p t n", p=P), "p_loaded")
            small(wr[:], router_w[0].rearrange("(k p) n -> p k n", p=P), "wr_loaded")
            small(br, on_all(router_b[0], NE), "wr_loaded")
            G = nc.gpsimd
            steps = [0]

            def fin(ins):
                steps[0] += 1
                ins.then_inc(S("pool_step"), 1)
                pool.wait_ge(S("pool_step"), steps[0])

            def total(dst, v):
                fin(G.tensor_tensor(v[:, 0:4], v[:, 0:4], v[:, 4:8], ALU.add))
                fin(G.tensor_tensor(v[:, 0:2], v[:, 0:2], v[:, 2:4], ALU.add))
                fin(G.tensor_tensor(dst, v[:, 0:1], v[:, 1:2], ALU.add))

            pool.wait_ge(S("ranked"), NT)
            pool.wait_ge(S("e_pick"), 1)
            over, upto, rank, pick1 = rt[:, 13, 0:8], rt[:, 13, 8:16], rt[:, 14, 0:8], rt[:, 14, 8:16]
            part, listf = rt[:, 15, 0:8], rt[:, 12, 8:16]
            fin(G.tensor_scalar(over, count_of, float(P) + 0.5, None, ALU.is_gt))
            fin(G.tensor_copy(upto, over))
            for e in range(1, NE):
                fin(G.tensor_tensor(upto[:, e:e + 1], upto[:, e - 1:e], over[:, e:e + 1], ALU.add))
            fin(G.tensor_tensor(rank, upto, over, ALU.subtract))
            fin(G.memset(listf, 0.0))
            fin(G.tensor_copy(listf[:, 0:1], upto[:, 7:8]))
            for j in range(EXTRA):
                fin(G.tensor_scalar(pick1, rank, float(j), None, ALU.is_equal))
                fin(G.tensor_tensor(pick1, pick1, over, ALU.mult))
                fin(G.tensor_tensor(part, pick1, iota[:, 0:NE], ALU.mult))
                total(listf[:, j + 1:j + 2], part)
                for t in range(NT):
                    fin(G.tensor_scalar(part, posm[:, t, 0:NE], -float(P), None, ALU.add))
                    fin(G.tensor_tensor(part, part, pick1, ALU.mult))
                    total(posm[:, t, NE + j:NE + j + 1], part)
                    fin(G.tensor_tensor(part, gates[:, t, 0:NE], pick1, ALU.mult))
                    total(gates[:, t, NE + j:NE + j + 1], part)
            G.tensor_copy(ctrl[:, 0:8], listf).then_inc(S("routed"), 1)

        @block.scalar
        def _(act):
            count_from_one(act, "e_gT", "e_yout", "e_s")
            count = {}

            def inc(ins, name):
                count[name] = count.get(name, 0) + 1
                ins.then_inc(S(name), 1)

            def fin(ins, name="act_step"):
                inc(ins, name)
                act.wait_ge(S(name), count[name])

            def copy(o, i, scale=1.0):
                return nc.scalar.activation(o, i, ACT.Copy, scale=scale)

            def split(g, pc):
                act.wait_ge(S(f"loaded{g % RAW}"), landed(g))
                if g >= SPLIT:
                    act.wait_ge(S("piece_used"), g - SPLIT + 1)
                n = pc.k * pc.n
                copy(hi[0:pc.rows, g % SPLIT, 0:n], raw[0:pc.rows, g % RAW, 0:n]).then_inc(S("hi_done"), 1)

            split_n = [0]

            def split_all(name, k=2):
                while split_n[0] < where[name] + k:
                    split(split_n[0], pieces[split_n[0]])
                    split_n[0] += 1

            nxt = [0]

            def transposed(keep=None):
                for q in range(4):
                    act.wait_ge(S("xT_psum"), nxt[0] + 1)
                    nxt[0] += 1
                    t, half = q // 2, q % 2
                    src = ps[:, 4 + q, :].rearrange("p (k t) -> p k t", k=4)
                    if keep is not None:
                        copy(keep[:, 4 * half:4 * half + 4, t * P:(t + 1) * P], src).then_inc(S("xT_full"), 1)
                    copy(xh[:, 4 * half:4 * half + 4, t * P:(t + 1) * P], src).then_inc(S("xT_hi"), 1)

            proj_n = [0]

            def projected(layer, j, how):
                n = proj_n[0]
                proj_n[0] += 1
                multiplied(act, ("in", layer, j))
                for t in range(NT):
                    src = ps[:, 2 * (n % 2) + t, :]
                    if how == "forget":
                        copy(H[j][:, t, 0:SEQ], src[:, 0:SEQ])
                        ins = nc.scalar.activation(H[j][:, t, SEQ:NC], src[:, SEQ:NC], ACT.Sigmoid)
                    elif how == "silu":
                        ins = nc.scalar.activation(H[j][:, t, :], src, ACT.Silu)
                    else:
                        ins = copy(H[j][:, t, :], src)
                    ins.then_inc(S("proj_out"), 1)

            def decays(layer):
                for t in range(NT):
                    act.wait_ge(S("gT_psum"), 2 * layer + t + 1)
                    src = ps[:, 4 + t, :].rearrange("p (i t) -> p i t", i=4)
                    copy(gT[:, 0:2, t * P:(t + 1) * P], src[:, 0:2, :], scale=LK ** -0.5 if layer == 0 else 1.0)
                    copy(gT[:, 2:4, t * P:(t + 1) * P], src[:, 2:4, :]).then_inc(S("gT_out"), 1)
                n = 0
                for dt in range(2):
                    for t in range(NT):
                        for half in range(2):
                            act.wait_ge(S("sum_psum"), 8 * layer + n + 1)
                            nc.scalar.activation(
                                E[:, 8 * dt + 4 * half:8 * dt + 4 * half + 4, t * P:(t + 1) * P],
                                ps[:, 4 + n % 4, :].rearrange("p (l t) -> p l t", l=4), ACT.Exp,
                                scale=1.0 / 16 if layer == 0 else 1.0).then_inc(S("decay_out"), 1)
                            n += 1

            def join_out(layer):
                act.wait_ge(S("join_psum"), layer + 1)
                copy(SC[layer].rearrange("p (b d) t -> p b (d t)", b=2), ps[:, 4:6, 0:SEQ]).then_inc(S("join_out"), 1)

            norm_n = [0]

            def head_norm(banks, k):
                for t in range(NT):
                    n = norm_n[0]
                    norm_n[0] += 1
                    act.wait_ge(S("sumsq"), n + 1)
                    v = st[:, 64 + 4 * t:68 + 4 * t]
                    fin(nc.scalar.activation(v, v, ACT.Ln, bias=eps_head, scale=1.0 / LV))
                    nc.scalar.activation(v, v, ACT.Exp, scale=-0.5).then_inc(S("head_rstd"), 1)

            ln_n = [0]

            def layer_norm():
                n = ln_n[0]
                ln_n[0] += 1
                for t in range(NT):
                    act.wait_ge(S("ln_var"), 2 * n + t + 1)
                    v = st[:, 84 + t:85 + t]
                    fin(nc.scalar.activation(v, st[:, 81 + 2 * t:82 + 2 * t], ACT.Ln, bias=eps_ln))
                    nc.scalar.activation(v, v, ACT.Exp, scale=-0.5).then_inc(S("ln_rstd"), 1)

            def ple_p(i):
                act.wait_ge(S("pT_psum"), i + 1)
                copy(ah[:, 0:NC], ps[:, 4, :]).then_inc(S("pT_hi"), 1)

            def ple_out(i, used):
                used()
                for b in range(4):
                    copy(PW[:, b, :], ps[:, 4 + b, :]).then_inc(S("p_out"), 1)

            def ple_gate(n, used):
                used()
                for t in range(NT):
                    nc.scalar.activation(O[:, t, n * NC:(n + 1) * NC], ps[:, 2 * n + t, :],
                                         ACT.Sigmoid).then_inc(S("gate_out"), 1)

            act.wait_ge(S("tab_loaded"), 16)
            transposed(XT)
            split_all(("in", 0, 0))
            split_all(("in", 0, 1))
            projected(0, 0, "copy")
            act.wait_ge(S("gaT_psum"), 1)
            copy(gaT[0:RANK, :], ps[0:RANK, 4, 0:SEQ]).then_inc(S("gaT_out"), 1)
            split_all(("in", 0, 2))
            projected(0, 1, "copy")
            act.wait_ge(S("row_stored"), 16)
            act.wait_ge(S("mask_ready"), 1)
            for i in range(2):
                for t in range(NT):
                    act.wait_ge(S("mT_psum"), 2 * i + t + 1)
                    copy(qkT[:, i, :, t * P:(t + 1) * P],
                         ps[:, 4 + 2 * i + t, :].rearrange("p (g t) -> p g t", g=4)).then_inc(S("mT_out"), 1)
            split_all(("in", 0, 3))
            projected(0, 2, "copy")
            split_all(("in", 0, 4))
            for h in range(MH):
                for t in range(NT):
                    act.wait_ge(S("row_max"), 1)
                    sl = logits[:, h, 0:P] if t == 0 else logits[:, h, P:384]
                    nc.scalar.activation(sl, sl, ACT.Exp, bias=st[:, 16 + t * 8 + h:17 + t * 8 + h],
                                         accum_out=st[:, 32 + t * 8 + h:33 + t * 8 + h]).then_inc(S("exp_done"), 1)
            projected(0, 3, "copy")
            split_all(("in", 0, 5))
            projected(0, 4, "copy")
            projected(0, 5, "silu")
            for t in range(NT):
                act.wait_ge(S("gate_abs"), t + 1)
                v = tmp[0][t][:, 0:SEQ]
                fin(nc.scalar.activation(v, v, ACT.Exp))
                nc.scalar.activation(v, v, ACT.Ln, bias=1.0).then_inc(S("softplus"), 1)
            decays(0)
            split_all(("out", 0, 0))
            join_out(0)
            def squares(banks, k):
                for t in range(NT):
                    act.wait_ge(S("lin_psum"), 2 * k + t + 1)
                    nc.scalar.activation(tmp[0 if k == 0 else 1][t], ps[:, banks + t, :],
                                         ACT.Square).then_inc(S("squares"), 1)
            squares(6, 0)
            head_norm(6, 0)
            transposed()
            split_all(("out", 0, 0))
            split_all(("out", 0, 1))
            split_all(("w1", 0))
            layer_norm()
            transposed()
            def units(c):
                return -(-min(NC, FFN - c * NC) // P) * SEQ

            for c in range(CF + 1):
                if c < CF:
                    split_all(("w1", c))
                if c > 0:
                    act.wait_ge(S("a_done"), c)
                    if c > 1:
                        multiplied(act, ("w2", c - 2))
                    copy(ah[:, 0:units(c - 1)], aT[:, 0:units(c - 1)]).then_inc(S("ah_done"), 1)
                if c < CF:
                    split_all(("w3", c))
                    multiplied(act, ("w1", c))
                    if c > 0:
                        act.wait_ge(S("a_done"), c)
                    for b in range(0, units(c), NC):
                        ins = nc.scalar.activation(s1T[:, b:b + NC], ps[:, 4 + b // NC, :], ACT.Silu)
                    ins.then_inc(S("s_done"), 1)
                if c > 0:
                    split_all(("w2", c - 1))
            split_all(("proj", 0), 1)
            ple_p(0)
            split_all(("gate", 0, 0), 1)
            layer_norm()
            split_all(("gate", 0, 0))
            ple_out(0, lambda: multiplied(act, ("proj", 0), 1))
            transposed()
            split_all(("gate", 0, 1))
            ple_gate(0, lambda: multiplied(act, ("gate", 0, 0)))
            split_all(("in", 1, 0))
            ple_gate(1, lambda: multiplied(act, ("gate", 0, 1)))
            transposed()
            act.wait_ge(S("gamma_diff"), 1)
            nc.scalar.activation(lb, lb, ACT.Sigmoid).then_inc(S("lb_done"), 1)
            for j in range(6):
                split_all(("in", 1, j))
                if j > 0:
                    projected(1, j - 1, {0: "forget", 2: "silu"}.get(j - 1, "copy"))
            projected(1, 5, "silu")
            act.wait_ge(S("forget"), 1)
            for t in range(NT):
                nc.scalar.activation(la[1][:, t, :], la[1][:, t, :], ACT.Ln).then_inc(S("log_f"), 1)
            decays(1)
            split_all(("out", 1, 0))
            join_out(1)
            squares(6, 1)
            head_norm(6, 1)
            for t in range(NT):
                act.wait_ge(S("rT_psum"), t + 1)
                copy(gT[:, :, t * P:(t + 1) * P],
                     ps[:, 4 + t, :].rearrange("p (i t) -> p i t", i=4)).then_inc(S("rT_out"), 1)
            for t in range(NT):
                act.wait_ge(S("ret_centred"), t + 1)
                nc.scalar.activation(tmp[1][t], H[3][:, t, :], ACT.Square).then_inc(S("squares"), 1)
            head_norm(6, 2)
            transposed()
            split_all(("out", 1, 0))
            split_all(("out", 1, 1))
            layer_norm()
            for q in range(4):
                act.wait_ge(S("xT_psum"), nxt[0] + 1)
                nxt[0] += 1
                t, half = q // 2, q % 2
                copy(XR[:, 4 * half:4 * half + 4, t * P:(t + 1) * P],
                     ps[:, 4 + q, :].rearrange("p (k t) -> p k t", k=4)).then_inc(S("xT_full"), 1)

            def xsplit(i, idx, off=0):
                g = N1 + idx
                act.wait_ge(S(f"loaded{g % RAW}"), i * (16 * PASS // RAW) + off * 16 + landed(g))
                act.wait_ge(S("piece_used"), i * PASS + off * 6 + (g - SPLIT + 1))
                copy(hi[:, g % SPLIT, :], raw[:, g % RAW, :]).then_inc(S("hi_done"), 1)

            def expert_silu(i, c):
                act.wait_ge(S("piece_used"), i * PASS + (c * 6 + N1 if not (isinstance(c, int) and c == 0) else N1 + 2))
                act.wait_ge(S("e_a"), i * CE + c + 1)
                nc.scalar.activation(s1, ps[:, 2, :], ACT.Silu).then_inc(S("e_s"), 1)

            def expert_xh(i, half):
                act.wait_ge(S("e_gather"), i * 3 + (3 + half))
                copy(xh[:, 4 * half:4 * half + 4, 0:P],
                     ps[:, 5 + half, :].rearrange("p (k t) -> p k t", k=4)).then_inc(S("e_xh"), 1)

            def expert_ah(i, c):
                act.wait_ge(S("e_T"), i * CE + c + 2)
                copy(ah[:, 0:NC], ps[:, 4, :]).then_inc(S("e_ah"), 1)

            def expert(i):
                xsplit(i, 2)
                act.wait_ge(S("e_gather"), i * 3 + 2)
                act.wait_ge(S("e_scatter"), i * 4 + 1)
                copy(pickgT, ps[:, 7, 0:SEQ]).then_inc(S("e_gT"), 1)
                xsplit(i, 3)
                expert_silu(i, 0)
                with act.Fori(1, CE) as c:
                    for j in range(4):
                        xsplit(i, 4 + j, c - 1)
                    expert_ah(i, c - 1)
                    expert_silu(i, c)
                    for j in range(2):
                        xsplit(i, 8 + j, c - 1)
                xsplit(i, 40)
                xsplit(i, 41)
                expert_ah(i, CE - 1)
                xsplit(i, PASS)
                expert_xh(i + 1, 0)
                expert_xh(i + 1, 1)
                xsplit(i, PASS + 1)
                act.wait_ge(S("piece_used"), i * PASS + (N1 + PASS))
                copy(ysb, ps[:, 0:2, :].rearrange("p a n -> p (a n)")).then_inc(S("e_yout"), 1)

            xsplit(0, 0)
            xsplit(0, 1)
            for t in range(NT):
                act.wait_ge(S("top_diff"), t + 1)
                nc.scalar.activation(rt[:, 4 + t, 0:1], rt[:, 4 + t, 0:1], ACT.Exp).then_inc(S("top_exp"), 1)
            expert_xh(0, 0)
            expert_xh(0, 1)
            with act.Fori(0, NE) as i:
                expert(i)
            act.wait_ge(S("routed"), 1)
            n_extra = act.value_load(ctrl[0:1, 0:1], min_val=0, max_val=EXTRA)
            with act.Fori(0, EXTRA) as j:
                with act.If(j < n_extra):
                    expert(j + NE)

            def tail_split(u):
                g = N1 + u
                act.wait_ge(S(f"loaded{g % RAW}"), (n_extra + NE) * (16 * PASS // RAW) + landed(g))
                act.wait_ge(S("piece_used"), (n_extra + NE) * PASS + (g - SPLIT + 1))
                copy(hi[:, g % SPLIT, :], raw[:, g % RAW, :]).then_inc(S("hi_done"), 1)

            def tail_used(u):
                return lambda: act.wait_ge(S("piece_used"), (n_extra + NE) * PASS + (N1 + u))

            ple_p(1)
            layer_norm()
            tail_split(2)
            ple_out(1, tail_used(1))
            transposed()
            tail_split(3)
            tail_split(4)
            ple_gate(0, tail_used(3))
            ple_gate(1, tail_used(5))

        @block.vector
        def _(dve):
            count_from_one(dve, "e_added", "e_a", "e_al")
            count = {}
            V = nc.vector

            def inc(ins, name):
                count[name] = count.get(name, 0) + 1
                ins.then_inc(S(name), 1)

            def fin(ins, name="dve_step"):
                inc(ins, name)
                dve.wait_ge(S(name), count[name])

            def rest(g, pc):
                n = pc.k * pc.n
                dve.wait_ge(S("hi_done"), g + 1)
                V.tensor_tensor(lo[0:pc.rows, g % SPLIT, 0:n], raw[0:pc.rows, g % RAW, 0:n],
                                hi[0:pc.rows, g % SPLIT, 0:n].bitcast(F32), ALU.subtract).then_inc(S("lo_done"), 1)

            rest_n = [0]

            def rest_all(name, k=2):
                while rest_n[0] < where[name] + k:
                    rest(rest_n[0], pieces[rest_n[0]])
                    rest_n[0] += 1

            nxt = [0]

            def transposed():
                for q in range(4):
                    nxt[0] += 1
                    dve.wait_ge(S("xT_hi"), nxt[0])
                    t, half = q // 2, q % 2
                    sl = slice(4 * half, 4 * half + 4)
                    V.tensor_tensor(xl[:, sl, t * P:(t + 1) * P], ps[:, 4 + q, :].rearrange("p (k t) -> p k t", k=4),
                                    xh[:, sl, t * P:(t + 1) * P].bitcast(F32), ALU.subtract).then_inc(S("xT_lo"), 1)

            def col(v, n):
                return v.rearrange("p (a b) -> p a b", b=1).broadcast_to([P, v.shape[1], n])

            def each(v, a):
                return v.rearrange("p (a n) -> p a n", a=1).broadcast_to([P, a, v.shape[1]])

            def linear(layer):
                dve.wait_ge(S("mask_ready"), 1)
                dve.wait_ge(S("gT_out"), 2 * layer + 2)
                for dt in range(2):
                    dve.wait_ge(S("decay_out"), 8 * layer + 4 * dt + 4)
                    for level in range(8):
                        half = 1 << level
                        z = E[:, 8 * dt + level, :].rearrange("p (b s h) -> p b s h", s=2, h=half)
                        for side, i in ((1, 0), (0, 1)):
                            v = gT[:, 2 * i + dt, :].rearrange("p (b s h) -> p b s h", s=2, h=half)
                            ins = V.tensor_tensor(z[:, :, side, :], z[:, :, side, :], v[:, :, side, :], ALU.mult)
                        inc(ins, "Z_done")
                n = 0
                for t in range(NT):
                    for plane in range(8):
                        dve.wait_ge(S("plane_psum"), 16 * layer + n + 1)
                        b = 4 + 2 * (n % 2)
                        src = ps[:, b:b + 2, 0:SEQ].rearrange("p b (d t) -> p b d t", d=2)
                        dst = score[layer][:, t, :].rearrange("p (b d t) -> p b d t", b=2, d=2)
                        if plane == 0:
                            m = ident.rearrange("p (a b t) -> p a b t", a=1, b=1).broadcast_to([P, 2, 2, P])
                            fin(V.tensor_tensor(dst, src, m, ALU.mult), "plane_done")
                        else:
                            m = mask_sb[:, plane - 1, :].rearrange("p (a b t) -> p a b t", a=1, b=1)
                            fin(V.copy_predicated(dst, m.broadcast_to([P, 2, 2, P]), src), "plane_done")
                        n += 1

            norm_n = [0]

            def head_norm(layer, k, src, gate, o0):
                dve.wait_ge(S("normw_loaded"), 16 * (k + 1))
                for t in range(NT):
                    dve.wait_ge(S("squares"), 2 * k + t + 1)
                    V.tensor_reduce(st[:, 64 + 4 * t:68 + 4 * t],
                                    tmp[layer][t].rearrange("p (h n) -> p h n", h=LH), AX_X,
                                    ALU.add).then_inc(S("sumsq"), 1)
                for t in range(NT):
                    dve.wait_ge(S("head_rstd"), 2 * k + t + 1)
                    v = tmp[layer][t]
                    fin(V.tensor_tensor(v.rearrange("p (h n) -> p h n", h=LH), src(t).rearrange("p (h n) -> p h n", h=LH),
                                        col(st[:, 64 + 4 * t:68 + 4 * t], LV), ALU.mult))
                    fin(V.tensor_tensor(v, v, normw, ALU.mult))
                    inc(V.tensor_tensor(O[:, t, o0:o0 + NC], v, gate[:, t, :], ALU.mult), "mix_out")
                dve.wait_ge(S("mix_out"), count["mix_out"])

            ln_n = [0]

            def layer_norm(src, ready):
                n = ln_n[0]
                ln_n[0] += 1
                stats = st[:, 96:120].rearrange("p (t n s) -> p t n s", t=NT, n=2)

                def add(t, nn):
                    sl = slice(nn * NC, (nn + 1) * NC)
                    ready(nn, t)
                    inc(V.scalar_tensor_tensor(out=O[:, t, sl], in0=X[:, t, sl], scalar=ALPHA, in1=src(t, nn),
                                               op0=ALU.mult, op1=ALU.add), "dve_step")

                def stat(t, nn):
                    inc(V.bn_stats(stats[:, t, nn, :], O[:, t, nn * NC:(nn + 1) * NC]), "dve_step")

                def step():
                    dve.wait_ge(S("dve_step"), count["dve_step"])

                add(0, 0)
                add(1, 0)
                step()
                stat(0, 0)
                stat(1, 0)
                for t in range(NT):
                    add(t, 1)
                    step()
                    stat(t, 1)
                    step()
                    inc(V.bn_aggr(st[:, 80 + 2 * t:82 + 2 * t], stats[:, t, :, :].rearrange("p n s -> p (n s)")), "ln_var")
                dve.wait_ge(S("lnp_loaded"), 32 * (n + 1))
                for t in range(NT):
                    dve.wait_ge(S("ln_var"), 2 * n + t + 1)
                    fin(V.scalar_tensor_tensor(out=O[:, t, :], in0=O[:, t, :], scalar=st[:, 80 + 2 * t:81 + 2 * t],
                                               in1=lnp[:, 0, :], op0=ALU.subtract, op1=ALU.mult))
                    dve.wait_ge(S("ln_rstd"), 2 * n + t + 1)
                    inc(V.scalar_tensor_tensor(out=X[:, t, :], in0=O[:, t, :], scalar=st[:, 84 + t:85 + t],
                                               in1=lnp[:, 1, :], op0=ALU.mult, op1=ALU.add), "ln_x")
                dve.wait_ge(S("ln_x"), count["ln_x"])

            def ple_p(i):
                dve.wait_ge(S("pT_hi"), i + 1)
                V.tensor_tensor(al[:, 0:NC], ps[:, 4, :], ah[:, 0:NC].bitcast(F32), ALU.subtract).then_inc(S("pT_lo"), 1)

            def ple_add(i):
                for n in range(2):
                    for t in range(NT):
                        sl = slice(n * NC, (n + 1) * NC)
                        dve.wait_ge(S("p_out"), 4 * (i + 1))
                        dve.wait_ge(S("gate_out"), 4 * i + 2 * n + t + 1)
                        fin(V.tensor_tensor(O[:, t, sl], O[:, t, sl], PW[:, 2 * n + t, :], ALU.mult))
                        inc(V.tensor_tensor(X[:, t, sl], X[:, t, sl], O[:, t, sl], ALU.add), "ple_x")
                dve.wait_ge(S("ple_x"), count["ple_x"])

            V.memset(relb[32:33, :], NEG).then_inc(S("rel_neg"), 1)
            dve.wait_ge(S("row_psum"), 1)
            V.tensor_copy(row_sb[0:MH, :], ps[0:MH, 0, 0:384]).then_inc(S("row_ready"), 1)
            transposed()
            rest_all(("in", 0, 0))
            rest_all(("in", 0, 1))
            rest_all(("in", 0, 2))
            rest_all(("in", 0, 3))
            dve.wait_ge(S("bias_loaded"), 16 * MH)
            for h in range(MH):
                dve.wait_ge(S("score_psum"), h + 1)
                V.scalar_tensor_tensor(out=logits[:, h, 0:P], in0=ps[:, 4 + h % 4, 0:P], scalar=MD ** -0.5,
                                       in1=bias_t[:, h, P - 1::-1], op0=ALU.mult, op1=ALU.add)
                fin(V.scalar_tensor_tensor(out=logits[:, h, P:384], in0=ps[:, 4 + h % 4, P:384], scalar=MD ** -0.5,
                                           in1=bias_t[:, h, ::-1], op0=ALU.mult, op1=ALU.add), "logits_done")
            V.tensor_reduce(st[:, 0:8], logits[:, :, 0:P], AX_X, ALU.max)
            fin(V.tensor_reduce(st[:, 8:16], logits[:, :, P:384], AX_X, ALU.max))
            fin(V.tensor_scalar(st[:, 16:32], st[:, 0:16], -1.0, None, ALU.mult), "row_max")
            rest_all(("in", 0, 4))
            for h in range(MH):
                dve.wait_ge(S("PT_psum"), h + 1)
                if h >= 2:
                    dve.wait_ge(S("PV_used"), h - 1)
                V.tensor_copy(PT[h % 2], ps[:, 4 + h % 2, 0:384]).then_inc(S("PT_out"), 1)
            dve.wait_ge(S("exp_done"), 2 * MH)
            fin(V.reciprocal(st[:, 48:64], st[:, 32:48]))
            dve.wait_ge(S("PV_used"), MH)
            for t in range(NT):
                ins = V.tensor_tensor(O[:, t, 0:NC].rearrange("p (h n) -> p h n", h=MH),
                                      ps[:, 6 + t, :].rearrange("p (h n) -> p h n", h=MH),
                                      col(st[:, 48 + 8 * t:56 + 8 * t], MD), ALU.mult)
            ins.then_inc(S("moba_out"), 1)
            rest_all(("in", 0, 5))
            dve.wait_ge(S("ga_loaded"), 48)
            dve.wait_ge(S("z_psum"), 1)
            for t in range(NT):
                z = tmp[0][t][:, SEQ:NC]
                v = tmp[0][t][:, 0:SEQ]
                fin(V.tensor_tensor(z, ps[:, 5, t * SEQ:(t + 1) * SEQ], gla_b, ALU.add))
                inc(V.scalar_tensor_tensor(out=v, in0=z, scalar=-1.0, in1=z, op0=ALU.mult, op1=ALU.min), "gate_abs")
            for t in range(NT):
                dve.wait_ge(S("softplus"), t + 1)
                inc(V.scalar_tensor_tensor(out=la[0][:, t, :], in0=tmp[0][t][:, SEQ:NC], scalar=0.0,
                                           in1=tmp[0][t][:, 0:SEQ], op0=ALU.min, op1=ALU.subtract), "la_done")
            linear(0)
            rest_all(("out", 0, 0))
            head_norm(0, 0, lambda t: ps[:, 6 + t, :], H[5], NC)
            transposed()
            rest_all(("out", 0, 0))
            rest_all(("out", 0, 1))
            rest_all(("w1", 0))
            layer_norm(lambda t, n: ps[:, 2 * n + t, :], lambda n, t: dve.wait_ge(S("out_tile0"), 1) if (n, t) == (1, 0) else multiplied(dve, ("out", 0, n)))
            transposed()
            for c in range(CF + 1):
                if c < CF:
                    rest_all(("w1", c))
                if c > 0:
                    dve.wait_ge(S("ah_done"), c)
                    m = -(-min(NC, FFN - (c - 1) * NC) // P) * SEQ
                    V.tensor_tensor(al[:, 0:m], aT[:, 0:m], ah[:, 0:m].bitcast(F32), ALU.subtract).then_inc(S("al_done"), 1)
                if c < CF:
                    rest_all(("w3", c))
                if c > 0:
                    rest_all(("w2", c - 1))
                if c < CF:
                    m = -(-min(NC, FFN - c * NC) // P) * SEQ
                    multiplied(dve, ("w3", c))
                    dve.wait_ge(S("s_done"), c + 1)
                    if c > 0:
                        dve.wait_ge(S("al_done"), c)
                    V.tensor_tensor(aT[:, 0:m], s1T[:, 0:m], ps[:, 6:8, :].rearrange("p a n -> p (a n)")[:, 0:m],
                                    ALU.mult).then_inc(S("a_done"), 1)
            rest_all(("proj", 0), 1)
            ple_p(0)
            rest_all(("gate", 0, 0), 1)
            layer_norm(lambda t, n: ps[:, 2 * n + t, :], lambda n, t: dve.wait_ge(S("ffn_tile0"), 1) if t == 0 else multiplied(dve, ("w2", CF - 1)))
            transposed()
            rest_all(("gate", 0, 1))
            rest_all(("in", 1, 0))
            ple_add(0)
            transposed()
            dve.wait_ge(S("gamma_loaded"), 32)
            inc(V.tensor_tensor(lb, oml, lb, ALU.subtract), "gamma_diff")
            for j in range(6):
                rest_all(("in", 1, j))
                if j == 1:
                    dve.wait_ge(S("lb_done"), 1)
                    fin(V.tensor_scalar(oml, lb, -1.0, 1.0, ALU.mult, ALU.add))
            for t in range(NT):
                dve.wait_ge(S("proj_out"), 12 + t + 1)
                f = H[0][:, t, SEQ:NC]
                fin(V.tensor_tensor(f, f, oml, ALU.mult))
                fin(V.tensor_tensor(f, f, lb, ALU.add))
                V.tensor_scalar(la[1][:, t, :], f, 2.0 ** -63, None, ALU.max)
                fin(V.tensor_scalar(f, f, -1.0, 1.0, ALU.mult, ALU.add), "k_done")
            fin(V.tensor_copy(st[:, 91:92], st[:, 84:85]), "forget")
            linear(1)
            head_norm(1, 1, lambda t: ps[:, 6 + t, :], H[2], 0)
            fin(V.tensor_copy(st[:, 92:93], st[:, 84:85]), "hgrn_done")
            for t in range(NT):
                dve.wait_ge(S("proj_out"), 12 + 2 * 3 + t + 1)
                v = H[3][:, t, :].rearrange("p (h s n) -> p h s n", h=8, s=2)
                x1, x2 = v[:, :, 0, :], v[:, :, 1, :]
                cos = each(T[:, C_COS + 32 * t:C_COS + 32 * t + 32], 8)
                sin = each(T[:, C_SIN + 32 * t:C_SIN + 32 * t + 32], 8)
                r = [tmp[1][b][:, q * SEQ:(q + 1) * SEQ].rearrange("p (h n) -> p h n", h=8) for b in range(2) for q in range(2)]
                for d, a, b in ((0, x1, cos), (1, x2, sin), (2, x1, sin), (3, x2, cos)):
                    inc(V.tensor_tensor(r[d], a, b, ALU.mult), "dve_step")
                dve.wait_ge(S("dve_step"), count["dve_step"])
                inc(V.tensor_tensor(x1, r[0], r[1], ALU.subtract), "dve_step")
                inc(V.tensor_tensor(x2, r[2], r[3], ALU.add), "dve_step")
                dve.wait_ge(S("dve_step"), count["dve_step"])
                fin(V.tensor_copy(st[:, 93:94], st[:, 84:85]), "rotated")
            dve.wait_ge(S("decay_loaded"), 16)
            for h in range(LH):
                dve.wait_ge(S("ret_psum"), h + 1)
                V.tensor_tensor(ret_score[:, h, :], ps[:, 4 + h % 2, 0:384], ret_decay[:, h, :],
                                ALU.mult).then_inc(S("ret_scored"), 1)
            rest_all(("out", 1, 0))
            for t in range(NT):
                dve.wait_ge(S("ret_out"), t + 1)
                m = st[:, 72 + 4 * t:76 + 4 * t]
                src = ps[:, 6 + t, :].rearrange("p (h n) -> p h n", h=LH)
                fin(V.tensor_reduce(m, src, AX_X, ALU.add))
                fin(V.tensor_scalar(m, m, 1.0 / LV, None, ALU.mult))
                fin(V.tensor_tensor(H[3][:, t, :].rearrange("p (h n) -> p h n", h=LH), src, col(m, LV),
                                    ALU.subtract), "ret_centred")
            head_norm(1, 2, lambda t: H[3][:, t, :], H[5], NC)
            transposed()
            rest_all(("out", 1, 0))
            rest_all(("out", 1, 1))
            layer_norm(lambda t, n: ps[:, 2 * n + t, :], lambda n, t: dve.wait_ge(S("out_tile0"), 2) if (n, t) == (1, 0) else multiplied(dve, ("out", 1, n)))
            def xrest(i, idx, off=0):
                g = N1 + idx
                dve.wait_ge(S("hi_done"), i * PASS + off * 6 + (g + 1))
                V.tensor_tensor(lo[:, g % SPLIT, :], raw[:, g % RAW, :], hi[:, g % SPLIT, :].bitcast(F32),
                                ALU.subtract).then_inc(S("lo_done"), 1)

            both = range(NT)
            sel = [rt[:, 0 + t, 0:NE] for t in both]
            gate8 = [rt[:, 2 + t, 0:NE] for t in both]
            iota8 = iota[:, 0:NE]
            lg = [rt[:, 6 + 2 * t, 0:8] for t in both]
            top = [rt[:, 6 + 2 * t, 8:16] for t in both]
            idx = [rt[:, 7 + 2 * t, 0:8].bitcast(U32) for t in both]
            idf = [rt[:, 7 + 2 * t, 8:16] for t in both]
            hot1, hot2 = [rt[:, 10 + t, 0:8] for t in both], [rt[:, 10 + t, 8:16] for t in both]
            e, g1, g2 = ([rt[:, 4 + t, n:n + 1] for t in both] for n in range(3))

            def abreast(op, name="dve_step"):
                for t in both:
                    inc(op(t), name)
                dve.wait_ge(S(name), count[name])

            V.memset(O[:, :, :], 0.0)
            V.memset(posm[:, :, NE:], -1.0)
            fin(V.memset(gates[:, :, NE:], 0.0))
            xrest(0, 0)
            xrest(0, 1)
            dve.wait_ge(S("wr_loaded"), 32)
            dve.wait_ge(S("route_psum"), 1)
            abreast(lambda t: V.tensor_tensor(lg[t], ps[:, 0, 8 * t:8 * t + 8], br, ALU.add))
            abreast(lambda t: V.max(top[t], lg[t]))
            abreast(lambda t: V.max_index(idx[t], top[t], lg[t]))
            abreast(lambda t: V.tensor_copy(idf[t], idx[t]))
            for t in both:
                inc(V.tensor_scalar(hot1[t], iota8, idf[t][:, 0:1], None, ALU.is_equal), "dve_step")
            abreast(lambda t: V.tensor_scalar(hot2[t], iota8, idf[t][:, 1:2], None, ALU.is_equal))
            abreast(lambda t: V.tensor_tensor(sel[t], hot1[t], hot2[t], ALU.add), "selected")
            abreast(lambda t: V.tensor_tensor(e[t], top[t][:, 1:2], top[t][:, 0:1], ALU.subtract), "top_diff")
            dve.wait_ge(S("top_exp"), NT)
            abreast(lambda t: V.tensor_scalar(g1[t], e[t], 1.0, None, ALU.add))
            abreast(lambda t: V.reciprocal(g1[t], g1[t]))
            abreast(lambda t: V.tensor_tensor(g2[t], g1[t], e[t], ALU.mult))
            for t in both:
                inc(V.tensor_scalar(hot1[t], hot1[t], g1[t], None, ALU.mult), "dve_step")
            abreast(lambda t: V.tensor_scalar(hot2[t], hot2[t], g2[t], None, ALU.mult))
            for t in both:
                inc(V.tensor_tensor(gates[:, t, 0:NE], hot1[t], hot2[t], ALU.add), "dve_step")
            dve.wait_ge(S("rank_psum"), 1)
            inc(V.tensor_copy(count_of, ps[:, 1, 16:24]), "dve_step")
            abreast(lambda t: V.tensor_scalar(posm[:, t, 0:NE], ps[:, 1, 8 * t:8 * t + 8], 1.0, None, ALU.add))
            abreast(lambda t: V.tensor_tensor(posm[:, t, 0:NE], posm[:, t, 0:NE], sel[t], ALU.mult))
            abreast(lambda t: V.tensor_scalar(posm[:, t, 0:NE], posm[:, t, 0:NE], -1.0, None, ALU.add), "ranked")

            def expert_a(i, c, last=False):
                dve.wait_ge(S("e_s"), i * CE + c + 2)
                dve.wait_ge(S("piece_used"), i * PASS + c * 6 + (N1 + (2 if last else 4)))
                dve.wait_ge(S("e_T"), i * CE + c + 1)
                V.tensor_tensor(a1, s1, ps[:, 3, :], ALU.mult).then_inc(S("e_a"), 1)

            def expert_al(i, c):
                dve.wait_ge(S("e_ah"), i * CE + c + 1)
                V.tensor_tensor(al[:, 0:NC], ps[:, 4, :], ah[:, 0:NC].bitcast(F32), ALU.subtract).then_inc(S("e_al"), 1)

            def expert_pick(i):
                for t in range(NT):
                    V.tensor_scalar(pick[:, t, :], iota, posm[:, t, bass.ds(i, 1)], None, ALU.is_equal)
                    ins = V.tensor_scalar(pickg[:, t, :], iota, posm[:, t, bass.ds(i, 1)], gates[:, t, bass.ds(i, 1)],
                                          ALU.is_equal, ALU.mult)
                ins.then_inc(S("e_pick"), 1)

            def expert_xl(i, half):
                dve.wait_ge(S("e_xh"), i * 2 + (half + 1))
                sl = slice(4 * half, 4 * half + 4)
                V.tensor_tensor(xl[:, sl, 0:P], ps[:, 5 + half, :].rearrange("p (k t) -> p k t", k=4),
                                xh[:, sl, 0:P].bitcast(F32), ALU.subtract).then_inc(S("e_xl"), 1)

            def expert(i):
                xrest(i, 2)
                xrest(i, 3)
                with dve.Fori(1, CE) as c:
                    xrest(i, 4, c - 1)
                    xrest(i, 5, c - 1)
                    expert_a(i, c - 1)
                    xrest(i, 6, c - 1)
                    xrest(i, 7, c - 1)
                    expert_al(i, c - 1)
                    xrest(i, 8, c - 1)
                    xrest(i, 9, c - 1)
                dve.wait_ge(S("e_gather"), i * 3 + 4)
                dve.wait_ge(S("routed"), 1)
                expert_pick(i + 1)
                xrest(i, 40)
                expert_a(i, CE - 1, True)
                xrest(i, 41)
                expert_al(i, CE - 1)
                xrest(i, PASS)
                expert_xl(i + 1, 0)
                expert_xl(i + 1, 1)
                xrest(i, PASS + 1)
                for q in range(4):
                    t, n = q // 2, q % 2
                    dve.wait_ge(S("e_scatter"), i * 4 + q + 2)
                    sl = slice(n * NC, (n + 1) * NC)
                    V.tensor_tensor(O[:, t, sl], O[:, t, sl], ps[:, 5 + q % 2, :], ALU.add).then_inc(S("e_added"), 1)

            expert_pick(0)
            expert_xl(0, 0)
            expert_xl(0, 1)
            with dve.Fori(0, NE) as i:
                expert(i)
            n_extra = dve.value_load(ctrl[0:1, 0:1], min_val=0, max_val=EXTRA)
            with dve.Fori(0, EXTRA) as j:
                with dve.If(j < n_extra):
                    expert(j + NE)
            dve.wait_ge(S("e_added"), (n_extra + NE) * 4 + 1)

            def tail_rest(u):
                g = N1 + u
                dve.wait_ge(S("hi_done"), (n_extra + NE) * PASS + (g + 1))
                V.tensor_tensor(lo[:, g % SPLIT, :], raw[:, g % RAW, :], hi[:, g % SPLIT, :].bitcast(F32),
                                ALU.subtract).then_inc(S("lo_done"), 1)

            ple_p(1)
            layer_norm(lambda t, n: O[:, t, n * NC:(n + 1) * NC], lambda n, t: None)
            transposed()
            for u in range(2, 5):
                tail_rest(u)
            ple_add(1)

        @block.tensor
        def _(pe):
            count_from_one(pe, "e_gather", "e_scatter", "e_T")
            mm = nc.tensor.matmul

            def three(o, l_hi, l_lo, r_hi, r_lo, start, stop, **kw):
                mm(o, l_hi, r_hi, start=start, stop=False, **kw)
                mm(o, l_hi, r_lo, start=False, stop=False, **kw)
                return mm(o, l_lo, r_hi, start=False, stop=stop, **kw)

            nxt = [0]

            def transpose_x(src, name, base):
                for q in range(4):
                    t, half = q // 2, q % 2
                    if half == 0:
                        pe.wait_ge(S(name), base(t))
                    for k in range(4):
                        c0 = (4 * half + k) * P
                        ins = nc.tensor.transpose(ps[:, 4 + q, k * P:(k + 1) * P], src[:, t, c0:c0 + P], ident)
                    ins.then_inc(S("xT_psum"), 1)
                nxt[0] += 4

            def need_xT(h, t):
                pe.wait_ge(S("xT_lo"), nxt[0] - 3 + 2 * t + h)

            def product(g0, banks, wait_piece=None, fresh=False, early=None):
                for h in range(2):
                    g = g0 + h
                    if wait_piece is None:
                        pe.wait_ge(S("lo_done"), g + 1)
                    else:
                        wait_piece(g)
                    wh = hi[:, g % SPLIT, :].rearrange("p (k n) -> p k n", k=4)
                    wl = lo[:, g % SPLIT, :].rearrange("p (k n) -> p k n", k=4)
                    for t in range(NT):
                        if fresh:
                            need_xT(h, t)
                        for k in range(4):
                            kk = 4 * h + k
                            ins = three(ps[:, banks[t], :], xh[:, kk, t * P:(t + 1) * P], xl[:, kk, t * P:(t + 1) * P],
                                        wh[:, k, :], wl[:, k, :], kk == 0, kk == KD - 1)
                        if early is not None and h == 1 and t == 0:
                            ins.then_inc(S(early), 1)
                    ins.then_inc(S("piece_used"), 1)

            proj_n = [0]

            def project(layer, j):
                n = proj_n[0]
                proj_n[0] += 1
                if n >= 2:
                    pe.wait_ge(S("proj_out"), 2 * (n - 1))
                product(where[("in", layer, j)], [2 * (n % 2), 2 * (n % 2) + 1], fresh=(j == 0))

            def linear(layer, j):
                v = H[j + 1]
                for t in range(NT):
                    for i in range(4):
                        ins = nc.tensor.transpose(ps[:, 4 + t, i * P:(i + 1) * P], H[j][:, t, i * P:(i + 1) * P], ident)
                    ins.then_inc(S("gT_psum"), 1)
                pe.wait_ge(S("gT_out"), 2 * layer + 2)
                n = 0
                for dt in range(2):
                    for t in range(NT):
                        for half in range(2):
                            if n >= 4:
                                pe.wait_ge(S("decay_out"), 8 * layer + n - 3)
                            lhs = la[layer][:, t, dt * P:(dt + 1) * P]
                            o = ps[:, 4 + n % 4, :]
                            c0 = C_SUM + 4 * half * P
                            if half and t:
                                mm(o[:, 0:3 * P], lhs, T[:, c0:c0 + 3 * P], start=True, stop=True)
                                ins = mm(o[:, 3 * P:], lhs, T[:, c0 + 4 * P:c0 + 5 * P], start=True, stop=True)
                            else:
                                ins = mm(o, lhs, T[:, c0:c0 + 4 * P], start=True, stop=True)
                            ins.then_inc(S("sum_psum"), 1)
                            n += 1
                pe.wait_ge(S("decay_out"), 8 * layer + 8)
                n = 0
                for t in range(NT):
                    for plane in range(8):
                        if n >= 2:
                            pe.wait_ge(S("plane_done"), 16 * layer + n - 1)
                        pe.wait_ge(S("Z_done"), 16 * layer + (16 if plane else 0))
                        for h in range(LH):
                            dt, r = h // 2, 64 * (h % 2)
                            if plane == 0:
                                a, b = gT[r:r + 64, 2 + dt, t * P:(t + 1) * P], gT[r:r + 64, dt, t * P:(t + 1) * P]
                            else:
                                a = b = E[r:r + 64, 8 * dt + plane - 1, t * P:(t + 1) * P]
                            ins = mm(ps[:, 4 + 2 * (n % 2) + h % 2, dt * P:(dt + 1) * P], a, b, start=True, stop=True)
                        ins.then_inc(S("plane_psum"), 1)
                        n += 1
                pe.wait_ge(S("plane_done"), 16 * layer + 15)
                for h in range(LH):
                    dt, r = h // 2, 64 * (h % 2)
                    ins = mm(ps[:, 4 + h % 2, dt * P:(dt + 1) * P], E[r:r + 64, 8 * dt + 7, 0:P],
                             E[r:r + 64, 8 * dt + 7, P:SEQ], start=True, stop=True)
                ins.then_inc(S("join_psum"), 1)
                pe.wait_ge(S("plane_done"), 16 * layer + 16)
                pe.wait_ge(S("join_out"), layer + 1)
                sc = [score[layer][:, t, :].rearrange("p (h t) -> p h t", h=LH) for t in range(NT)]
                place = [2 * (h % 2) + h // 2 for h in range(LH)]
                for h in range(LH):
                    ins = mm(ps[:, 6, h * P:(h + 1) * P], sc[0][:, place[h], :], v[:, 0, h * P:(h + 1) * P], start=True, stop=True)
                ins.then_inc(S("lin_psum"), 1)
                for h in range(LH):
                    mm(ps[:, 7, h * P:(h + 1) * P], SC[layer][:, place[h], :], v[:, 0, h * P:(h + 1) * P], start=True, stop=False)
                    ins = mm(ps[:, 7, h * P:(h + 1) * P], sc[1][:, place[h], :], v[:, 1, h * P:(h + 1) * P], start=False, stop=True)
                ins.then_inc(S("lin_psum"), 1)

            def output(layer):
                for n in range(2):
                    product(where[("out", layer, n)], [2 * n, 2 * n + 1], fresh=(n == 0),
                            early="out_tile0" if n == 1 else None)

            def ple_p(i, wait_piece, g):
                pe.wait_ge(S("p_loaded"), 16 * (i + 1))
                for t in range(NT):
                    for k in range(2):
                        ins = nc.tensor.transpose(ps[:, 4, (2 * t + k) * P:(2 * t + k + 1) * P],
                                                  p_sb[:, t, k * P:(k + 1) * P], ident)
                ins.then_inc(S("pT_psum"), 1)
                pe.wait_ge(S("pT_lo"), i + 1)
                wait_piece(g)
                wh = hi[:, g % SPLIT, :].rearrange("p (k n) -> p k n", k=2)
                wl = lo[:, g % SPLIT, :].rearrange("p (k n) -> p k n", k=2)
                for t in range(NT):
                    for n in range(2):
                        for k in range(2):
                            sl = slice((2 * t + k) * P, (2 * t + k + 1) * P)
                            ins = three(ps[:, 4 + 2 * n + t, :], ah[:, sl], al[:, sl], wh[:, k, n * NC:(n + 1) * NC],
                                        wl[:, k, n * NC:(n + 1) * NC], k == 0, k == 1)
                ins.then_inc(S("piece_used"), 1)

            def ple(i, wait_piece, g):
                pe.wait_ge(S("p_out"), 4 * (i + 1))
                transpose_x(X, "ln_x", lambda t: 2 + 4 * i + t + 1)
                for n in range(2):
                    product(g + 2 * n, [2 * n, 2 * n + 1], wait_piece, fresh=(n == 0))

            pe.wait_ge(S("tab_loaded"), 16)
            transpose_x(X, "x_loaded", lambda t: 16)
            pe.wait_ge(S("hot_loaded"), 32)
            pe.wait_ge(S("rel_neg"), 1)
            mm(ps[0:MH, 0, 0:384], relb[:, :], hot_sb[0:33, :], start=True, stop=True).then_inc(S("row_psum"), 1)
            pe.wait_ge(S("row_ready"), 1)
            project(0, 0)
            pe.wait_ge(S("ga_loaded"), 48)
            pe.wait_ge(S("xT_full"), 4)
            for k in range(KD):
                ins = mm(ps[0:RANK, 4, 0:SEQ], wga[:, k, :], XT[:, k, :], start=(k == 0), stop=(k == KD - 1))
            ins.then_inc(S("gaT_psum"), 1)
            pe.wait_ge(S("gaT_out"), 1)
            project(0, 1)
            for i in range(2):
                pe.wait_ge(S("proj_out"), 2 * i + 2)
                for t in range(NT):
                    for g in range(4):
                        ins = nc.tensor.transpose(ps[:, 4 + 2 * i + t, g * P:(g + 1) * P],
                                                  H[i][:, t, g * P:(g + 1) * P], ident)
                    ins.then_inc(S("mT_psum"), 1)
            project(0, 2)
            pe.wait_ge(S("mT_out"), 4)
            for h in range(MH):
                g, r = h // 2, 64 * (h % 2)
                if h >= 4:
                    pe.wait_ge(S("logits_done"), h - 3)
                mm(ps[:, 4 + h % 4, 0:P], qkT[r:r + 64, 0, g, 0:P], qkT[r:r + 64, 1, g, 0:P], start=True, stop=True)
                mm(ps[:, 4 + h % 4, P:384], qkT[r:r + 64, 0, g, P:SEQ], qkT[r:r + 64, 1, g, :], start=True,
                   stop=True).then_inc(S("score_psum"), 1)
            project(0, 3)
            pe.wait_ge(S("logits_done"), MH)
            pe.wait_ge(S("proj_out"), 6)
            for h in range(MH):
                pe.wait_ge(S("exp_done"), 2 * h + 2)
                if h >= 2:
                    pe.wait_ge(S("PT_out"), h - 1)
                for b in range(3):
                    ins = nc.tensor.transpose(ps[:, 4 + h % 2, b * P:(b + 1) * P], logits[:, h, b * P:(b + 1) * P], ident)
                ins.then_inc(S("PT_psum"), 1)
                pe.wait_ge(S("PT_out"), h + 1)
                sl = slice(h * MD, (h + 1) * MD)
                mm(ps[:, 6, sl], PT[h % 2][:, 0:P], H[2][:, 0, sl], start=True, stop=True)
                mm(ps[:, 7, sl], PT[h % 2][:, P:2 * P], H[2][:, 0, sl], start=True, stop=False)
                mm(ps[:, 7, sl], PT[h % 2][:, 2 * P:384], H[2][:, 1, sl], start=False, stop=True).then_inc(S("PV_used"), 1)
            project(0, 4)
            project(0, 5)
            for t in range(NT):
                ins = mm(ps[:, 5, t * SEQ:(t + 1) * SEQ], gaT[0:RANK, t * P:(t + 1) * P], wgate[0:RANK, :],
                         start=True, stop=True)
            ins.then_inc(S("z_psum"), 1)
            pe.wait_ge(S("moba_out"), 1)
            pe.wait_ge(S("proj_out"), 12)
            pe.wait_ge(S("la_done"), 2)
            linear(0, 3)
            transpose_x(O, "mix_out", lambda t: t + 1)
            output(0)
            transpose_x(X, "ln_x", lambda t: 0 + t + 1)
            for c in range(CF + 1):
                if c < CF:
                    w = min(NC, FFN - c * NC)
                    for j, name in enumerate(("w1", "w3")):
                        if c > 0:
                            pe.wait_ge(S("s_done" if j == 0 else "a_done"), c)
                        for h in range(2):
                            g = where[(name, c)] + h
                            pe.wait_ge(S("lo_done"), g + 1)
                            if c == 0 and j == 0:
                                need_xT(h, 1)
                            for m in range(-(-w // P)):
                                o = ps[:, 4 + 2 * j + m // 2, (m % 2) * SEQ:(m % 2 + 1) * SEQ]
                                for k in range(4):
                                    kk = 4 * h + k
                                    c0 = k * w + m * P
                                    wh, wl = hi[:, g % SPLIT, c0:c0 + P], lo[:, g % SPLIT, c0:c0 + P]
                                    first = kk == 0 and m % 2 == 0
                                    ins = three(o, wh, wl, xh[:, kk, :], xl[:, kk, :], first, kk == KD - 1,
                                                skip_group_check=True)
                            ins.then_inc(S("piece_used"), 1)
                if c > 0:
                    pe.wait_ge(S("al_done"), c)
                    w = min(NC, FFN - (c - 1) * NC)
                    g0 = where[("w2", c - 1)]
                    for h in range(2):
                        g = g0 + h
                        pe.wait_ge(S("lo_done"), g + 1)
                        kn = pieces[g].k
                        rows = pieces[g].rows
                        wh = hi[0:rows, g % SPLIT, 0:kn * D].rearrange("p (k n) -> p k n", k=kn)
                        wl = lo[0:rows, g % SPLIT, 0:kn * D].rearrange("p (k n) -> p k n", k=kn)
                        last = c == CF and h == 1
                        for t in range(NT):
                            for n in range(2):
                                for k in range(kn):
                                    m = kn * h + k
                                    sl = slice(m * SEQ + t * P, m * SEQ + (t + 1) * P)
                                    ins = three(ps[:, 2 * n + t, :], ah[0:rows, sl], al[0:rows, sl],
                                                wh[:, k, n * NC:(n + 1) * NC], wl[:, k, n * NC:(n + 1) * NC],
                                                c == 1 and m == 0, last, skip_group_check=True)
                            if t == 0 and last:
                                ins.then_inc(S("ffn_tile0"), 1)
                        ins.then_inc(S("piece_used"), 1)
            split_wait = lambda g: pe.wait_ge(S("lo_done"), g + 1)
            ple_p(0, split_wait, where[("proj", 0)])
            ple(0, split_wait, where[("gate", 0, 0)])
            transpose_x(X, "ple_x", lambda t: 3 + t)
            for j in range(6):
                project(1, j)
            pe.wait_ge(S("k_done"), 2)
            pe.wait_ge(S("log_f"), 2)
            linear(1, 0)
            for t in range(NT):
                pe.wait_ge(S("rotated"), t + 1)
                for i in range(4):
                    ins = nc.tensor.transpose(ps[:, 4 + t, i * P:(i + 1) * P], H[3][:, t, i * P:(i + 1) * P], ident)
                ins.then_inc(S("rT_psum"), 1)
            pe.wait_ge(S("rT_out"), 2)
            for h in range(LH):
                dt, r = h // 2, 64 * (h % 2)
                if h >= 2:
                    pe.wait_ge(S("ret_scored"), h - 1)
                mm(ps[:, 4 + h % 2, 0:SEQ], gT[r:r + 64, 2 + dt, 0:P], gT[r:r + 64, dt, :], start=True, stop=True)
                mm(ps[:, 4 + h % 2, SEQ:384], gT[r:r + 64, 2 + dt, P:SEQ], gT[r:r + 64, dt, P:SEQ], start=True,
                   stop=True).then_inc(S("ret_psum"), 1)
            pe.wait_ge(S("ret_scored"), LH)
            for t in range(NT):
                for h in range(LH):
                    o, sl = ps[:, 6 + t, h * P:(h + 1) * P], slice(h * P, (h + 1) * P)
                    if t == 0:
                        ins = mm(o, ret_score[:, h, 0:P], H[4][:, 0, sl], start=True, stop=True)
                    else:
                        mm(o, ret_score[:, h, P:SEQ], H[4][:, 0, sl], start=True, stop=False)
                        ins = mm(o, ret_score[:, h, SEQ:384], H[4][:, 1, sl], start=False, stop=True)
                ins.then_inc(S("ret_out"), 1)
            transpose_x(O, "mix_out", lambda t: 4 + t + 1)
            output(1)
            transpose_x(X, "ln_x", lambda t: 4 + t + 1)
            nxt[0] -= 4
            pe.wait_ge(S("wr_loaded"), 32)
            pe.wait_ge(S("xT_full"), 8)
            for t in range(NT):
                for k in range(KD):
                    ins = mm(ps[:, 0, 8 * t:8 * t + 8], XR[:, k, t * P:(t + 1) * P], wr[:, k, :],
                             start=(k == 0), stop=(k == KD - 1))
            ins.then_inc(S("route_psum"), 1)
            pe.wait_ge(S("selected"), 2)
            sel = [rt[:, t, 0:NE] for t in range(NT)]
            mm(ps[:, 1, 0:8], before, sel[0], start=True, stop=True)
            mm(ps[:, 1, 8:16], ones, sel[0], start=True, stop=False)
            mm(ps[:, 1, 8:16], before, sel[1], start=False, stop=True)
            mm(ps[:, 1, 16:24], ones, sel[0], start=True, stop=False)
            mm(ps[:, 1, 16:24], ones, sel[1], start=False, stop=True).then_inc(S("rank_psum"), 1)

            def need(i, idx, off=0):
                pe.wait_ge(S("lo_done"), i * PASS + off * 6 + (N1 + idx + 1))

            def columns(i, idx, off, bank):
                for h in range(2):
                    need(i, idx + h, off)
                    s = (N1 + idx + h) % SPLIT
                    wh = hi[:, s, :].rearrange("p (k n) -> p k n", k=4)
                    wl = lo[:, s, :].rearrange("p (k n) -> p k n", k=4)
                    for k in range(4):
                        kk = 4 * h + k
                        ins = three(ps[:, bank, :], xh[:, kk, 0:P], xl[:, kk, 0:P], wh[:, k, :], wl[:, k, :],
                                    kk == 0, kk == KD - 1)
                    ins.then_inc(S("piece_used"), 1)

            def h1(i, c, idx, off=0):
                pe.wait_ge(S("e_s"), i * CE + c + 1)
                columns(i, idx, off, 2)

            def h3(i, c, idx, off=0):
                pe.wait_ge(S("e_a"), i * CE + c + 1)
                columns(i, idx, off, 3)

            def turn(i, c):
                pe.wait_ge(S("e_a"), i * CE + c + 2)
                pe.wait_ge(S("e_al"), i * CE + c + 1)
                for k in range(4):
                    ins = nc.tensor.transpose(ps[:, 4, k * P:(k + 1) * P], a1[:, k * P:(k + 1) * P], ident)
                ins.then_inc(S("e_T"), 1)

            def second(i, c, idx, off, first, last):
                pe.wait_ge(S("e_al"), i * CE + c + 2)
                for h in range(2):
                    need(i, idx + h, off)
                    s = (N1 + idx + h) % SPLIT
                    wh = hi[:, s, :].rearrange("p (k n) -> p k n", k=2)
                    wl = lo[:, s, :].rearrange("p (k n) -> p k n", k=2)
                    for n in range(2):
                        for k in range(2):
                            m = 2 * h + k
                            sl = slice(m * P, (m + 1) * P)
                            ins = three(ps[:, n, :], ah[:, sl], al[:, sl], wh[:, k, n * NC:(n + 1) * NC],
                                        wl[:, k, n * NC:(n + 1) * NC], first and m == 0, last and m == 3,
                                        skip_group_check=True)
                    ins.then_inc(S("piece_used"), 1)

            def gather(i):
                pe.wait_ge(S("e_pick"), i + 1)
                for t in range(NT):
                    ins = nc.tensor.transpose(ps[:, 7, t * P:(t + 1) * P], pickg[:, t, :], ident)
                ins.then_inc(S("e_gather"), 1)
                for half in range(2):
                    for k in range(4):
                        kk = 4 * half + k
                        for t in range(NT):
                            ins = mm(ps[:, 5 + half, k * P:(k + 1) * P], X[:, t, kk * P:(kk + 1) * P], pick[:, t, :],
                                     start=(t == 0), stop=(t == NT - 1))
                    ins.then_inc(S("e_gather"), 1)

            def expert(i):
                pe.wait_ge(S("e_xl"), i * 2 + 2)
                h1(i, 0, 0)
                h3(i, 0, 2)
                pe.wait_ge(S("e_yout"), i + 1)
                h1(i, 1, 4)
                turn(i, 0)
                h3(i, 1, 6)
                second(i, 0, 8, 0, True, False)
                with pe.Fori(2, CE) as c:
                    h1(i, c, 4, c - 1)
                    turn(i, c - 1)
                    h3(i, c, 6, c - 1)
                    second(i, c - 1, 8, c - 1, False, False)
                turn(i, CE - 1)
                pe.wait_ge(S("e_gT"), i + 2)
                pe.wait_ge(S("e_added"), i * 4 + 1)
                gather(i + 1)
                second(i, CE - 1, 40, 0, False, True)
                pe.wait_ge(S("e_xl"), i * 2 + 4)
                pe.wait_ge(S("e_yout"), i + 2)
                for q in range(4):
                    t, n = q // 2, q % 2
                    if q >= 2:
                        pe.wait_ge(S("e_added"), i * 4 + q)
                    mm(ps[:, 5 + q % 2, :], pickgT[:, t * P:(t + 1) * P], ysb[:, n * NC:(n + 1) * NC],
                       start=True, stop=True).then_inc(S("e_scatter"), 1)

            gather(0)
            with pe.Fori(0, NE) as i:
                expert(i)
            pe.wait_ge(S("routed"), 1)
            n_extra = pe.value_load(ctrl[0:1, 0:1], min_val=0, max_val=EXTRA)
            with pe.Fori(0, EXTRA) as j:
                with pe.If(j < n_extra):
                    expert(j + NE)
            pe.wait_ge(S("e_added"), (n_extra + NE) * 4 + 1)
            tail_wait = lambda g: pe.wait_ge(S("lo_done"), (n_extra + NE) * PASS + (g + 1))
            ple_p(1, tail_wait, N1)
            ple(1, tail_wait, N1 + 1)


_INS = ['x', 'p', 'rel_bias', 'even_w_in', 'gla_w_gate', 'gla_b_gate', 'gla_norm', 'even_w_out',
        'odd_w_in', 'hgrn_gamma', 'hgrn_norm', 'ret_norm', 'odd_w_out', 'ln_mix_g', 'ln_mix_b',
        'ln_ffn_g', 'ln_ffn_b', 'ffn_w1', 'ffn_w3', 'ffn_w2', 'router_w', 'router_b', 'expert_w1',
        'expert_w3', 'expert_w2', 'ple_w_gate', 'ple_w_proj']


def kernel(**inputs):
    import concourse.bacc as bacc
    from concourse.bass_utils import run_bass_kernel_spmd

    nc = bacc.Bacc("TRN2", target_bir_lowering=False, num_devices=1)
    arrays, args = {}, []
    tables = dict(zip(("tab", "masks", "decay", "hot"), constants()))
    for name in _INS + list(tables):
        a = np.ascontiguousarray(tables[name] if name in tables else inputs[name])
        arrays[f"in_{name}"] = a
        args.append(nc.dram_tensor(f"in_{name}", a.shape, mybir.dt.from_np(a.dtype), kind="ExternalInput").ap())
    out = nc.dram_tensor("out_x", (1, SEQ, D), F32, kind="ExternalOutput").ap()
    trunk(nc, *args, out)
    r = run_bass_kernel_spmd(nc, [arrays], core_ids=[0])
    return r.results[0]["out_x"]
```

```python
from contextlib import ExitStack
import math

import numpy as np

import concourse.bass as bass
from concourse import mybir

F32 = mybir.dt.float32
F32R = mybir.dt.float32r
I32 = mybir.dt.int32
U32 = mybir.dt.uint32
U8 = mybir.dt.uint8
ALU = mybir.AluOpType
ACT = mybir.ActivationFunctionType
AX_X = mybir.AxisListType.X

P = 128
SEQ = 256
NT = SEQ // P
D = 1024
KD = D // P
NC = 512
DEPTH = 2
ALPHA = (2.0 * DEPTH) ** 0.25
LN_EPS = 1e-5
HEAD_EPS = 1e-6
MH, MD = 8, 64
LH, LK, LV = 4, 64, 128
BUCKETS, MAX_DIST = 32, 128
RANK = 16
FFN = 2752
NE = 8
FE = 3584
CE = FE // NC
EXTRA = 3
PLE = 256
LEVELS = 7
RAW, SPLIT = 6, 3
PIECE = 2048
NEG = -1e30

C_ID, C_IOTA, C_BEFORE, C_ONE = 0, 128, 256, 384
C_SUM = 512
C_COS = C_SUM + 9 * P
C_SIN = C_COS + NT * 32
C_SMALL = C_SIN + NT * 32
C_ALL = C_SMALL + 4


def constants():
    c = np.zeros((P, C_ALL), np.float32)
    i = np.arange(P)
    c[:, C_ID:C_ID + P] = np.eye(P)
    c[:, C_IOTA:C_IOTA + P] = i[None, :]
    c[:, C_BEFORE:C_BEFORE + P] = i[:, None] < i[None, :]
    c[:, C_ONE:C_ONE + P] = 1.0
    masks = np.zeros((P, LEVELS, P), np.float32)
    s, t = i[:, None], i[None, :]
    for level in range(LEVELS):
        half = 1 << level
        mid = t // (2 * half) * 2 * half + half
        right = t >= mid
        c[:, C_SUM + level * P:C_SUM + (level + 1) * P] = np.where(
            right, (s >= mid) & (s <= t), (s > t) & (s < mid))
        masks[:, level, :] = (s // (2 * half) == t // (2 * half)) & (s < mid) & right
    c[:, C_SUM + 7 * P:C_SUM + 8 * P] = s > t
    c[:, C_SUM + 8 * P:C_SUM + 9 * P] = s <= t
    half_dim = 32
    inv = (10000.0 ** (-np.arange(half_dim, dtype=np.float32) / np.float32(half_dim))).astype(np.float32)
    ang = np.arange(SEQ, dtype=np.float32)[:, None] * inv[None, :]
    for tile in range(NT):
        c[:, C_COS + 32 * tile:C_COS + 32 * tile + 32] = np.cos(ang[P * tile:P * tile + P])
        c[:, C_SIN + 32 * tile:C_SIN + 32 * tile + 32] = np.sin(ang[P * tile:P * tile + P])
    c[:, C_SMALL:] = [LN_EPS, HEAD_EPS, 1.0, 0.0]
    log_g = np.log1p(-np.exp2(-5.0 - np.arange(LH)))
    rel = np.arange(SEQ)[None, :] - i[:, None]
    dm = np.where(rel[:, None, :] >= 0, np.exp(np.maximum(rel, 0)[:, None, :] * log_g[None, :, None]), 0.0)
    dm = dm * LK ** -0.5
    decay = np.concatenate([dm, dm[:, :, 0:P]], axis=2).astype(np.float32)
    dist = np.arange(-127, 256)
    n = np.maximum(dist, 0)
    nf = np.maximum(n, 1).astype(np.float32)
    large = 16 + (np.log(nf / np.float32(16)) / np.float32(math.log(MAX_DIST / 16)) * np.float32(16)).astype(np.int32)
    bucket = np.where(n < 16, n, np.minimum(large, BUCKETS - 1))
    hot = np.zeros((BUCKETS + 1, 384), np.float32)
    hot[bucket, dist + 127] = dist >= 0
    hot[BUCKETS, dist + 127] = dist < 0
    return c, masks, decay, hot


class Piece:

    def __init__(self, src, rows, k, n):
        self.src, self.rows, self.k, self.n = src, rows, k, n


def column_pieces(w, n0, width):
    v = w.rearrange("(k p) n -> p k n", p=P)
    return [Piece(v[:, 4 * h:4 * h + 4, n0:n0 + width], P, 4, width) for h in range(2)]


def row_piece(w, f0):
    v = w[f0:f0 + 2 * P, :].rearrange("(k p) n -> p k n", p=P)
    return Piece(v, P, 2, D)


def trunk(nc, x, p, rel_bias, even_w_in, gla_w_gate, gla_b_gate, gla_norm, even_w_out, odd_w_in,
          hgrn_gamma, hgrn_norm, ret_norm, odd_w_out, ln_mix_g, ln_mix_b, ln_ffn_g, ln_ffn_b,
          ffn_w1, ffn_w3, ffn_w2, router_w, router_b, expert_w1, expert_w3, expert_w2,
          ple_w_gate, ple_w_proj, tab, masks, decay, hot, out):
    even_cols = [0, 512, 1024, 1536, 2048, 2576]
    pieces = []
    where = {}

    def add(name, some):
        where[name] = len(pieces)
        pieces.extend(some)

    for j, n0 in enumerate(even_cols):
        add(("in", 0, j), column_pieces(even_w_in[0], n0, NC))
    for n in range(2):
        add(("out", 0, n), column_pieces(even_w_out[0], n * NC, NC))
    CF = -(-FFN // NC)

    def ffn_w2_pieces(c):
        if c < CF - 1:
            return [row_piece(ffn_w2[0], c * NC), row_piece(ffn_w2[0], c * NC + 2 * P)]
        rest = FFN - c * NC - P
        v = ffn_w2[0]
        return [Piece(v[c * NC:c * NC + P, :].rearrange("(k p) n -> p k n", p=P), P, 1, D),
                Piece(v[c * NC + P:FFN, :].rearrange("(k p) n -> p k n", p=rest), rest, 1, D)]

    for c in range(CF + 1):
        if c < CF:
            width = min(NC, FFN - c * NC)
            add(("w1", c), column_pieces(ffn_w1[0], c * NC, width))
            add(("w3", c), column_pieces(ffn_w3[0], c * NC, width))
        if c > 0:
            add(("w2", c - 1), ffn_w2_pieces(c - 1))

    def add_proj(i):
        add(("proj", i), [row_piece(ple_w_proj[i], 0)])

    add_proj(0)
    for n in range(2):
        add(("gate", 0, n), column_pieces(ple_w_gate[0], n * NC, NC))
    ODD_ORDER = (0, 1, 3, 4, 2, 5)
    for j in ODD_ORDER:
        add(("in", 1, j), column_pieces(odd_w_in[0], j * NC, NC))
    for n in range(2):
        add(("out", 1, n), column_pieces(odd_w_out[0], n * NC, NC))
    add_proj(1)
    N1 = len(pieces)
    PASS = 6 * CE
    tail = [pc for n in range(2) for pc in column_pieces(ple_w_gate[1], n * NC, NC)]

    with ExitStack() as ctx:
        def sb(name, shape, dt=F32):
            return ctx.enter_context(nc.sbuf_tensor(name, shape, dt))

        sems = {}

        def S(name):
            if name not in sems:
                sems[name] = ctx.enter_context(nc.semaphore(name))
            return sems[name]

        raw = sb("raw", [P, RAW, PIECE])
        hi = sb("hi", [P, SPLIT, PIECE], F32R)
        lo = sb("lo", [P, SPLIT, PIECE], F32R)
        X = sb("X", [P, NT, D])
        xh = sb("xh", [P, KD, SEQ], F32R)
        xl = sb("xl", [P, KD, SEQ], F32R)
        ah = sb("ah", [P, 1024], F32R)
        al = sb("al", [P, 1024], F32R)
        XO = sb("XO", [P, 2048])
        lnp = sb("lnp", [P, 2, D])
        T = sb("T", [P, C_ALL])
        mask_sb = sb("mask_sb", [P, LEVELS, P], U8)
        st = sb("st", [P, 256])
        ctrl = sb("ctrl", [P, 8], I32)
        W = sb("W", [P, 13824])
        bias_dram = nc.dram_tensor("bias_rows", [MH, 384], F32).ap()
        ps = ctx.enter_context(nc.psum_tensor("ps", [P, 8, NC], F32))

        O = XO[:].rearrange("p (t n) -> p t n", t=NT)
        ident = T[:, C_ID:C_ID + P]
        iota = T[:, C_IOTA:C_IOTA + P]
        before = T[:, C_BEFORE:C_BEFORE + P]
        ones = T[:, C_ONE:C_ONE + P]
        eps_ln = T[:, C_SMALL:C_SMALL + 1]
        eps_head = T[:, C_SMALL + 1:C_SMALL + 2]

        def arena(w0, *shape):
            n = int(np.prod(shape))
            v = W[:, w0:w0 + n]
            if len(shape) == 2:
                v = v.rearrange("p (a b) -> p a b", a=shape[0])
            if len(shape) == 3:
                v = v.rearrange("p (a b c) -> p a b c", a=shape[0], b=shape[1])
            return v

        H = [arena(w0, NT, NC) for w0 in (4096, 5120, 0, 1024, 2048, 3072)]
        logits = arena(4096, MH, 384)
        bias_t = arena(7168, MH, SEQ)
        qkT = arena(9216, 2, 4, SEQ)
        PT = [arena(12288 + 384 * b, 384) for b in range(2)]
        E = arena(7168, 2 * 8, SEQ)
        gT = arena(11264, 2 * 2, SEQ)
        normw = arena(13312, NC)
        gla_b = arena(13056, SEQ)
        gz = [lnp[:, 1, NC * t:NC * t + SEQ] for t in range(NT)]
        ge = [lnp[:, 1, NC * t + SEQ:NC * t + NC] for t in range(NT)]
        la = {0: gz, 1: [arena(6144 + SEQ * t, SEQ) for t in range(NT)]}
        SC = {0: arena(4608, LH, P), 1: arena(6144, LH, P)}
        tmp = {0: [arena(5120, NC), arena(5632, NC)], 1: [arena(12288, NC), arena(12800, NC)]}
        score = {0: H[3], 1: H[0]}
        lb, oml = arena(6656, SEQ), arena(6912, SEQ)
        ret_score = arena(7168, LH, 384)
        ret_decay = arena(8704, LH, 384)
        p_sb = arena(4096, NT, PLE)
        PW = arena(7168, 4, NC)
        s1T, aT = arena(0, 1024), arena(1024, 1024)

        def units_split(c):
            if c < CF - 1:
                return ah[:], al[:]
            return xh[:].rearrange("p k t -> p (k t)"), xl[:].rearrange("p k t -> p (k t)")

        XR = arena(0, KD, SEQ)
        s1, a1, ysb = arena(0, NC), arena(512, NC), arena(1024, 1024)
        pick, pickg, pickgT = arena(2048, NT, P), arena(2304, NT, P), arena(2560, SEQ)
        PASSES = NE + EXTRA + 1
        posm, gates = arena(2816, NT, PASSES), arena(2816 + NT * PASSES, NT, PASSES)
        rt = arena(5200, 16, 16)
        count_of = rt[:, 12, 0:8]
        wga = lnp[:, 0, 0:P].rearrange("p (k n) -> p k n", k=KD)
        wgate, gaT = lnp[:, 0, P:P + SEQ], lnp[:, 0, P + SEQ:P + 2 * SEQ]
        wgah, wgal = ah[:, 0:P], al[:, 0:P]
        relb = sb("relb", [33, MH])
        wr = sb("wr", [P, KD, NE])
        br = sb("br", [P, NE])
        masks_f = arena(9984, LEVELS, P)
        hot_sb = arena(9216, 384)
        row_sb = arena(9600, 384)

        PLANES = [(t, 0) for t in range(NT)] + [(t, level) for t in range(NT) for level in range(1, 8)]

        def plane_bank(n):
            return (4, 6, 0, 2)[n % 4]

        def ret_bank(h):
            return (4, 5, 2, 3)[h]

        def sum_bank(n):
            return 4 + (n + 2) % 4

        block = ctx.enter_context(nc.Block())

        def count_from_one(eng, *names):
            for name in names:
                eng.sem_inc(S(name), 1)

        def multiplied(eng, name, k=2):
            eng.wait_ge(S("piece_used"), where[name] + k)

        def landed(g):
            return 16 * (g // RAW + 1)

        @block.sync
        def _(sp):
            def load(slot, pc):
                sp.dma_start(raw[0:pc.rows, slot, 0:pc.k * pc.n].rearrange("p (k n) -> p k n", k=pc.k),
                             pc.src).then_inc(S(f"loaded{slot}"), 16)

            sp.dma_start(T[:, 0:C_SUM], tab[:, 0:C_SUM]).then_inc(S("tab_loaded"), 16)
            load(0, pieces[0])
            for t in range(NT):
                sp.dma_start(X[:, t, :], x[0, t * P:(t + 1) * P, :]).then_inc(S(f"x_loaded{t}"), 16)
            sp.dma_start(T[:, C_SMALL:], tab[:, C_SMALL:]).then_inc(S("tab_loaded"), 16)
            for g, pc in enumerate(pieces):
                if g == RAW:
                    sp.dma_start(T[:, C_SUM:C_SMALL], tab[:, C_SUM:C_SMALL]).then_inc(S("sums_loaded"), 16)
                if g >= RAW:
                    sp.wait_ge(S("lo_done"), g - RAW + 1)
                if g > 0:
                    load(g % RAW, pc)

            w1 = expert_w1[0].rearrange("e (k p) n -> p e k n", p=P)
            w3 = expert_w3[0].rearrange("e (k p) n -> p e k n", p=P)
            w2 = expert_w2[0].rearrange("e (k p) n -> p e k n", p=P)

            def expert_piece(i, e, idx, off, src):
                slot = (N1 + idx) % RAW
                sp.wait_ge(S("lo_done"), i * PASS + off + (N1 + idx - RAW + 1))
                sp.dma_start(raw[:, slot, :].rearrange("p (k n) -> p k n", k=src.shape[2]),
                             src.rearrange("p e k n -> p (e k) n")).then_inc(S(f"loaded{slot}"), 16)

            def columns(w, e, c, h):
                return w[:, bass.ds(e, 1), 4 * h:4 * h + 4, bass.ds(c * NC, NC)]

            def rows(e, c, h):
                return w2[:, bass.ds(e, 1), bass.ds(c * 4 + 2 * h, 2), :]

            def expert(i, e):
                for j, w in enumerate((w1, w3)):
                    for h in range(2):
                        expert_piece(i, e, 2 * j + h, 0, columns(w, e, 0, h))
                with sp.Fori(1, CE) as c:
                    for j, w in enumerate((w1, w3)):
                        for h in range(2):
                            expert_piece(i, e, 4 + 2 * j + h, (c - 1) * 6, columns(w, e, c, h))
                    for h in range(2):
                        expert_piece(i, e, 8 + h, (c - 1) * 6, rows(e, c - 1, h))
                for h in range(2):
                    expert_piece(i, e, 40 + h, 0, rows(e, CE - 1, h))

            with sp.Fori(0, NE) as i:
                expert(i, i)
            sp.wait_ge(S("routed"), 1)
            n_extra = sp.value_load(ctrl[0:1, 0:1], min_val=0, max_val=EXTRA)
            with sp.Fori(0, EXTRA) as j:
                with sp.If(j < n_extra):
                    e = sp.value_load(ctrl[0:1, bass.ds(j + 1, 1)], min_val=0, max_val=NE - 1)
                    expert(j + NE, e)
            for u, pc in enumerate(tail):
                slot = (N1 + u) % RAW
                sp.wait_ge(S("lo_done"), (n_extra + NE) * PASS + (N1 + u - RAW + 1))
                load(slot, pc)
            for n in range(2):
                for t in range(NT):
                    sp.wait_ge(S("ple_x"), 4 + 2 * n + t + 1)
                    sp.dma_start(out[0, t * P:(t + 1) * P, n * NC:(n + 1) * NC],
                                 X[:, t, n * NC:(n + 1) * NC]).then_inc(S("stored"), 16)
            sp.wait_ge(S("stored"), 64)

        assert PASS % RAW == 0 and PASS % SPLIT == 0

        @block.gpsimd
        def _(pool):
            def small(dst, src, name):
                pool.dma_start(dst, src).then_inc(S(name), 16)

            def on_all(v, n):
                return v.rearrange("(a n) -> a n", a=1).partition_broadcast(P).rearrange("p a n -> p (a n)")

            small(wga, even_w_in[0].rearrange("(k p) n -> p k n", p=P)[:, :, 2560:2560 + RANK], "wga_loaded")
            small(wgate[0:RANK, :], gla_w_gate[0], "ga_loaded")
            small(masks_f, masks, "mask_loaded")
            pool.wait_ge(S("mask_loaded"), 16)
            nc.gpsimd.tensor_copy(mask_sb[:], masks_f).then_inc(S("mask_ready"), 1)
            small(gla_b, on_all(gla_b_gate[0], SEQ), "ga_loaded")
            small(normw, on_all(gla_norm[0], NC), "normw_loaded")
            small(wr[:], router_w[0].rearrange("(k p) n -> p k n", p=P), "wr_loaded")
            small(br[:], on_all(router_b[0], NE), "wr_loaded")
            pool.wait_ge(S("row_ready"), 1)
            small(bias_dram, row_sb[0:MH, :], "row_stored")
            pool.wait_ge(S("row_stored"), 16)
            for q in range(MH):
                toeplitz = bass.AP(bias_dram.tensor, q * 384, [[1, P], [1, SEQ]])
                small(bias_t[:, q, :], toeplitz, "bias_loaded")
            pool.wait_ge(S("sum_psum"), 8)
            small(lnp[:, 0, :], on_all(ln_mix_g[0], D), "lnp_loaded")
            small(lnp[:, 1, :], on_all(ln_mix_b[0], D), "lnp_loaded")
            pool.wait_ge(S("ln_x"), 2)
            small(lnp[:, 0, :], on_all(ln_ffn_g[0], D), "lnp_loaded")
            small(lnp[:, 1, :], on_all(ln_ffn_b[0], D), "lnp_loaded")
            small(p_sb[:], p[0, 0].rearrange("(t p) n -> p t n", p=P), "p_loaded")
            small(normw, on_all(hgrn_norm[0], NC), "normw_loaded")
            small(lb, on_all(hgrn_gamma[0], SEQ), "gamma_loaded")
            small(oml, on_all(hgrn_gamma[1], SEQ), "gamma_loaded")
            pool.wait_ge(S("ln_x"), 4)
            small(lnp[:, 0, :], on_all(ln_mix_g[1], D), "lnp_loaded")
            small(lnp[:, 1, :], on_all(ln_mix_b[1], D), "lnp_loaded")
            pool.wait_ge(S("join_psum"), 2)
            small(ret_decay[:], decay, "decay_loaded")
            pool.wait_ge(S("lin_psum"), 4)
            small(p_sb[:], p[1, 0].rearrange("(t p) n -> p t n", p=P), "p_loaded")
            pool.wait_ge(S("hgrn_normed"), 2)
            small(normw, on_all(ret_norm[0], NC), "normw_loaded")
            pool.wait_ge(S("ln_x"), 6)
            small(lnp[:, 0, :], on_all(ln_ffn_g[1], D), "lnp_loaded")
            small(lnp[:, 1, :], on_all(ln_ffn_b[1], D), "lnp_loaded")
            G = nc.gpsimd
            steps = [0]

            def fin(ins):
                steps[0] += 1
                ins.then_inc(S("pool_step"), 1)
                pool.wait_ge(S("pool_step"), steps[0])

            def total(dst, v):
                fin(G.tensor_tensor(v[:, 0:4], v[:, 0:4], v[:, 4:8], ALU.add))
                fin(G.tensor_tensor(v[:, 0:2], v[:, 0:2], v[:, 2:4], ALU.add))
                fin(G.tensor_tensor(dst, v[:, 0:1], v[:, 1:2], ALU.add))

            pool.wait_ge(S("ranked"), NT)
            pool.wait_ge(S("e_pick"), 1)
            over, upto, rank, pick1 = rt[:, 13, 0:8], rt[:, 13, 8:16], rt[:, 14, 0:8], rt[:, 14, 8:16]
            part, listf = rt[:, 15, 0:8], rt[:, 12, 8:16]
            fin(G.tensor_scalar(over, count_of, float(P) + 0.5, None, ALU.is_gt))
            fin(G.tensor_copy(upto, over))
            for e in range(1, NE):
                fin(G.tensor_tensor(upto[:, e:e + 1], upto[:, e - 1:e], over[:, e:e + 1], ALU.add))
            fin(G.tensor_tensor(rank, upto, over, ALU.subtract))
            fin(G.memset(listf, 0.0))
            fin(G.tensor_copy(listf[:, 0:1], upto[:, 7:8]))
            for j in range(EXTRA):
                fin(G.tensor_scalar(pick1, rank, float(j), None, ALU.is_equal))
                fin(G.tensor_tensor(pick1, pick1, over, ALU.mult))
                fin(G.tensor_tensor(part, pick1, iota[:, 0:NE], ALU.mult))
                total(listf[:, j + 1:j + 2], part)
                for t in range(NT):
                    fin(G.tensor_scalar(part, posm[:, t, 0:NE], -float(P), None, ALU.add))
                    fin(G.tensor_tensor(part, part, pick1, ALU.mult))
                    total(posm[:, t, NE + j:NE + j + 1], part)
                    fin(G.tensor_tensor(part, gates[:, t, 0:NE], pick1, ALU.mult))
                    total(gates[:, t, NE + j:NE + j + 1], part)
            G.tensor_copy(ctrl[:, 0:8], listf).then_inc(S("routed"), 1)

        @block.scalar
        def _(act):
            act.dma_start(relb[0:32, :], rel_bias).then_inc(S("hot_loaded"), 16)
            act.dma_start(hot_sb[0:33, :], hot).then_inc(S("hot_loaded"), 16)
            count_from_one(act, "e_gT", "e_yout", "e_s")
            count = {}

            def inc(ins, name):
                count[name] = count.get(name, 0) + 1
                ins.then_inc(S(name), 1)

            def fin(ins, name="act_step"):
                inc(ins, name)
                act.wait_ge(S(name), count[name])

            def copy(o, i, scale=1.0):
                return nc.scalar.activation(o, i, ACT.Copy, scale=scale)

            def split(g, pc):
                act.wait_ge(S(f"loaded{g % RAW}"), landed(g))
                if g >= SPLIT:
                    act.wait_ge(S("piece_used"), g - SPLIT + 1)
                n = pc.k * pc.n
                copy(hi[0:pc.rows, g % SPLIT, 0:n], raw[0:pc.rows, g % RAW, 0:n]).then_inc(S("hi_done"), 1)

            split_n = [0]

            def split_all(name, k=2):
                while split_n[0] < where[name] + k:
                    split(split_n[0], pieces[split_n[0]])
                    split_n[0] += 1

            nxt = [0]

            def transposed():
                for q in range(4):
                    act.wait_ge(S("xT_psum"), nxt[0] + 1)
                    nxt[0] += 1
                    t, half = q // 2, q % 2
                    src = ps[:, 4 + q, :].rearrange("p (k t) -> p k t", k=4)
                    copy(xh[:, 4 * half:4 * half + 4, t * P:(t + 1) * P], src).then_inc(S("xT_hi"), 1)

            proj_n = [0]

            def projected(layer, j, how):
                n = proj_n[0]
                proj_n[0] += 1
                multiplied(act, ("in", layer, j))
                for t in range(NT):
                    src = ps[:, 2 * (n % 2) + t, :]
                    if how == "forget":
                        copy(H[j][:, t, 0:SEQ], src[:, 0:SEQ])
                        ins = nc.scalar.activation(H[j][:, t, SEQ:NC], src[:, SEQ:NC], ACT.Sigmoid)
                    elif how == "silu":
                        ins = nc.scalar.activation(H[j][:, t, :], src, ACT.Silu)
                    else:
                        ins = copy(H[j][:, t, :], src)
                    ins.then_inc(S("proj_out"), 1)

            def decays(layer):
                for t in range(NT):
                    act.wait_ge(S("gT_psum"), 2 * layer + t + 1)
                    src = ps[:, 4 + t, :].rearrange("p (i t) -> p i t", i=4)
                    copy(gT[:, 0:2, t * P:(t + 1) * P], src[:, 0:2, :], scale=LK ** -0.5 if layer == 0 else 1.0)
                    copy(gT[:, 2:4, t * P:(t + 1) * P], src[:, 2:4, :]).then_inc(S("gT_out"), 1)
                n = 0
                for dt in range(2):
                    for t in range(NT):
                        for half in range(2):
                            act.wait_ge(S("sum_psum"), 8 * layer + n + 1)
                            nc.scalar.activation(
                                E[:, 8 * dt + 4 * half:8 * dt + 4 * half + 4, t * P:(t + 1) * P],
                                ps[:, sum_bank(n), :].rearrange("p (l t) -> p l t", l=4), ACT.Exp,
                                scale=1.0 / 16 if layer == 0 else 1.0).then_inc(S("decay_out"), 1)
                            n += 1

            def join_out(layer):
                act.wait_ge(S("join_psum"), layer + 1)
                copy(SC[layer].rearrange("p (b d) t -> p b (d t)", b=2), ps[:, 4:6, 0:SEQ]).then_inc(S("join_out"), 1)

            norm_n = [0]

            def head_norm():
                for t in range(NT):
                    n = norm_n[0]
                    norm_n[0] += 1
                    act.wait_ge(S("sumsq"), n + 1)
                    v = st[:, 64 + 4 * t:68 + 4 * t]
                    nc.scalar.activation(v, v, ACT.Sqrt, bias=eps_head, scale=1.0 / LV).then_inc(S("head_rms"), 1)

            ln_n = [0]

            def layer_norm(between=None):
                n = ln_n[0]
                ln_n[0] += 1
                for t in range(NT):
                    if t == 1 and between is not None:
                        between()
                    act.wait_ge(S("ln_var"), 2 * n + t + 1)
                    nc.scalar.activation(st[:, 84 + t:85 + t], st[:, 81 + 2 * t:82 + 2 * t], ACT.Sqrt,
                                         bias=eps_ln).then_inc(S("ln_std"), 1)

            def ple_p(i):
                act.wait_ge(S("pT_psum"), i + 1)
                copy(ah[:, 0:NC], ps[:, 4, :]).then_inc(S("pT_hi"), 1)

            def ple_out(i, used):
                used()
                for b in range(4):
                    copy(PW[:, b, :], ps[:, 4 + b, :]).then_inc(S("p_out"), 1)

            def ple_gate(i, n, used):
                act.wait_ge(S("gate_tile0"), 2 * i + n + 1)
                for t in range(NT):
                    if t == 1:
                        used()
                    nc.scalar.activation(O[:, t, n * NC:(n + 1) * NC], ps[:, 2 * n + t, :],
                                         ACT.Sigmoid).then_inc(S("gate_out"), 1)

            split_all(("in", 0, 0), 1)
            transposed()
            split_all(("in", 0, 0))
            act.wait_ge(S("wga_loaded"), 16)
            copy(wgah, wga.rearrange("p k n -> p (k n)")).then_inc(S("wga_hi"), 1)
            split_all(("in", 0, 1))
            projected(0, 0, "copy")
            act.wait_ge(S("gaT_psum"), 1)
            copy(gaT[0:RANK, :], ps[0:RANK, 4, 0:SEQ]).then_inc(S("gaT_out"), 1)
            split_all(("in", 0, 2))
            projected(0, 1, "copy")
            act.wait_ge(S("row_stored"), 16)
            act.wait_ge(S("mask_ready"), 1)
            for i in range(2):
                for t in range(NT):
                    act.wait_ge(S("mT_psum"), 2 * i + t + 1)
                    copy(qkT[:, i, :, t * P:(t + 1) * P],
                         ps[:, 4 + 2 * i + t, :].rearrange("p (g t) -> p g t", g=4)).then_inc(S("mT_out"), 1)
            split_all(("in", 0, 3))
            for t in range(NT):
                act.wait_ge(S("gate_abs"), t + 1)
                inc(nc.scalar.activation(ge[t], ge[t], ACT.Exp), "act_step")
            act.wait_ge(S("act_step"), count["act_step"])
            for t in range(NT):
                nc.scalar.activation(ge[t], ge[t], ACT.Ln, bias=1.0).then_inc(S("softplus"), 1)
            projected(0, 2, "copy")
            split_all(("in", 0, 4))
            act.wait_ge(S("row_max"), 1)
            for h in range(MH):
                for t in range(NT):
                    sl = logits[:, h, 0:P] if t == 0 else logits[:, h, P:384]
                    nc.scalar.activation(sl, sl, ACT.Exp, bias=st[:, 16 + t * 8 + h:17 + t * 8 + h],
                                         accum_out=st[:, 32 + t * 8 + h:33 + t * 8 + h]).then_inc(S("exp_done"), 1)
            projected(0, 3, "copy")
            split_all(("in", 0, 5), 1)
            decays(0)
            split_all(("in", 0, 5))
            projected(0, 4, "copy")
            split_all(("out", 0, 0), 1)
            join_out(0)

            def squares(banks, k):
                for t in range(NT):
                    act.wait_ge(S("lin_psum"), 2 * k + t + 1)
                    nc.scalar.activation(tmp[0 if k == 0 else 1][t], ps[:, banks + t, :],
                                         ACT.Square).then_inc(S("squares"), 1)
            squares(6, 0)
            head_norm()
            split_all(("out", 0, 0))
            projected(0, 5, "silu")
            transposed()
            split_all(("out", 0, 1))
            split_all(("w1", 0))
            layer_norm()
            transposed()
            def units(c):
                return -(-min(NC, FFN - c * NC) // P) * SEQ

            for c in range(CF + 1):
                if c < CF:
                    split_all(("w1", c))
                if c > 0:
                    act.wait_ge(S("a_done"), c)
                    if 1 < c < CF:
                        multiplied(act, ("w2", c - 2))
                    copy(units_split(c - 1)[0][:, 0:units(c - 1)], aT[:, 0:units(c - 1)]).then_inc(S("ah_done"), 1)
                if c < CF:
                    split_all(("w3", c))
                    multiplied(act, ("w1", c))
                    if c > 0:
                        act.wait_ge(S("a_done"), c)
                    for b in range(0, units(c), NC):
                        ins = nc.scalar.activation(s1T[:, b:b + NC], ps[:, 4 + b // NC, :], ACT.Silu)
                    ins.then_inc(S("s_done"), 1)
                if c > 0:
                    split_all(("w2", c - 1))
            ple_p(0)
            split_all(("proj", 0), 1)
            split_all(("gate", 0, 0), 1)
            layer_norm(lambda: ple_out(0, lambda: multiplied(act, ("proj", 0), 1)))
            split_all(("gate", 0, 0))
            transposed()
            split_all(("gate", 0, 1))
            ple_gate(0, 0, lambda: multiplied(act, ("gate", 0, 0)))
            split_all(("in", 1, 0))
            ple_gate(0, 1, lambda: multiplied(act, ("gate", 0, 1)))
            transposed()
            act.wait_ge(S("gamma_diff"), 1)
            nc.scalar.activation(lb, lb, ACT.Sigmoid).then_inc(S("lb_done"), 1)
            split_all(("in", 1, 0))
            split_all(("in", 1, 1))
            projected(1, 0, "forget")
            split_all(("in", 1, 3))
            projected(1, 1, "copy")
            act.wait_ge(S("forget"), 2)
            for t in range(NT):
                nc.scalar.activation(la[1][t], la[1][t], ACT.Ln).then_inc(S("log_f"), 1)
            split_all(("in", 1, 4))
            projected(1, 3, "copy")
            decays(1)
            split_all(("in", 1, 2))
            projected(1, 4, "copy")
            join_out(1)
            for t in range(NT):
                act.wait_ge(S("rT_psum"), t + 1)
                copy(gT[:, :, t * P:(t + 1) * P],
                     ps[:, 2 + t, :].rearrange("p (i t) -> p i t", i=4)).then_inc(S("rT_out"), 1)
            squares(6, 1)
            head_norm()
            split_all(("in", 1, 5), 1)
            projected(1, 2, "silu")
            split_all(("in", 1, 5))
            split_all(("out", 1, 0), 1)
            for t in range(NT):
                act.wait_ge(S("ret_centred"), t + 1)
                nc.scalar.activation(tmp[1][t], H[3][:, t, :], ACT.Square).then_inc(S("squares"), 1)
            head_norm()
            projected(1, 5, "silu")
            split_all(("out", 1, 0))
            transposed()
            split_all(("out", 1, 1))
            ple_p(1)
            split_all(("proj", 1), 1)
            layer_norm(lambda: ple_out(1, lambda: multiplied(act, ("proj", 1), 1)))
            def xsplit(i, idx, off=0):
                g = N1 + idx
                act.wait_ge(S(f"loaded{g % RAW}"), i * (16 * PASS // RAW) + off * 16 + landed(g))
                act.wait_ge(S("piece_used"), i * PASS + off * 6 + (g - SPLIT + 1))
                copy(hi[:, g % SPLIT, :], raw[:, g % RAW, :]).then_inc(S("hi_done"), 1)

            for t in range(NT):
                for half in range(2):
                    nxt[0] += 1
                    act.wait_ge(S("xT_psum"), nxt[0])
                    copy(XR[:, 4 * half:4 * half + 4, t * P:(t + 1) * P],
                         ps[:, 4 + 2 * t + half, :].rearrange("p (k t) -> p k t", k=4)).then_inc(S("xT_full"), 1)
                xsplit(0, t)

            def expert_silu(i, c):
                act.wait_ge(S("piece_used"), i * PASS + (c * 6 + N1 if not (isinstance(c, int) and c == 0) else N1 + 2))
                act.wait_ge(S("e_a"), i * CE + c + 1)
                nc.scalar.activation(s1, ps[:, 2, :], ACT.Silu).then_inc(S("e_s"), 1)

            def expert_xh(i, half):
                act.wait_ge(S("e_gather"), i * 3 + (3 + half))
                copy(xh[:, 4 * half:4 * half + 4, 0:P],
                     ps[:, 5 + half, :].rearrange("p (k t) -> p k t", k=4)).then_inc(S("e_xh"), 1)

            def expert_ah(i, c):
                act.wait_ge(S("e_T"), i * CE + c + 2)
                copy(ah[:, 0:NC], ps[:, 4, :]).then_inc(S("e_ah"), 1)

            def expert(i):
                xsplit(i, 2)
                act.wait_ge(S("e_gather"), i * 3 + 2)
                act.wait_ge(S("e_scatter"), i * 4 + 1)
                copy(pickgT, ps[:, 7, 0:SEQ]).then_inc(S("e_gT"), 1)
                xsplit(i, 3)
                expert_silu(i, 0)
                with act.Fori(1, CE) as c:
                    for j in range(4):
                        xsplit(i, 4 + j, c - 1)
                    expert_ah(i, c - 1)
                    expert_silu(i, c)
                    for j in range(2):
                        xsplit(i, 8 + j, c - 1)
                xsplit(i, 40)
                xsplit(i, 41)
                expert_ah(i, CE - 1)
                xsplit(i, PASS)
                expert_xh(i + 1, 0)
                expert_xh(i + 1, 1)
                xsplit(i, PASS + 1)
                act.wait_ge(S("piece_used"), i * PASS + (N1 + PASS))
                copy(ysb, ps[:, 0:2, :].rearrange("p a n -> p (a n)")).then_inc(S("e_yout"), 1)

            for t in range(NT):
                act.wait_ge(S("top_diff"), t + 1)
                nc.scalar.activation(rt[:, 4 + t, 0:1], rt[:, 4 + t, 0:1], ACT.Exp).then_inc(S("top_exp"), 1)
            expert_xh(0, 0)
            expert_xh(0, 1)
            with act.Fori(0, NE) as i:
                expert(i)
            act.wait_ge(S("routed"), 1)
            n_extra = act.value_load(ctrl[0:1, 0:1], min_val=0, max_val=EXTRA)
            with act.Fori(0, EXTRA) as j:
                with act.If(j < n_extra):
                    expert(j + NE)

            def tail_split(u):
                g = N1 + u
                act.wait_ge(S(f"loaded{g % RAW}"), (n_extra + NE) * (16 * PASS // RAW) + landed(g))
                act.wait_ge(S("piece_used"), (n_extra + NE) * PASS + (g - SPLIT + 1))
                copy(hi[:, g % SPLIT, :], raw[:, g % RAW, :]).then_inc(S("hi_done"), 1)

            def tail_used(u):
                return lambda: act.wait_ge(S("piece_used"), (n_extra + NE) * PASS + (N1 + u))

            layer_norm()
            tail_split(2)
            transposed()
            tail_split(3)
            ple_gate(1, 0, tail_used(2))
            ple_gate(1, 1, tail_used(4))

        @block.vector
        def _(dve):
            count_from_one(dve, "e_added", "e_a", "e_al")
            count = {}
            V = nc.vector

            def inc(ins, name):
                count[name] = count.get(name, 0) + 1
                ins.then_inc(S(name), 1)

            def fin(ins, name="dve_step"):
                inc(ins, name)
                dve.wait_ge(S(name), count[name])

            def rest(g, pc):
                n = pc.k * pc.n
                dve.wait_ge(S("hi_done"), g + 1)
                V.tensor_tensor(lo[0:pc.rows, g % SPLIT, 0:n], raw[0:pc.rows, g % RAW, 0:n],
                                hi[0:pc.rows, g % SPLIT, 0:n].bitcast(F32), ALU.subtract).then_inc(S("lo_done"), 1)

            rest_n = [0]

            def rest_all(name, k=2):
                while rest_n[0] < where[name] + k:
                    rest(rest_n[0], pieces[rest_n[0]])
                    rest_n[0] += 1

            nxt = [0]

            def transposed(between=None):
                for q in range(4):
                    if q == 2 and between is not None:
                        between()
                    nxt[0] += 1
                    dve.wait_ge(S("xT_hi"), nxt[0])
                    t, half = q // 2, q % 2
                    sl = slice(4 * half, 4 * half + 4)
                    V.tensor_tensor(xl[:, sl, t * P:(t + 1) * P], ps[:, 4 + q, :].rearrange("p (k t) -> p k t", k=4),
                                    xh[:, sl, t * P:(t + 1) * P].bitcast(F32), ALU.subtract).then_inc(S("xT_lo"), 1)

            def col(v, n):
                return v.rearrange("p (a b) -> p a b", b=1).broadcast_to([P, v.shape[1], n])

            def each(v, a):
                return v.rearrange("p (a n) -> p a n", a=1).broadcast_to([P, a, v.shape[1]])

            def linear(layer):
                dve.wait_ge(S("mask_ready"), 1)
                dve.wait_ge(S("gT_out"), 2 * layer + 2)
                def plane_out(n):
                    t, plane = PLANES[n]
                    dve.wait_ge(S("plane_psum"), 16 * layer + n + 1)
                    src = ps[:, plane_bank(n):plane_bank(n) + 2, 0:SEQ].rearrange("p b (d t) -> p b d t", d=2)
                    dst = score[layer][:, t, :].rearrange("p (b d t) -> p b d t", b=2, d=2)
                    if plane == 0:
                        m = ident.rearrange("p (a b t) -> p a b t", a=1, b=1).broadcast_to([P, 2, 2, P])
                        fin(V.tensor_tensor(dst, src, m, ALU.mult), "plane_done")
                    else:
                        m = mask_sb[:, plane - 1, :].rearrange("p (a b t) -> p a b t", a=1, b=1)
                        fin(V.copy_predicated(dst, m.broadcast_to([P, 2, 2, P]), src), "plane_done")

                for dt in range(2):
                    dve.wait_ge(S("decay_out"), 8 * layer + 4 * dt + 4)
                    for level in range(8):
                        half = 1 << level
                        z = E[:, 8 * dt + level, :].rearrange("p (b s h) -> p b s h", s=2, h=half)
                        for side, i in ((1, 0), (0, 1)):
                            v = gT[:, 2 * i + dt, :].rearrange("p (b s h) -> p b s h", s=2, h=half)
                            ins = V.tensor_tensor(z[:, :, side, :], z[:, :, side, :], v[:, :, side, :], ALU.mult)
                        inc(ins, "Z_done")
                for n in range(len(PLANES)):
                    plane_out(n)

            norm_n = [0]

            def head_norm(layer, k, src, name):
                for t in range(NT):
                    dve.wait_ge(S("squares"), 2 * k + t + 1)
                    V.tensor_reduce(st[:, 64 + 4 * t:68 + 4 * t],
                                    tmp[layer][t].rearrange("p (h n) -> p h n", h=LH), AX_X,
                                    ALU.add).then_inc(S("sumsq"), 1)
                dve.wait_ge(S("normw_loaded"), 16 * (k + 1))
                for t in range(NT):
                    dve.wait_ge(S("head_rms"), 2 * k + t + 1)
                    g = st[:, 64 + 4 * t:68 + 4 * t]
                    v = tmp[layer][t]
                    fin(V.reciprocal(g, g))
                    fin(V.tensor_tensor(v.rearrange("p (h n) -> p h n", h=LH), src(t).rearrange("p (h n) -> p h n", h=LH),
                                        col(g, LV), ALU.mult))
                    inc(V.tensor_tensor(v, v, normw, ALU.mult), name)
                dve.wait_ge(S(name), count[name])

            def gated(layer, gate, o0, number):
                for t in range(NT):
                    dve.wait_ge(S("proj_out"), 2 * number + t + 1)
                    inc(V.tensor_tensor(O[:, t, o0:o0 + NC], tmp[layer][t], gate[:, t, :], ALU.mult), "mix_out")
                dve.wait_ge(S("mix_out"), count["mix_out"])

            ln_n = [0]

            def layer_norm(src, ready, summed=False, between=None):
                n = ln_n[0]
                ln_n[0] += 1
                stats = st[:, 96:120].rearrange("p (t n s) -> p t n s", t=NT, n=2)

                def add(t, nn):
                    sl = slice(nn * NC, (nn + 1) * NC)
                    ready(nn, t)
                    inc(V.scalar_tensor_tensor(out=O[:, t, sl], in0=X[:, t, sl], scalar=ALPHA, in1=src(t, nn),
                                               op0=ALU.mult, op1=ALU.add), "dve_step")

                def stat(t, nn):
                    inc(V.bn_stats(stats[:, t, nn, :], O[:, t, nn * NC:(nn + 1) * NC]), "dve_step")

                def step():
                    dve.wait_ge(S("dve_step"), count["dve_step"])

                if between is not None:
                    for t in range(NT):
                        add(t, 0)
                    step()
                    for t in range(NT):
                        stat(t, 0)
                    between()
                for t in range(NT):
                    if not summed:
                        for nn in range(2 if between is None else 1):
                            add(t, 1 - nn)
                        step()
                    if between is None:
                        stat(t, 0)
                    stat(t, 1)
                    step()
                    fin(V.bn_aggr(st[:, 80 + 2 * t:82 + 2 * t], stats[:, t, :, :].rearrange("p n s -> p (n s)")), "ln_var")
                    dve.wait_ge(S("lnp_loaded"), 32 * (n + 1))
                    fin(V.scalar_tensor_tensor(out=O[:, t, :], in0=O[:, t, :], scalar=st[:, 80 + 2 * t:81 + 2 * t],
                                               in1=lnp[:, 0, :], op0=ALU.subtract, op1=ALU.mult))
                    dve.wait_ge(S("ln_std"), 2 * n + t + 1)
                    fin(V.reciprocal(st[:, 84 + t:85 + t], st[:, 84 + t:85 + t]))
                    inc(V.scalar_tensor_tensor(out=X[:, t, :], in0=O[:, t, :], scalar=st[:, 84 + t:85 + t],
                                               in1=lnp[:, 1, :], op0=ALU.mult, op1=ALU.add), "ln_x")
                dve.wait_ge(S("ln_x"), count["ln_x"])

            def ple_p(i):
                dve.wait_ge(S("pT_hi"), i + 1)
                V.tensor_tensor(al[:, 0:NC], ps[:, 4, :], ah[:, 0:NC].bitcast(F32), ALU.subtract).then_inc(S("pT_lo"), 1)

            def ple_add(i, n):
                for t in range(NT):
                    sl = slice(n * NC, (n + 1) * NC)
                    dve.wait_ge(S("p_out"), 4 * (i + 1))
                    dve.wait_ge(S("gate_out"), 4 * i + 2 * n + t + 1)
                    fin(V.tensor_tensor(O[:, t, sl], O[:, t, sl], PW[:, 2 * n + t, :], ALU.mult))
                    inc(V.tensor_tensor(X[:, t, sl], X[:, t, sl], O[:, t, sl], ALU.add), "ple_x")
                dve.wait_ge(S("ple_x"), count["ple_x"])

            V.memset(relb[32:33, :], NEG).then_inc(S("rel_neg"), 1)
            rest_all(("in", 0, 0), 1)
            transposed()
            rest_all(("in", 0, 0))
            dve.wait_ge(S("wga_hi"), 1)
            V.tensor_tensor(wgal, wga.rearrange("p k n -> p (k n)"), wgah.bitcast(F32), ALU.subtract).then_inc(S("wga_lo"), 1)
            rest_all(("in", 0, 1), 1)
            dve.wait_ge(S("row_psum"), 1)
            V.tensor_copy(row_sb[0:MH, :], ps[0:MH, 3, 0:384]).then_inc(S("row_ready"), 1)
            rest_all(("in", 0, 2))
            dve.wait_ge(S("z_psum"), 1)
            for t in range(NT):
                dve.wait_ge(S("ga_loaded"), 32)
                inc(V.tensor_tensor(gz[t], ps[:, 7, t * SEQ:(t + 1) * SEQ], gla_b, ALU.add), "z_out")
            for t in range(NT):
                dve.wait_ge(S("z_out"), t + 1)
                inc(V.scalar_tensor_tensor(out=ge[t], in0=gz[t], scalar=-1.0, in1=gz[t], op0=ALU.mult, op1=ALU.min), "gate_abs")
            rest_all(("in", 0, 3))
            dve.wait_ge(S("bias_loaded"), 16 * MH)
            for h in range(MH):
                dve.wait_ge(S("score_psum"), h + 1)
                V.scalar_tensor_tensor(out=logits[:, h, 0:P], in0=ps[:, 4 + h % 4, 0:P], scalar=MD ** -0.5,
                                       in1=bias_t[:, h, P - 1::-1], op0=ALU.mult, op1=ALU.add)
                fin(V.scalar_tensor_tensor(out=logits[:, h, P:384], in0=ps[:, 4 + h % 4, P:384], scalar=MD ** -0.5,
                                           in1=bias_t[:, h, ::-1], op0=ALU.mult, op1=ALU.add), "logits_done")
            V.tensor_reduce(st[:, 0:8], logits[:, :, 0:P], AX_X, ALU.max)
            fin(V.tensor_reduce(st[:, 8:16], logits[:, :, P:384], AX_X, ALU.max))
            fin(V.tensor_scalar(st[:, 16:32], st[:, 0:16], -1.0, None, ALU.mult), "row_max")
            rest_all(("in", 0, 4))
            for t in range(NT):
                dve.wait_ge(S("softplus"), t + 1)
                inc(V.scalar_tensor_tensor(out=gz[t], in0=gz[t], scalar=0.0, in1=ge[t], op0=ALU.min,
                                           op1=ALU.subtract), "la_done")
            for h in range(MH):
                dve.wait_ge(S("PT_psum"), h + 1)
                if h >= 2:
                    dve.wait_ge(S("PV_used"), h - 1)
                V.tensor_copy(PT[h % 2], ps[:, 4 + h % 2, 0:384]).then_inc(S("PT_out"), 1)
            dve.wait_ge(S("exp_done"), 2 * MH)
            fin(V.reciprocal(st[:, 48:64], st[:, 32:48]))
            dve.wait_ge(S("PV_used"), MH)
            for t in range(NT):
                ins = V.tensor_tensor(O[:, t, 0:NC].rearrange("p (h n) -> p h n", h=MH),
                                      ps[:, 6 + t, :].rearrange("p (h n) -> p h n", h=MH),
                                      col(st[:, 48 + 8 * t:56 + 8 * t], MD), ALU.mult)
            ins.then_inc(S("moba_out"), 1)
            rest_all(("in", 0, 5), 1)
            linear(0)
            rest_all(("in", 0, 5))
            head_norm(0, 0, lambda t: ps[:, 6 + t, :], "gla_normed")
            rest_all(("out", 0, 0))
            gated(0, H[5], NC, 5)
            transposed()
            rest_all(("out", 0, 1))
            layer_norm(lambda t, n: ps[:, 2 * n + t, :], lambda n, t: dve.wait_ge(S("out_tile0"), 1) if (n, t) == (1, 0) else multiplied(dve, ("out", 0, n)),
                       between=lambda: rest_all(("w1", 0), 1))
            transposed(lambda: rest_all(("w1", 0)))
            for c in range(CF + 1):
                if c < CF:
                    rest_all(("w1", c))
                if c > 0:
                    dve.wait_ge(S("ah_done"), c)
                    m = -(-min(NC, FFN - (c - 1) * NC) // P) * SEQ
                    uh, ul = units_split(c - 1)
                    V.tensor_tensor(ul[:, 0:m], aT[:, 0:m], uh[:, 0:m].bitcast(F32), ALU.subtract).then_inc(S("al_done"), 1)
                if c < CF:
                    rest_all(("w3", c))
                if c > 0:
                    rest_all(("w2", c - 1))
                if c == 0:
                    rest_all(("w1", 1), 1)
                if c < CF:
                    m = -(-min(NC, FFN - c * NC) // P) * SEQ
                    multiplied(dve, ("w3", c))
                    dve.wait_ge(S("s_done"), c + 1)
                    if c > 0:
                        dve.wait_ge(S("al_done"), c)
                    V.tensor_tensor(aT[:, 0:m], s1T[:, 0:m], ps[:, 6:8, :].rearrange("p a n -> p (a n)")[:, 0:m],
                                    ALU.mult).then_inc(S("a_done"), 1)
            ple_p(0)
            rest_all(("proj", 0), 1)
            layer_norm(lambda t, n: ps[:, 2 * n + t, :], lambda n, t: dve.wait_ge(S("ffn_tile0"), 1) if t == 0 else multiplied(dve, ("w2", CF - 1)))
            transposed(lambda: rest_all(("gate", 0, 0), 1))
            rest_all(("gate", 0, 1))
            ple_add(0, 0)
            rest_all(("in", 1, 0))
            ple_add(0, 1)
            transposed()
            dve.wait_ge(S("gamma_loaded"), 32)
            inc(V.tensor_tensor(lb, oml, lb, ALU.subtract), "gamma_diff")
            rest_all(("in", 1, 0))
            dve.wait_ge(S("lb_done"), 1)
            fin(V.tensor_scalar(oml, lb, -1.0, 1.0, ALU.mult, ALU.add))
            rest_all(("in", 1, 1))
            for t in range(NT):
                dve.wait_ge(S("proj_out"), 12 + t + 1)
                f = H[0][:, t, SEQ:NC]
                fin(V.tensor_tensor(f, f, oml, ALU.mult))
                fin(V.tensor_tensor(f, f, lb, ALU.add))
                inc(V.tensor_scalar(la[1][t], f, 2.0 ** -63, None, ALU.max), "forget")
                fin(V.tensor_scalar(f, f, -1.0, 1.0, ALU.mult, ALU.add), "k_done")
            rest_all(("in", 1, 3))
            rest_all(("in", 1, 4))
            for t in range(NT):
                dve.wait_ge(S("proj_out"), 12 + 2 * 2 + t + 1)
                v = H[3][:, t, :].rearrange("p (h s n) -> p h s n", h=8, s=2)
                x1, x2 = v[:, :, 0, :], v[:, :, 1, :]
                cos = each(T[:, C_COS + 32 * t:C_COS + 32 * t + 32], 8)
                sin = each(T[:, C_SIN + 32 * t:C_SIN + 32 * t + 32], 8)
                r = [tmp[1][b][:, q * SEQ:(q + 1) * SEQ].rearrange("p (h n) -> p h n", h=8) for b in range(2) for q in range(2)]
                for d, a, b in ((0, x1, cos), (1, x2, sin), (2, x1, sin), (3, x2, cos)):
                    inc(V.tensor_tensor(r[d], a, b, ALU.mult), "dve_step")
                dve.wait_ge(S("dve_step"), count["dve_step"])
                inc(V.tensor_tensor(x1, r[0], r[1], ALU.subtract), "rotated")
                inc(V.tensor_tensor(x2, r[2], r[3], ALU.add), "rotated")
                dve.wait_ge(S("rotated"), count["rotated"])
            linear(1)
            rest_all(("in", 1, 2))
            head_norm(1, 1, lambda t: ps[:, 6 + t, :], "hgrn_normed")
            dve.wait_ge(S("decay_loaded"), 16)
            for h in range(LH):
                dve.wait_ge(S("ret_psum"), h + 1)
                V.tensor_tensor(ret_score[:, h, :], ps[:, ret_bank(h), 0:384], ret_decay[:, h, :],
                                ALU.mult).then_inc(S("ret_scored"), 1)
            rest_all(("in", 1, 5), 1)
            gated(1, H[2], 0, 6 + 4)
            rest_all(("in", 1, 5))
            for t in range(NT):
                dve.wait_ge(S("ret_out"), t + 1)
                m = st[:, 72 + 4 * t:76 + 4 * t]
                src = ps[:, 6 + t, :].rearrange("p (h n) -> p h n", h=LH)
                fin(V.tensor_reduce(m, src, AX_X, ALU.add))
                fin(V.tensor_scalar(m, m, 1.0 / LV, None, ALU.mult))
                fin(V.tensor_tensor(H[3][:, t, :].rearrange("p (h n) -> p h n", h=LH), src, col(m, LV),
                                    ALU.subtract), "ret_centred")
            rest_all(("out", 1, 0), 1)
            head_norm(1, 2, lambda t: H[3][:, t, :], "ret_normed")
            gated(1, H[5], NC, 6 + 5)
            rest_all(("out", 1, 0))
            transposed()
            rest_all(("out", 1, 1))

            def project_p():
                ple_p(1)
                rest_all(("proj", 1), 1)

            layer_norm(lambda t, n: ps[:, 2 * n + t, :], lambda n, t: dve.wait_ge(S("out_tile0"), 2) if (n, t) == (1, 0) else multiplied(dve, ("out", 1, n)),
                       between=project_p)
            def xrest(i, idx, off=0):
                g = N1 + idx
                dve.wait_ge(S("hi_done"), i * PASS + off * 6 + (g + 1))
                V.tensor_tensor(lo[:, g % SPLIT, :], raw[:, g % RAW, :], hi[:, g % SPLIT, :].bitcast(F32),
                                ALU.subtract).then_inc(S("lo_done"), 1)

            both = range(NT)
            sel = [rt[:, 0 + t, 0:NE] for t in both]
            gate8 = [rt[:, 2 + t, 0:NE] for t in both]
            iota8 = iota[:, 0:NE]
            lg = [rt[:, 6 + 2 * t, 0:8] for t in both]
            top = [rt[:, 6 + 2 * t, 8:16] for t in both]
            idx = [rt[:, 7 + 2 * t, 0:8].bitcast(U32) for t in both]
            idf = [rt[:, 7 + 2 * t, 8:16] for t in both]
            hot1, hot2 = [rt[:, 10 + t, 0:8] for t in both], [rt[:, 10 + t, 8:16] for t in both]
            e, g1, g2 = ([rt[:, 4 + t, n:n + 1] for t in both] for n in range(3))

            def abreast(op, name="dve_step"):
                for t in both:
                    inc(op(t), name)
                dve.wait_ge(S(name), count[name])

            inc(V.tensor_scalar(O, X[:], ALPHA, None, ALU.mult), "dve_step")
            V.memset(posm[:, :, NE:], -1.0)
            fin(V.memset(gates[:, :, NE:], 0.0))
            xrest(0, 0)
            xrest(0, 1)
            dve.wait_ge(S("wr_loaded"), 32)
            dve.wait_ge(S("route_psum"), 1)
            abreast(lambda t: V.tensor_tensor(lg[t], ps[:, 0, 8 * t:8 * t + 8], br[:], ALU.add))
            abreast(lambda t: V.max(top[t], lg[t]))
            abreast(lambda t: V.max_index(idx[t], top[t], lg[t]))
            abreast(lambda t: V.tensor_copy(idf[t], idx[t]))
            for t in both:
                inc(V.tensor_scalar(hot1[t], iota8, idf[t][:, 0:1], None, ALU.is_equal), "dve_step")
            abreast(lambda t: V.tensor_scalar(hot2[t], iota8, idf[t][:, 1:2], None, ALU.is_equal))
            abreast(lambda t: V.tensor_tensor(sel[t], hot1[t], hot2[t], ALU.add), "selected")
            abreast(lambda t: V.tensor_tensor(e[t], top[t][:, 1:2], top[t][:, 0:1], ALU.subtract), "top_diff")
            dve.wait_ge(S("top_exp"), NT)
            abreast(lambda t: V.tensor_scalar(g1[t], e[t], 1.0, None, ALU.add))
            abreast(lambda t: V.reciprocal(g1[t], g1[t]))
            abreast(lambda t: V.tensor_tensor(g2[t], g1[t], e[t], ALU.mult))
            for t in both:
                inc(V.tensor_scalar(hot1[t], hot1[t], g1[t], None, ALU.mult), "dve_step")
            abreast(lambda t: V.tensor_scalar(hot2[t], hot2[t], g2[t], None, ALU.mult))
            for t in both:
                inc(V.tensor_tensor(gates[:, t, 0:NE], hot1[t], hot2[t], ALU.add), "dve_step")
            dve.wait_ge(S("rank_psum"), 1)
            inc(V.tensor_copy(count_of, ps[:, 1, 16:24]), "dve_step")
            abreast(lambda t: V.tensor_scalar(posm[:, t, 0:NE], ps[:, 1, 8 * t:8 * t + 8], 1.0, None, ALU.add))
            abreast(lambda t: V.tensor_tensor(posm[:, t, 0:NE], posm[:, t, 0:NE], sel[t], ALU.mult))
            abreast(lambda t: V.tensor_scalar(posm[:, t, 0:NE], posm[:, t, 0:NE], -1.0, None, ALU.add), "ranked")

            def expert_a(i, c, last=False):
                dve.wait_ge(S("e_s"), i * CE + c + 2)
                dve.wait_ge(S("piece_used"), i * PASS + c * 6 + (N1 + (2 if last else 4)))
                dve.wait_ge(S("e_T"), i * CE + c + 1)
                V.tensor_tensor(a1, s1, ps[:, 3, :], ALU.mult).then_inc(S("e_a"), 1)

            def expert_al(i, c):
                dve.wait_ge(S("e_ah"), i * CE + c + 1)
                V.tensor_tensor(al[:, 0:NC], ps[:, 4, :], ah[:, 0:NC].bitcast(F32), ALU.subtract).then_inc(S("e_al"), 1)

            def expert_pick(i):
                for t in range(NT):
                    V.tensor_scalar(pick[:, t, :], iota, posm[:, t, bass.ds(i, 1)], None, ALU.is_equal)
                    ins = V.tensor_scalar(pickg[:, t, :], iota, posm[:, t, bass.ds(i, 1)], gates[:, t, bass.ds(i, 1)],
                                          ALU.is_equal, ALU.mult)
                ins.then_inc(S("e_pick"), 1)

            def expert_xl(i, half):
                dve.wait_ge(S("e_xh"), i * 2 + (half + 1))
                sl = slice(4 * half, 4 * half + 4)
                V.tensor_tensor(xl[:, sl, 0:P], ps[:, 5 + half, :].rearrange("p (k t) -> p k t", k=4),
                                xh[:, sl, 0:P].bitcast(F32), ALU.subtract).then_inc(S("e_xl"), 1)

            def expert(i):
                xrest(i, 2)
                xrest(i, 3)
                with dve.Fori(1, CE) as c:
                    xrest(i, 4, c - 1)
                    xrest(i, 5, c - 1)
                    expert_a(i, c - 1)
                    xrest(i, 6, c - 1)
                    xrest(i, 7, c - 1)
                    expert_al(i, c - 1)
                    xrest(i, 8, c - 1)
                    xrest(i, 9, c - 1)
                dve.wait_ge(S("e_gather"), i * 3 + 4)
                dve.wait_ge(S("routed"), 1)
                expert_pick(i + 1)
                xrest(i, 40)
                expert_a(i, CE - 1, True)
                xrest(i, 41)
                expert_al(i, CE - 1)
                xrest(i, PASS)
                expert_xl(i + 1, 0)
                expert_xl(i + 1, 1)
                xrest(i, PASS + 1)
                for q in range(4):
                    t, n = q // 2, q % 2
                    dve.wait_ge(S("e_scatter"), i * 4 + q + 2)
                    sl = slice(n * NC, (n + 1) * NC)
                    V.tensor_tensor(O[:, t, sl], O[:, t, sl], ps[:, 5 + q % 2, :], ALU.add).then_inc(S("e_added"), 1)

            expert_pick(0)
            expert_xl(0, 0)
            expert_xl(0, 1)
            with dve.Fori(0, NE) as i:
                expert(i)
            n_extra = dve.value_load(ctrl[0:1, 0:1], min_val=0, max_val=EXTRA)
            with dve.Fori(0, EXTRA) as j:
                with dve.If(j < n_extra):
                    expert(j + NE)
            dve.wait_ge(S("e_added"), (n_extra + NE) * 4 + 1)

            def tail_rest(u):
                g = N1 + u
                dve.wait_ge(S("hi_done"), (n_extra + NE) * PASS + (g + 1))
                V.tensor_tensor(lo[:, g % SPLIT, :], raw[:, g % RAW, :], hi[:, g % SPLIT, :].bitcast(F32),
                                ALU.subtract).then_inc(S("lo_done"), 1)

            layer_norm(None, None, summed=True)
            transposed()
            for u in range(2, 4):
                tail_rest(u)
            ple_add(1, 0)
            ple_add(1, 1)

        @block.tensor
        def _(pe):
            count_from_one(pe, "e_gather", "e_scatter", "e_T")
            mm = nc.tensor.matmul

            def three(o, l_hi, l_lo, r_hi, r_lo, start, stop, **kw):
                mm(o, l_hi, r_hi, start=start, stop=False, **kw)
                mm(o, l_hi, r_lo, start=False, stop=False, **kw)
                return mm(o, l_lo, r_hi, start=False, stop=stop, **kw)

            nxt = [0]

            def transpose_tile(src, t):
                for half in range(2):
                    for k in range(4):
                        c0 = (4 * half + k) * P
                        ins = nc.tensor.transpose(ps[:, 4 + 2 * t + half, k * P:(k + 1) * P], src[:, t, c0:c0 + P], ident)
                    ins.then_inc(S("xT_psum"), 1)

            def transpose_x(src, wait):
                for t in range(NT):
                    wait(t)
                    transpose_tile(src, t)
                nxt[0] += 4

            def need_xT(h, t):
                pe.wait_ge(S("xT_lo"), nxt[0] - 3 + 2 * t + h)

            def product(g0, banks, wait_piece=None, fresh=False, early=None):
                for h in range(2):
                    g = g0 + h
                    if wait_piece is None:
                        pe.wait_ge(S("lo_done"), g + 1)
                    else:
                        wait_piece(g)
                    wh = hi[:, g % SPLIT, :].rearrange("p (k n) -> p k n", k=4)
                    wl = lo[:, g % SPLIT, :].rearrange("p (k n) -> p k n", k=4)
                    for t in range(NT):
                        if fresh:
                            need_xT(h, t)
                        for k in range(4):
                            kk = 4 * h + k
                            ins = three(ps[:, banks[t], :], xh[:, kk, t * P:(t + 1) * P], xl[:, kk, t * P:(t + 1) * P],
                                        wh[:, k, :], wl[:, k, :], kk == 0, kk == KD - 1)
                        if early is not None and h == 1 and t == 0:
                            ins.then_inc(S(early), 1)
                    ins.then_inc(S("piece_used"), 1)

            proj_n = [0]

            def project(layer, j):
                n = proj_n[0]
                proj_n[0] += 1
                if n >= 2:
                    pe.wait_ge(S("proj_out"), 2 * (n - 1))
                product(where[("in", layer, j)], [2 * (n % 2), 2 * (n % 2) + 1], fresh=(j == 0))

            def linear_sums(layer, j):
                for t in range(NT):
                    for i in range(4):
                        ins = nc.tensor.transpose(ps[:, 4 + t, i * P:(i + 1) * P], H[j][:, t, i * P:(i + 1) * P], ident)
                    ins.then_inc(S("gT_psum"), 1)
                n = 0
                for dt in range(2):
                    for t in range(NT):
                        for half in range(2):
                            if n == 2:
                                pe.wait_ge(S("gT_out"), 2 * layer + 2)
                            if n >= 4:
                                pe.wait_ge(S("decay_out"), 8 * layer + n - 3)
                            lhs = la[layer][t][:, dt * P:(dt + 1) * P]
                            o = ps[:, sum_bank(n), :]
                            c0 = C_SUM + 4 * half * P
                            if half and t:
                                mm(o[:, 0:3 * P], lhs, T[:, c0:c0 + 3 * P], start=True, stop=True)
                                ins = mm(o[:, 3 * P:], lhs, T[:, c0 + 4 * P:c0 + 5 * P], start=True, stop=True)
                            else:
                                ins = mm(o, lhs, T[:, c0:c0 + 4 * P], start=True, stop=True)
                            ins.then_inc(S("sum_psum"), 1)
                            n += 1

            def linear(layer, values, projected, meanwhile):
                pe.wait_ge(S("decay_out"), 8 * layer + 8)
                for n, (t, plane) in enumerate(PLANES):
                    if n == 2:
                        pe.wait_ge(S("proj_out"), projected)
                    if n >= 4:
                        pe.wait_ge(S("plane_done"), 16 * layer + n - 3)
                    if plane > 0:
                        pe.wait_ge(S("Z_done"), 16 * layer + 8 + plane)
                    for h in range(LH):
                        dt, r = h // 2, 64 * (h % 2)
                        if plane == 0:
                            a, b = gT[r:r + 64, 2 + dt, t * P:(t + 1) * P], gT[r:r + 64, dt, t * P:(t + 1) * P]
                        else:
                            a = b = E[r:r + 64, 8 * dt + plane - 1, t * P:(t + 1) * P]
                        ins = mm(ps[:, plane_bank(n) + h % 2, dt * P:(dt + 1) * P], a, b, start=True, stop=True)
                    ins.then_inc(S("plane_psum"), 1)
                pe.wait_ge(S("Z_done"), 16 * layer + 16)
                pe.wait_ge(S("plane_done"), 16 * layer + 13)
                for h in range(LH):
                    dt, r = h // 2, 64 * (h % 2)
                    ins = mm(ps[:, 4 + h % 2, dt * P:(dt + 1) * P], E[r:r + 64, 8 * dt + 7, 0:P],
                             E[r:r + 64, 8 * dt + 7, P:SEQ], start=True, stop=True)
                ins.then_inc(S("join_psum"), 1)
                pe.wait_ge(S("plane_done"), 16 * layer + 16)
                meanwhile()
                pe.wait_ge(S("join_out"), layer + 1)
                sc = [score[layer][:, t, :].rearrange("p (h t) -> p h t", h=LH) for t in range(NT)]
                place = [2 * (h % 2) + h // 2 for h in range(LH)]
                for h in range(LH):
                    ins = mm(ps[:, 6, h * P:(h + 1) * P], sc[0][:, place[h], :], values[:, 0, h * P:(h + 1) * P], start=True, stop=True)
                ins.then_inc(S("lin_psum"), 1)
                for h in range(LH):
                    mm(ps[:, 7, h * P:(h + 1) * P], SC[layer][:, place[h], :], values[:, 0, h * P:(h + 1) * P], start=True, stop=False)
                    ins = mm(ps[:, 7, h * P:(h + 1) * P], sc[1][:, place[h], :], values[:, 1, h * P:(h + 1) * P], start=False, stop=True)
                ins.then_inc(S("lin_psum"), 1)

            def output(layer):
                for n in range(2):
                    if layer == 1 and n == 1:
                        turn_p(1)
                    product(where[("out", layer, n)], [2 * n, 2 * n + 1], fresh=(n == 0),
                            early="out_tile0" if n == 1 else None)

            def turn_p(i):
                pe.wait_ge(S("p_loaded"), 16 * (i + 1))
                for t in range(NT):
                    for k in range(2):
                        ins = nc.tensor.transpose(ps[:, 4, (2 * t + k) * P:(2 * t + k + 1) * P],
                                                  p_sb[:, t, k * P:(k + 1) * P], ident)
                ins.then_inc(S("pT_psum"), 1)

            def project_p(i, wait_piece, g):
                pe.wait_ge(S("pT_lo"), i + 1)
                wait_piece(g)
                wh = hi[:, g % SPLIT, :].rearrange("p (k n) -> p k n", k=2)
                wl = lo[:, g % SPLIT, :].rearrange("p (k n) -> p k n", k=2)
                for t in range(NT):
                    for n in range(2):
                        for k in range(2):
                            sl = slice((2 * t + k) * P, (2 * t + k + 1) * P)
                            ins = three(ps[:, 4 + 2 * n + t, :], ah[:, sl], al[:, sl], wh[:, k, n * NC:(n + 1) * NC],
                                        wl[:, k, n * NC:(n + 1) * NC], k == 0, k == 1)
                ins.then_inc(S("piece_used"), 1)

            def ple(i, wait_piece, g):
                pe.wait_ge(S("p_out"), 4 * (i + 1))
                transpose_x(X, lambda t: pe.wait_ge(S("ln_x"), 2 + 4 * i + t + 1))
                for n in range(2):
                    product(g + 2 * n, [2 * n, 2 * n + 1], wait_piece, fresh=(n == 0), early="gate_tile0")

            pe.wait_ge(S("tab_loaded"), 32)
            transpose_x(X, lambda t: pe.wait_ge(S(f"x_loaded{t}"), 16))
            project(0, 0)
            pe.wait_ge(S("hot_loaded"), 32)
            pe.wait_ge(S("rel_neg"), 1)
            mm(ps[0:MH, 3, 0:384], relb[:, :], hot_sb[0:33, :], start=True, stop=True).then_inc(S("row_psum"), 1)
            pe.wait_ge(S("wga_lo"), 1)
            for k in range(KD):
                sl = slice(k * RANK, (k + 1) * RANK)
                ins = three(ps[0:RANK, 4, 0:SEQ], wgah[:, sl], wgal[:, sl], xh[:, k, :], xl[:, k, :],
                            k == 0, k == KD - 1)
            ins.then_inc(S("gaT_psum"), 1)
            pe.wait_ge(S("row_ready"), 1)
            project(0, 1)
            pe.wait_ge(S("gaT_out"), 1)
            pe.wait_ge(S("ga_loaded"), 32)
            for t in range(NT):
                ins = mm(ps[:, 7, t * SEQ:(t + 1) * SEQ], gaT[0:RANK, t * P:(t + 1) * P], wgate[0:RANK, :],
                         start=True, stop=True)
            ins.then_inc(S("z_psum"), 1)
            for i in range(2):
                pe.wait_ge(S("proj_out"), 2 * i + 2)
                for t in range(NT):
                    if i == 1 and t == 1:
                        pe.wait_ge(S("z_out"), 2)
                    for g in range(4):
                        ins = nc.tensor.transpose(ps[:, 4 + 2 * i + t, g * P:(g + 1) * P],
                                                  H[i][:, t, g * P:(g + 1) * P], ident)
                    ins.then_inc(S("mT_psum"), 1)
            project(0, 2)
            pe.wait_ge(S("mT_out"), 4)
            for h in range(MH):
                g, r = h // 2, 64 * (h % 2)
                if h >= 4:
                    pe.wait_ge(S("logits_done"), h - 3)
                mm(ps[:, 4 + h % 4, 0:P], qkT[r:r + 64, 0, g, 0:P], qkT[r:r + 64, 1, g, 0:P], start=True, stop=True)
                mm(ps[:, 4 + h % 4, P:384], qkT[r:r + 64, 0, g, P:SEQ], qkT[r:r + 64, 1, g, :], start=True,
                   stop=True).then_inc(S("score_psum"), 1)
            project(0, 3)
            pe.wait_ge(S("logits_done"), MH)
            pe.wait_ge(S("proj_out"), 6)

            def turn_probabilities(h):
                pe.wait_ge(S("exp_done"), 2 * h + 2)
                if h >= 2:
                    pe.wait_ge(S("PT_out"), h - 1)
                for b in range(3):
                    ins = nc.tensor.transpose(ps[:, 4 + h % 2, b * P:(b + 1) * P], logits[:, h, b * P:(b + 1) * P], ident)
                ins.then_inc(S("PT_psum"), 1)

            turn_probabilities(0)
            for h in range(MH):
                if h + 1 < MH:
                    turn_probabilities(h + 1)
                pe.wait_ge(S("PT_out"), h + 1)
                sl = slice(h * MD, (h + 1) * MD)
                mm(ps[:, 6, sl], PT[h % 2][:, 0:P], H[2][:, 0, sl], start=True, stop=True)
                mm(ps[:, 7, sl], PT[h % 2][:, P:2 * P], H[2][:, 0, sl], start=True, stop=False)
                mm(ps[:, 7, sl], PT[h % 2][:, 2 * P:384], H[2][:, 1, sl], start=False, stop=True).then_inc(S("PV_used"), 1)
            pe.wait_ge(S("proj_out"), 8)
            pe.wait_ge(S("la_done"), 2)
            pe.wait_ge(S("moba_out"), 1)
            pe.wait_ge(S("sums_loaded"), 16)
            linear_sums(0, 3)
            project(0, 4)
            linear(0, H[4], 10, lambda: None)
            project(0, 5)
            transpose_x(O, lambda t: pe.wait_ge(S("mix_out"), t + 1))
            output(0)
            transpose_x(X, lambda t: pe.wait_ge(S("ln_x"), 0 + t + 1))
            for c in range(CF + 1):
                if c < CF:
                    w = min(NC, FFN - c * NC)
                    for j, name in enumerate(("w1", "w3")):
                        if c > 0:
                            pe.wait_ge(S("s_done" if j == 0 else "a_done"), c)
                        for h in range(2):
                            g = where[(name, c)] + h
                            pe.wait_ge(S("lo_done"), g + 1)
                            if c == 0 and j == 0:
                                need_xT(h, 1)
                            for m in range(-(-w // P)):
                                o = ps[:, 4 + 2 * j + m // 2, (m % 2) * SEQ:(m % 2 + 1) * SEQ]
                                for k in range(4):
                                    kk = 4 * h + k
                                    c0 = k * w + m * P
                                    wh, wl = hi[:, g % SPLIT, c0:c0 + P], lo[:, g % SPLIT, c0:c0 + P]
                                    first = kk == 0 and m % 2 == 0
                                    ins = three(o, wh, wl, xh[:, kk, :], xl[:, kk, :], first, kk == KD - 1,
                                                skip_group_check=True)
                            ins.then_inc(S("piece_used"), 1)
                if c == CF:
                    pe.wait_ge(S("a_done"), c)
                    turn_p(0)
                if c > 0:
                    uh, ul = units_split(c - 1)
                    pe.wait_ge(S("al_done"), c)
                    w = min(NC, FFN - (c - 1) * NC)
                    g0 = where[("w2", c - 1)]
                    for h in range(2):
                        g = g0 + h
                        pe.wait_ge(S("lo_done"), g + 1)
                        kn = pieces[g].k
                        rows = pieces[g].rows
                        wh = hi[0:rows, g % SPLIT, 0:kn * D].rearrange("p (k n) -> p k n", k=kn)
                        wl = lo[0:rows, g % SPLIT, 0:kn * D].rearrange("p (k n) -> p k n", k=kn)
                        last = c == CF and h == 1
                        for t in range(NT):
                            for n in range(2):
                                for k in range(kn):
                                    m = kn * h + k
                                    sl = slice(m * SEQ + t * P, m * SEQ + (t + 1) * P)
                                    ins = three(ps[:, 2 * n + t, :], uh[0:rows, sl], ul[0:rows, sl],
                                                wh[:, k, n * NC:(n + 1) * NC], wl[:, k, n * NC:(n + 1) * NC],
                                                c == 1 and m == 0, last, skip_group_check=True)
                            if t == 0 and last:
                                ins.then_inc(S("ffn_tile0"), 1)
                        ins.then_inc(S("piece_used"), 1)
            split_wait = lambda g: pe.wait_ge(S("lo_done"), g + 1)
            project_p(0, split_wait, where[("proj", 0)])
            ple(0, split_wait, where[("gate", 0, 0)])
            transpose_x(X, lambda t: pe.wait_ge(S("ple_x"), 3 + t))
            project(1, 0)
            project(1, 1)
            project(1, 3)
            pe.wait_ge(S("k_done"), 2)
            pe.wait_ge(S("log_f"), 2)
            linear_sums(1, 0)
            project(1, 4)

            def turn_retention():
                for t in range(NT):
                    pe.wait_ge(S("rotated"), 2 * t + 2)
                    for i in range(4):
                        ins = nc.tensor.transpose(ps[:, 2 + t, i * P:(i + 1) * P], H[3][:, t, i * P:(i + 1) * P], ident)
                    ins.then_inc(S("rT_psum"), 1)

            linear(1, H[1], 20, turn_retention)
            pe.wait_ge(S("rT_out"), 2)
            for h in range(LH):
                dt, r = h // 2, 64 * (h % 2)
                mm(ps[:, ret_bank(h), 0:SEQ], gT[r:r + 64, 2 + dt, 0:P], gT[r:r + 64, dt, :], start=True, stop=True)
                mm(ps[:, ret_bank(h), SEQ:384], gT[r:r + 64, 2 + dt, P:SEQ], gT[r:r + 64, dt, P:SEQ], start=True,
                   stop=True).then_inc(S("ret_psum"), 1)
            project(1, 2)
            pe.wait_ge(S("ret_scored"), LH)
            pe.wait_ge(S("hgrn_normed"), 2)
            for t in range(NT):
                for h in range(LH):
                    o, sl = ps[:, 6 + t, h * P:(h + 1) * P], slice(h * P, (h + 1) * P)
                    if t == 0:
                        ins = mm(o, ret_score[:, h, 0:P], H[4][:, 0, sl], start=True, stop=True)
                    else:
                        mm(o, ret_score[:, h, P:SEQ], H[4][:, 0, sl], start=True, stop=False)
                        ins = mm(o, ret_score[:, h, SEQ:384], H[4][:, 1, sl], start=False, stop=True)
                ins.then_inc(S("ret_out"), 1)
            project(1, 5)
            transpose_x(O, lambda t: pe.wait_ge(S("mix_out"), 4 + t + 1))
            output(1)
            project_p(1, split_wait, where[("proj", 1)])
            pe.wait_ge(S("p_out"), 8)
            pe.wait_ge(S("wr_loaded"), 32)
            for t in range(NT):
                pe.wait_ge(S("ln_x"), 4 + t + 1)
                transpose_tile(X, t)
                pe.wait_ge(S("xT_full"), 2 * t + 2)
                for k in range(KD):
                    ins = mm(ps[:, 0, 8 * t:8 * t + 8], XR[:, k, t * P:(t + 1) * P], wr[:, k, :],
                             start=(k == 0), stop=(k == KD - 1))
            ins.then_inc(S("route_psum"), 1)
            pe.wait_ge(S("selected"), 2)
            sel = [rt[:, t, 0:NE] for t in range(NT)]
            mm(ps[:, 1, 0:8], before, sel[0], start=True, stop=True)
            mm(ps[:, 1, 8:16], ones, sel[0], start=True, stop=False)
            mm(ps[:, 1, 8:16], before, sel[1], start=False, stop=True)
            mm(ps[:, 1, 16:24], ones, sel[0], start=True, stop=False)
            mm(ps[:, 1, 16:24], ones, sel[1], start=False, stop=True).then_inc(S("rank_psum"), 1)

            def need(i, idx, off=0):
                pe.wait_ge(S("lo_done"), i * PASS + off * 6 + (N1 + idx + 1))

            def columns(i, idx, off, bank):
                for h in range(2):
                    need(i, idx + h, off)
                    s = (N1 + idx + h) % SPLIT
                    wh = hi[:, s, :].rearrange("p (k n) -> p k n", k=4)
                    wl = lo[:, s, :].rearrange("p (k n) -> p k n", k=4)
                    for k in range(4):
                        kk = 4 * h + k
                        ins = three(ps[:, bank, :], xh[:, kk, 0:P], xl[:, kk, 0:P], wh[:, k, :], wl[:, k, :],
                                    kk == 0, kk == KD - 1)
                    ins.then_inc(S("piece_used"), 1)

            def h1(i, c, idx, off=0):
                pe.wait_ge(S("e_s"), i * CE + c + 1)
                columns(i, idx, off, 2)

            def h3(i, c, idx, off=0):
                pe.wait_ge(S("e_a"), i * CE + c + 1)
                columns(i, idx, off, 3)

            def turn(i, c):
                pe.wait_ge(S("e_a"), i * CE + c + 2)
                pe.wait_ge(S("e_al"), i * CE + c + 1)
                for k in range(4):
                    ins = nc.tensor.transpose(ps[:, 4, k * P:(k + 1) * P], a1[:, k * P:(k + 1) * P], ident)
                ins.then_inc(S("e_T"), 1)

            def second(i, c, idx, off, first, last):
                pe.wait_ge(S("e_al"), i * CE + c + 2)
                for h in range(2):
                    need(i, idx + h, off)
                    s = (N1 + idx + h) % SPLIT
                    wh = hi[:, s, :].rearrange("p (k n) -> p k n", k=2)
                    wl = lo[:, s, :].rearrange("p (k n) -> p k n", k=2)
                    for n in range(2):
                        for k in range(2):
                            m = 2 * h + k
                            sl = slice(m * P, (m + 1) * P)
                            ins = three(ps[:, n, :], ah[:, sl], al[:, sl], wh[:, k, n * NC:(n + 1) * NC],
                                        wl[:, k, n * NC:(n + 1) * NC], first and m == 0, last and m == 3,
                                        skip_group_check=True)
                    ins.then_inc(S("piece_used"), 1)

            def gather(i):
                pe.wait_ge(S("e_pick"), i + 1)
                for t in range(NT):
                    ins = nc.tensor.transpose(ps[:, 7, t * P:(t + 1) * P], pickg[:, t, :], ident)
                ins.then_inc(S("e_gather"), 1)
                for half in range(2):
                    for k in range(4):
                        kk = 4 * half + k
                        for t in range(NT):
                            ins = mm(ps[:, 5 + half, k * P:(k + 1) * P], X[:, t, kk * P:(kk + 1) * P], pick[:, t, :],
                                     start=(t == 0), stop=(t == NT - 1))
                    ins.then_inc(S("e_gather"), 1)

            def expert(i):
                pe.wait_ge(S("e_xl"), i * 2 + 2)
                h1(i, 0, 0)
                h3(i, 0, 2)
                pe.wait_ge(S("e_yout"), i + 1)
                h1(i, 1, 4)
                turn(i, 0)
                h3(i, 1, 6)
                second(i, 0, 8, 0, True, False)
                with pe.Fori(2, CE) as c:
                    h1(i, c, 4, c - 1)
                    turn(i, c - 1)
                    h3(i, c, 6, c - 1)
                    second(i, c - 1, 8, c - 1, False, False)
                turn(i, CE - 1)
                pe.wait_ge(S("e_gT"), i + 2)
                pe.wait_ge(S("e_added"), i * 4 + 1)
                gather(i + 1)
                second(i, CE - 1, 40, 0, False, True)
                pe.wait_ge(S("e_xl"), i * 2 + 4)
                pe.wait_ge(S("e_yout"), i + 2)
                for q in range(4):
                    t, n = q // 2, q % 2
                    if q >= 2:
                        pe.wait_ge(S("e_added"), i * 4 + q)
                    mm(ps[:, 5 + q % 2, :], pickgT[:, t * P:(t + 1) * P], ysb[:, n * NC:(n + 1) * NC],
                       start=True, stop=True).then_inc(S("e_scatter"), 1)

            gather(0)
            with pe.Fori(0, NE) as i:
                expert(i)
            pe.wait_ge(S("routed"), 1)
            n_extra = pe.value_load(ctrl[0:1, 0:1], min_val=0, max_val=EXTRA)
            with pe.Fori(0, EXTRA) as j:
                with pe.If(j < n_extra):
                    expert(j + NE)
            pe.wait_ge(S("e_added"), (n_extra + NE) * 4 + 1)
            tail_wait = lambda g: pe.wait_ge(S("lo_done"), (n_extra + NE) * PASS + (g + 1))
            ple(1, tail_wait, N1)


_INS = ['x', 'p', 'rel_bias', 'even_w_in', 'gla_w_gate', 'gla_b_gate', 'gla_norm', 'even_w_out',
        'odd_w_in', 'hgrn_gamma', 'hgrn_norm', 'ret_norm', 'odd_w_out', 'ln_mix_g', 'ln_mix_b',
        'ln_ffn_g', 'ln_ffn_b', 'ffn_w1', 'ffn_w3', 'ffn_w2', 'router_w', 'router_b', 'expert_w1',
        'expert_w3', 'expert_w2', 'ple_w_gate', 'ple_w_proj']


def kernel(**inputs):
    import concourse.bacc as bacc
    from concourse.bass_utils import run_bass_kernel_spmd

    nc = bacc.Bacc("TRN2", target_bir_lowering=False, num_devices=1)
    arrays, args = {}, []
    tables = dict(zip(("tab", "masks", "decay", "hot"), constants()))
    for name in _INS + list(tables):
        a = np.ascontiguousarray(tables[name] if name in tables else inputs[name])
        arrays[f"in_{name}"] = a
        args.append(nc.dram_tensor(f"in_{name}", a.shape, mybir.dt.from_np(a.dtype), kind="ExternalInput").ap())
    out = nc.dram_tensor("out_x", (1, SEQ, D), F32, kind="ExternalOutput").ap()
    trunk(nc, *args, out)
    r = run_bass_kernel_spmd(nc, [arrays], core_ids=[0])
    return r.results[0]["out_x"]
```
